# Optimizing a Trainium2 kernel written in Bass

```python
import math
import jax, jax.numpy as jnp
from jax import lax
import numpy as np

D_MODEL = 1024
BATCH = 1
SEQ = 512
DEPTH = 1
DEC_BATCH = 1
DEC_SEQ = 32
PAST_LEN = 128

CHUNK = 64
Q_BLOCK = 128
H_A = 8
DH_A = 64
WA = H_A * DH_A
H_B = 8
DK_B = 64
DV_B = 128
QK_B = H_B * DK_B
V_B = H_B * DV_B
CONV_W = 4
CONV_DIM = 2 * QK_B + V_B
N_GROUPS = 4
EXPERTS_PER_GROUP = 8
N_EXPERTS = N_GROUPS * EXPERTS_PER_GROUP
TOP_K = 2
D_EXPERT = 512
MOE_BLOCK = 128
EPS = 1e-6
IN_SPLITS = (WA, WA, WA, H_A, QK_B, QK_B, V_B, H_B, H_B, V_B, D_MODEL, D_MODEL)
D_IN = 3 * WA + H_A + 2 * QK_B + V_B + 2 * H_B + V_B + 2 * D_MODEL

kernel_name = "fox_gdn_hier_moe_streaming_step"

def rmsnorm(x, g):
    xf = x.astype(jnp.float32)
    y = xf * lax.rsqrt(jnp.mean(xf * xf, axis=-1, keepdims=True) + EPS) * g.astype(jnp.float32)
    return y.astype(x.dtype)

def l2norm(x):
    xf = x.astype(jnp.float32)
    return xf * lax.rsqrt(jnp.sum(xf * xf, axis=-1, keepdims=True) + EPS)

def causal_conv(u, buf, w):
    T = u.shape[1]
    full = jnp.concatenate([buf.astype(u.dtype), u], axis=1)
    out = full[:, 0:T] * w[0]
    for i in range(1, CONV_W):
        out = out + full[:, i:i + T] * w[i]
    new_buf = full[:, full.shape[1] - (CONV_W - 1):]
    return jax.nn.silu(out), new_buf

def fox_attend(q, k, v, c_q, c_k, pos_q, pos_k):
    B, Tq, H, dh = q.shape
    blk = Q_BLOCK if Tq % Q_BLOCK == 0 else Tq
    nb = Tq // blk
    scale = dh ** -0.5
    c_kt = c_k.transpose(0, 2, 1)
    qb = q.reshape(B, nb, blk, H, dh).swapaxes(0, 1)
    cqb = c_q.reshape(B, nb, blk, H).transpose(1, 0, 3, 2)
    pqb = pos_q.reshape(nb, blk)

    def one_block(args):
        q_n, cq_n, pq_n = args
        s = jnp.einsum('bqhd,bkhd->bhqk', q_n, k, preferred_element_type=jnp.float32) * scale
        s = s + cq_n[..., :, None] - c_kt[..., None, :]
        s = jnp.where(pos_k[None, :] <= pq_n[:, None], s, -jnp.inf)
        p = jax.nn.softmax(s, axis=-1)
        return jnp.einsum('bhqk,bkhd->bqhd', p.astype(v.dtype), v)

    o = lax.map(one_block, (qb, cqb, pqb))
    return o.swapaxes(0, 1).reshape(B, Tq, H, dh)

def gdn_chunked(q, k, v, g, beta, s0):
    f32 = jnp.float32
    B, T, H, dk = q.shape
    dv = v.shape[-1]
    L = CHUNK if T % CHUNK == 0 else T
    N = T // L

    def blocks(a):
        a = a.astype(f32).reshape((B, N, L) + a.shape[2:])
        return jnp.moveaxis(a, (1, 3), (0, 2))

    qc, kc, vc, gc, bc = blocks(q), blocks(k), blocks(v), blocks(g), blocks(beta)
    G = jnp.cumsum(gc, axis=-1)
    eG = jnp.exp(G)
    idx = jnp.arange(L)
    incl = idx[:, None] >= idx[None, :]
    strict = idx[:, None] > idx[None, :]
    decay = jnp.exp(jnp.where(incl, G[..., :, None] - G[..., None, :], -jnp.inf))
    kb = kc * bc[..., None]
    m = jnp.where(strict, jnp.einsum('nbhid,nbhjd->nbhij', kb, kc) * decay, 0.0)
    a = m + jnp.eye(L, dtype=f32)
    rhs = jnp.concatenate([vc * bc[..., None], kb * eG[..., None]], axis=-1)
    sol = lax.linalg.triangular_solve(a, rhs, left_side=True, lower=True, unit_diagonal=True)
    u, w = sol[..., :dv], sol[..., dv:]
    attn = jnp.where(incl, jnp.einsum('nbhid,nbhjd->nbhij', qc, kc) * decay, 0.0)
    q_dec = qc * eG[..., None]
    k_dec = kc * jnp.exp(G[..., -1:] - G)[..., None]
    g_last = jnp.exp(G[..., -1])

    def step(s, xs):
        u_n, w_n, attn_n, qd_n, kd_n, gl_n = xs
        v_new = u_n - jnp.einsum('bhld,bhdv->bhlv', w_n, s)
        o_n = jnp.einsum('bhld,bhdv->bhlv', qd_n, s) + jnp.einsum('bhij,bhjv->bhiv', attn_n, v_new)
        s = s * gl_n[..., None, None] + jnp.einsum('bhld,bhlv->bhdv', kd_n, v_new)
        return s, o_n

    s_final, o = lax.scan(step, s0.astype(f32), (u, w, attn, q_dec, k_dec, g_last))
    o = jnp.moveaxis(o, (0, 2), (1, 3)).reshape(B, T, H, dv)
    return o, s_final

def hier_moe(x, w_grp, b_grp, w_exp, b_exp, w_e1, w_e3, w_e2):
    f32 = jnp.float32
    B, T, D = x.shape
    NT = B * T
    xt = x.reshape(NT, D)
    rows = jnp.arange(NT)
    grp_logits = jnp.einsum('td,dg->tg', xt, w_grp).astype(f32) + b_grp.astype(f32)
    grp_prob = jax.nn.softmax(grp_logits, axis=-1)
    g_sel = jnp.argmax(grp_logits, axis=-1)
    p_g = grp_prob[rows, g_sel]
    e_logits = (jnp.einsum('td,de->te', xt, w_exp).astype(f32) + b_exp.astype(f32)).reshape(NT, N_GROUPS, EXPERTS_PER_GROUP)
    e_in_group = e_logits[rows, g_sel]
    top_val, top_idx = lax.top_k(e_in_group, TOP_K)
    p_e = jax.nn.softmax(top_val, axis=-1)
    expert_id = g_sel[:, None] * EXPERTS_PER_GROUP + top_idx
    weights = p_g[:, None] * p_e

    A = NT * TOP_K
    flat_e = expert_id.reshape(A).astype(jnp.int32)
    flat_tok = (jnp.arange(A) // TOP_K).astype(jnp.int32)
    flat_w = weights.reshape(A)
    order = jnp.argsort(flat_e)
    e_sorted = flat_e[order]
    counts = jax.ops.segment_sum(jnp.ones((A,), jnp.int32), flat_e, num_segments=N_EXPERTS)
    padded = ((counts + MOE_BLOCK - 1) // MOE_BLOCK) * MOE_BLOCK
    pad_end = jnp.cumsum(padded)
    pad_start = pad_end - padded
    start = jnp.cumsum(counts) - counts
    dest = pad_start[e_sorted] + jnp.arange(A, dtype=jnp.int32) - start[e_sorted]
    NB = -(-A // MOE_BLOCK) + N_EXPERTS
    P = NB * MOE_BLOCK
    slot_tok = jnp.full((P,), NT, jnp.int32).at[dest].set(flat_tok[order])
    slot_w = jnp.zeros((P,), f32).at[dest].set(flat_w[order])
    blk_expert = jnp.minimum(jnp.searchsorted(pad_end, jnp.arange(NB, dtype=jnp.int32) * MOE_BLOCK, side='right'), N_EXPERTS - 1)
    x_pad = jnp.concatenate([xt, jnp.zeros((1, D), xt.dtype)], axis=0)

    def run_block(args):
        tok, e, wt = args
        xb = x_pad[tok]
        h = jax.nn.silu(xb @ w_e1[e]) * (xb @ w_e3[e])
        return (h @ w_e2[e]) * wt[:, None].astype(xb.dtype)

    yb = lax.map(run_block, (slot_tok.reshape(NB, MOE_BLOCK), blk_expert, slot_w.reshape(NB, MOE_BLOCK)))
    y = jnp.zeros((NT + 1, D), x.dtype).at[slot_tok].add(yb.reshape(P, D).astype(x.dtype))
    return y[:NT].reshape(B, T, D)

def hybrid_layer(x, past_k, past_v, past_logf, s0, conv_buf, p):
    f32 = jnp.float32
    B, T, _ = x.shape
    P = past_k.shape[1]
    h = rmsnorm(x, p["g_mix"])
    proj = jnp.einsum('btd,de->bte', h, p["w_in"])
    offsets = np.cumsum(np.array(IN_SPLITS))[:-1].tolist()
    fq, fk, fv, flog, bq, bk, bv, bbeta, ba, bz, ga, gb = jnp.split(proj, offsets, axis=-1)

    fq = rmsnorm(fq.reshape(B, T, H_A, DH_A), p["g_qnorm"])
    fk = rmsnorm(fk.reshape(B, T, H_A, DH_A), p["g_knorm"])
    fv = fv.reshape(B, T, H_A, DH_A)
    logf = jax.nn.log_sigmoid(flog.astype(f32) + p["b_f"].astype(f32))
    k_all = jnp.concatenate([past_k.astype(fk.dtype), fk], axis=1)
    v_all = jnp.concatenate([past_v.astype(fv.dtype), fv], axis=1)
    c_all = jnp.cumsum(jnp.concatenate([past_logf.astype(f32), logf], axis=1), axis=1)
    pos_k = jnp.arange(P + T)
    y_a = fox_attend(fq, k_all, v_all, c_all[:, P:], c_all, pos_k[P:], pos_k)

    conv_out, new_buf = causal_conv(jnp.concatenate([bq, bk, bv], axis=-1), conv_buf, p["w_conv"])
    cq, ck, cv = jnp.split(conv_out, [QK_B, 2 * QK_B], axis=-1)
    cq = l2norm(cq.reshape(B, T, H_B, DK_B)) * (DK_B ** -0.5)
    ck = l2norm(ck.reshape(B, T, H_B, DK_B))
    cv = cv.reshape(B, T, H_B, DV_B)
    beta = jax.nn.sigmoid(bbeta.astype(f32))
    g = -jnp.exp(p["a_log"].astype(f32)) * jax.nn.softplus(ba.astype(f32) + p["dt_bias"].astype(f32))
    o_b, s_new = gdn_chunked(cq, ck, cv, g, beta, s0)
    y_b = (rmsnorm(o_b, p["g_onorm"]) * jax.nn.silu(bz.reshape(B, T, H_B, DV_B).astype(f32))).astype(x.dtype)

    gates = jax.nn.sigmoid(jnp.concatenate([ga, gb], axis=-1).astype(f32) + p["b_gate"].astype(f32)).astype(x.dtype)
    gate_a, gate_b = gates[..., :D_MODEL], gates[..., D_MODEL:]
    branch_a = jnp.einsum('bte,ed->btd', y_a.reshape(B, T, WA), p["w_br_a"])
    branch_b = jnp.einsum('bte,ed->btd', y_b.reshape(B, T, V_B), p["w_br_b"])
    x1 = x + jnp.einsum('btd,de->bte', gate_a * branch_a + gate_b * branch_b, p["w_out"])

    x2 = x1 + hier_moe(rmsnorm(x1, p["g_ffn"]), p["w_grp"], p["b_grp"], p["w_exp"], p["b_exp"],
                       p["w_e1"], p["w_e3"], p["w_e2"])
    return x2, fk, fv, logf, s_new, new_buf

def setup_inputs(seed: int = 0) -> dict:
    key = jax.random.key(seed)
    ks = jax.random.split(key, 32)
    f32 = jnp.float32
    L = DEPTH

    def nrm(k, shape, scale):
        return jax.random.normal(k, shape, f32) * scale

    def gain(k, shape):
        return 1.0 + 0.05 * jax.random.normal(k, shape, f32)

    dt = jnp.exp(jax.random.uniform(ks[13], (L, H_B), f32, math.log(0.001), math.log(0.1)))
    return {
        "x_prompt": nrm(ks[0], (BATCH, SEQ, D_MODEL), 1.0),
        "x_sample": nrm(ks[1], (DEC_BATCH, DEC_SEQ, D_MODEL), 1.0),
        "cache_fox_k": nrm(ks[2], (L, DEC_BATCH, PAST_LEN, H_A, DH_A), 1.0),
        "cache_fox_v": nrm(ks[3], (L, DEC_BATCH, PAST_LEN, H_A, DH_A), 1.0),
        "cache_fox_logf": jax.nn.log_sigmoid(1.0 + jax.random.normal(ks[4], (L, DEC_BATCH, PAST_LEN, H_A), f32)),
        "state_gdn": nrm(ks[5], (L, DEC_BATCH, H_B, DK_B, DV_B), 0.1),
        "state_gdn_conv": nrm(ks[6], (L, DEC_BATCH, CONV_W - 1, CONV_DIM), 1.0),
        "g_mix": gain(ks[7], (L, D_MODEL)),
        "w_in": nrm(ks[8], (L, D_MODEL, D_IN), D_MODEL ** -0.5),
        "b_f": 1.0 + 0.1 * jax.random.normal(ks[9], (L, H_A), f32),
        "g_qnorm": gain(ks[10], (L, DH_A)),
        "g_knorm": gain(ks[11], (L, DH_A)),
        "w_conv": nrm(ks[12], (L, CONV_W, CONV_DIM), CONV_W ** -0.5),
        "a_log": jnp.log(jax.random.uniform(ks[14], (L, H_B), f32, 1.0, 16.0)),
        "dt_bias": dt + jnp.log(-jnp.expm1(-dt)),
        "g_onorm": gain(ks[15], (L, DV_B)),
        "b_gate": nrm(ks[16], (L, 2 * D_MODEL), 0.1),
        "w_br_a": nrm(ks[17], (L, WA, D_MODEL), WA ** -0.5),
        "w_br_b": nrm(ks[18], (L, V_B, D_MODEL), V_B ** -0.5),
        "w_out": nrm(ks[19], (L, D_MODEL, D_MODEL), D_MODEL ** -0.5),
        "g_ffn": gain(ks[20], (L, D_MODEL)),
        "w_grp": nrm(ks[21], (L, D_MODEL, N_GROUPS), D_MODEL ** -0.5),
        "b_grp": nrm(ks[22], (L, N_GROUPS), 0.01),
        "w_exp": nrm(ks[23], (L, D_MODEL, N_EXPERTS), D_MODEL ** -0.5),
        "b_exp": nrm(ks[24], (L, N_EXPERTS), 0.01),
        "w_e1": nrm(ks[25], (L, N_EXPERTS, D_MODEL, D_EXPERT), D_MODEL ** -0.5),
        "w_e3": nrm(ks[26], (L, N_EXPERTS, D_MODEL, D_EXPERT), D_MODEL ** -0.5),
        "w_e2": nrm(ks[27], (L, N_EXPERTS, D_EXPERT, D_MODEL), D_EXPERT ** -0.5),
    }

def reference(x_prompt, x_sample, cache_fox_k, cache_fox_v, cache_fox_logf, state_gdn, state_gdn_conv,
              g_mix, w_in, b_f, g_qnorm, g_knorm, w_conv, a_log, dt_bias, g_onorm, b_gate,
              w_br_a, w_br_b, w_out, g_ffn, w_grp, b_grp, w_exp, b_exp, w_e1, w_e3, w_e2):
    f32 = jnp.float32
    Bp = x_prompt.shape[0]
    yp, ys = x_prompt, x_sample
    kp_l, vp_l, lp_l, sp_l, cp_l = [], [], [], [], []
    ks_l, vs_l, ls_l, ss_l, cs_l = [], [], [], [], []
    for l in range(DEPTH):
        p = {"g_mix": g_mix[l], "w_in": w_in[l], "b_f": b_f[l], "g_qnorm": g_qnorm[l], "g_knorm": g_knorm[l],
             "w_conv": w_conv[l], "a_log": a_log[l], "dt_bias": dt_bias[l], "g_onorm": g_onorm[l],
             "b_gate": b_gate[l], "w_br_a": w_br_a[l], "w_br_b": w_br_b[l], "w_out": w_out[l],
             "g_ffn": g_ffn[l], "w_grp": w_grp[l], "b_grp": b_grp[l], "w_exp": w_exp[l], "b_exp": b_exp[l],
             "w_e1": w_e1[l], "w_e3": w_e3[l], "w_e2": w_e2[l]}
        yp, kp, vp, lp, sp, cp = hybrid_layer(
            yp,
            jnp.zeros((Bp, 0, H_A, DH_A), yp.dtype), jnp.zeros((Bp, 0, H_A, DH_A), yp.dtype),
            jnp.zeros((Bp, 0, H_A), f32), jnp.zeros((Bp, H_B, DK_B, DV_B), f32),
            jnp.zeros((Bp, CONV_W - 1, CONV_DIM), yp.dtype), p)
        ys, kss, vss, lss, sss, css = hybrid_layer(
            ys, cache_fox_k[l], cache_fox_v[l], cache_fox_logf[l], state_gdn[l], state_gdn_conv[l], p)
        kp_l.append(kp); vp_l.append(vp); lp_l.append(lp); sp_l.append(sp); cp_l.append(cp)
        ks_l.append(kss); vs_l.append(vss); ls_l.append(lss); ss_l.append(sss); cs_l.append(css)
    return (yp, ys,
            jnp.stack(kp_l), jnp.stack(vp_l), jnp.stack(lp_l), jnp.stack(sp_l), jnp.stack(cp_l),
            jnp.stack(ks_l), jnp.stack(vs_l), jnp.stack(ls_l), jnp.stack(ss_l), jnp.stack(cs_l))


_drawn_inputs = setup_inputs


def setup_inputs(seed=0):
    import zlib

    import numpy as np

    out = dict(_drawn_inputs(seed))
    spreads = {}
    factors = {'b_grp': 2.777, 'b_exp': 4.275}
    for name, (base, spread) in spreads.items():
        noise = np.random.default_rng([zlib.crc32(name.encode()), seed]).standard_normal(out[name].shape)
        drawn = base * np.exp(spread * noise) if base else spread * noise
        out[name] = __import__('jax').numpy.asarray(drawn.astype(out[name].dtype))
    for name, factor in factors.items():
        out[name] = (out[name] * factor).astype(out[name].dtype)
    return out
```

```python
from contextlib import ExitStack

import concourse.bass as bass
from concourse import mybir

DT = mybir.dt
F32, F32R, I32, U32 = DT.float32, DT.float32r, DT.int32, DT.uint32
ALU = mybir.AluOpType
ACT = mybir.ActivationFunctionType
AX = mybir.AxisListType

D = 1024
KD = D // 128
NS, NP = 32, 512
NT = NS + NP
HALF = NT // 2
TILES = [(0, NS)] + [(NS + 128 * i, 128) for i in range(NP // 128)]
H, DH = 8, 64
DV = 128
PAST = 128
WA = H * DH
CONV_CH = 2 * H * DH + H * DV
CONV_W = 4
NCC = CONV_CH // 128
NE, GROUPS, PER_GROUP, FE = 32, 4, 8, 512
SLOTS = 64
MORE = (2 * NT - 1) // SLOTS
NB = NE + MORE
EPS = 1e-6
NEG = -1e30
C_FQ, C_FK, C_FV = 0, WA, 2 * WA
C_LOGF = 3 * WA
C_CONV = C_LOGF + H
C_BETA = C_CONV + CONV_CH
C_DECAY = C_BETA + H
C_Z = C_DECAY + H
C_GA = C_Z + H * DV
C_GB = C_GA + D


class Marks:

    def __init__(self, sem, names):
        self.sem, self.at, self.made = sem, {n: i + 1 for i, n in enumerate(names)}, 0

    def mark(self, ins, name):
        self.made += 1
        assert self.at[name] == self.made, (name, self.at[name], self.made)
        return ins.then_inc(self.sem, 1)

    def wait(self, eng, name):
        eng.wait_ge(self.sem, self.at[name])


class Chain:

    def __init__(self, eng, sem, start=0):
        self.eng, self.sem, self.n = eng, sem, start

    def __call__(self, ins):
        self.n += 1
        ins.then_inc(self.sem, 1)
        self.eng.wait_ge(self.sem, self.n)


class Kernel:
    def __init__(self, nc, ins, outs):
        self.nc, self.i, self.o = nc, ins, outs
        self.top = ExitStack()
        self.live = []

    def sb(self, name, shape, dt=F32, ctx=None):
        size = 4
        for n in shape[1:]:
            size *= n
        size = -(-size // 32) * 32
        at = -(-self.nc.sbuf_base // 32) * 32
        for a, b in sorted(self.live):
            if at + size <= a:
                break
            at = max(at, b)
        assert at + size <= self.nc.sbuf_top, (name, size, sorted(self.live))
        span = (at, at + size)
        self.live.append(span)
        (ctx or self.top).callback(self.live.remove, span)
        return self.nc.alloc_sbuf_tensor_at(name, shape, dt, offset=at)

    def sem(self, name, ctx=None):
        return (ctx or self.stage).enter_context(self.nc.semaphore(name))

    def run(self, part):
        with ExitStack() as self.stage:
            part(self)

    def marks(self, name, names):
        return Marks(self.sem(name), list(names))

    def chain(self, eng, which):
        c = self.chains.get(which)
        if c is None:
            c = self.chains[which] = Chain(eng, self.sem("own_" + which, self.top))
        c.eng = eng
        return c


def build(nc, ins, outs):
    k = Kernel(nc, ins, outs)
    k.chains = {}
    with k.top:
        for which in ("vector", "scalar"):
            k.chain(None, which)
        k.bank = [k.top.enter_context(nc.psum_tensor(f"bank{b}", [128, 512], F32)) for b in range(8)]
        k.x = k.sb("x_rows", [128, 5, D])
        k.run(constants)
        with ExitStack() as mixer:
            k.mixer = mixer
            mixer_tensors(k)
            k.run(norm_and_transpose)
            conv_ctx = mixer.enter_context(ExitStack())
            k.conv_ctx = conv_ctx
            k.run(convolved_projections)
            k.run(delta_net)
            conv_ctx.close()
            k.ybh = k.sb("yb_hi", [128, H, NT], F32R, mixer)
            k.ybl = k.sb("yb_lo", [128, H, NT], F32R, mixer)
            k.yah = k.sb("ya_hi", [128, 4, NT], F32R, mixer)
            k.yal = k.sb("ya_lo", [128, 4, NT], F32R, mixer)
            k.run(attention)
            k.yb_ctx.close()
            k.run(merge_branches)
        k.run(route_and_experts)


def constants(k):
    nc, i = k.nc, k.i
    k.ident = k.sb("ident", [128, 128])
    k.ones = k.sb("ones", [128, 128])
    k.head_ones = k.sb("head_ones", [128, 128])
    k.triu = k.sb("triu", [128, 512])
    k.striu = k.sb("striu", [128, 128])
    k.later_neg = k.sb("later_neg", [128, 4, 128])
    k.causal_neg = k.sb("causal_neg", [128, 128])
    k.level = k.sb("level", [128, 7, 128])
    k.sel = k.sb("sel", [8, 8, 128])
    k.selpair = k.sb("selpair", [8, 4, 128])
    k.eps = k.sb("eps", [128, 1])
    k.one = k.sb("one", [128, 1])
    k.wconv = k.sb("wconv", [128, CONV_W, NCC])
    k.hist = k.sb("hist", [128, 3, NCC])
    k.gq = k.sb("gq", [128, 1])
    k.gk = k.sb("gk", [128, 1])
    k.go = k.sb("go", [128, 1])
    k.bgate = k.sb("bgate", [128, 16])
    k.sm_bias = k.sb("sm_bias", [128, 1])
    k.sm_sign = k.sb("sm_sign", [128, 1])
    k.sm_coef = k.sb("sm_coef", [128, 1])
    xi = k.sb("xor_i", [128, 128], I32)
    xj = k.sb("xor_j", [128, 128], I32)
    xs = k.sb("xor_s", [128, 128], I32)
    filled, loaded, ints = k.sem("const_filled"), k.sem("const_loaded"), k.sem("const_ints")
    done = k.sem("const_done")
    with nc.Block() as block:
        @block.vector
        def _(v):
            c = k.chain(v, "vector")
            c(nc.vector.memset(k.x[:, 0, :], 0.0))
            for t, val in ((k.ident, 0.0), (k.ones, 1.0), (k.head_ones, 0.0), (k.triu, 1.0), (k.striu, 1.0),
                           (k.later_neg, 0.0), (k.causal_neg, 0.0), (k.sel, 0.0), (k.selpair, 0.0),
                           (k.eps, EPS), (k.one, 1.0), (k.sm_bias, 0.0), (k.sm_sign, 0.0), (k.sm_coef, 0.0)):
                c(nc.vector.memset(t[tuple(slice(None) for _ in t.shape)], val))
            c(nc.vector.memset(k.head_ones[0:64, 0:64], 1.0))
            c(nc.vector.memset(k.head_ones[64:128, 64:128], 1.0))
            c(nc.vector.memset(k.sm_sign[0:8, :], -1.0))
            c(nc.vector.memset(k.sm_sign[32:40, :], -1.0))
            c(nc.vector.memset(k.sm_sign[64:72, :], 1.0))
            c(nc.vector.memset(k.sm_coef[0:40, :], -1.0))
            nc.vector.memset(k.sm_coef[64:72, :], -1.0).then_inc(filled, 1)
            v.wait_ge(ints, 2)
            c(nc.vector.tensor_tensor(xs[:], xi[:], xj[:], ALU.bitwise_xor))
            for l in range(7):
                c(nc.vector.tensor_scalar(xi[:], xs[:], l, None, ALU.logical_shift_right))
                c(nc.vector.tensor_scalar(k.level[:, l, :], xi[:], 1, None, ALU.is_equal))
            v.wait_ge(ints, 3)
            for l in range(7):
                c(nc.vector.tensor_tensor(k.level[:, l, :], k.level[:, l, :], k.striu[:], ALU.mult))

        @block.gpsimd
        def _(g):
            g.iota(xi[:], pattern=[[1, 128]], base=0, channel_multiplier=0).then_inc(ints, 1)
            g.iota(xj[:], pattern=[[0, 128]], base=0, channel_multiplier=1).then_inc(ints, 1)
            g.wait_ge(filled, 1)
            g.affine_select(out=k.striu[:], in_=k.striu[:], compare_op=ALU.is_gt, fill=0.0, base=0,
                            pattern=[[1, 128]], channel_multiplier=-1).then_inc(ints, 1)
            g.affine_select(out=k.triu[:], in_=k.triu[:], compare_op=ALU.is_ge, fill=0.0, base=0,
                            pattern=[[1, 512]], channel_multiplier=-1).then_inc(done, 1)
            g.affine_select(out=k.ident[:], in_=k.ident[:], compare_op=ALU.not_equal, fill=1.0, base=0,
                            pattern=[[1, 128]], channel_multiplier=-1).then_inc(done, 1)
            g.affine_select(out=k.later_neg[:], in_=k.later_neg[:], compare_op=ALU.is_ge, fill=NEG, base=0,
                            pattern=[[0, 4], [1, 128]], channel_multiplier=-1).then_inc(done, 1)
            g.affine_select(out=k.causal_neg[:], in_=k.causal_neg[:], compare_op=ALU.is_ge, fill=NEG, base=0,
                            pattern=[[-1, 128]], channel_multiplier=1).then_inc(done, 1)
            g.affine_select(out=k.sel[:], in_=k.sel[:], compare_op=ALU.not_equal, fill=1.0, base=0,
                            pattern=[[-1, 8], [0, 128]], channel_multiplier=1).then_inc(done, 1)
            g.affine_select(out=k.selpair[:].rearrange("r p (a m) -> r p a m", a=2),
                            in_=k.selpair[:].rearrange("r p (a m) -> r p a m", a=2),
                            compare_op=ALU.not_equal, fill=1.0, base=0,
                            pattern=[[-2, 4], [-1, 2], [0, 64]], channel_multiplier=1).then_inc(done, 1)

        @block.sync
        def _(sp):
            sp.wait_ge(filled, 1)
            with nc.allow_non_contiguous_dma(reason="small parameters"):
                loads = [
                    (k.x[0:NS, 0, :], i["x_sample"][0]),
                    (k.x[:, 1:5, :], i["x_prompt"][0].rearrange("(t p) d -> p t d", p=128)),
                    (k.gq[0:64, :], i["g_qnorm"].rearrange("o c -> c o")),
                    (k.gq[64:128, :], i["g_qnorm"].rearrange("o c -> c o")),
                    (k.gk[0:64, :], i["g_knorm"].rearrange("o c -> c o")),
                    (k.gk[64:128, :], i["g_knorm"].rearrange("o c -> c o")),
                    (k.go[:], i["g_onorm"].rearrange("o c -> c o")),
                    (k.bgate[:], i["b_gate"][0].rearrange("(c p) -> p c", p=128)),
                    (k.sm_bias[0:8, :], i["b_f"].rearrange("o c -> c o")),
                    (k.sm_bias[64:72, :], i["dt_bias"].rearrange("o c -> c o")),
                    (k.sm_coef[64:72, :], i["a_log"].rearrange("o c -> c o")),
                ]
                for w in range(CONV_W):
                    loads.append((k.wconv[:, w, :], i["w_conv"][0, w].rearrange("(c p) -> p c", p=128)))
                for w in range(3):
                    loads.append((k.hist[:, w, :], i["state_gdn_conv"][0, 0, w].rearrange("(c p) -> p c", p=128)))
                for dst, src in loads:
                    sp.dma_start(dst, src).then_inc(loaded, 16)
            sp.wait_ge(loaded, 16 * len(loads))
    with nc.Block() as block:
        @block.scalar
        def _(a):
            c = k.chain(a, "scalar")
            c(nc.scalar.activation(k.sm_coef[64:72, :], k.sm_coef[64:72, :], ACT.Exp))
            c(nc.scalar.activation(k.sm_coef[64:72, :], k.sm_coef[64:72, :], ACT.Copy, scale=-1.0))


def mixer_tensors(k):
    ctx = k.mixer
    k.xhi = k.sb("xhi", [128, KD, NT], F32R, ctx)
    k.xlo = k.sb("xlo", [128, KD, NT], F32R, ctx)
    k.yb_ctx = ctx.enter_context(ExitStack())
    k.yb = k.sb("yb", [128, H, NT], F32, k.yb_ctx)
    k.smt = k.sb("small_rows", [128, 5, 96], F32, ctx)


def norm_and_transpose(k):
    nc = k.nc
    with ExitStack() as ctx:
        junk = k.sb("nt_sq", [128, D], F32, ctx)
        stat = k.sb("nt_stat", [128, 3, 5], F32, ctx)
        xn = k.sb("nt_xn", [128, 2, D], F32, ctx)
        rt, rr = stat[:, 1], stat[:, 2]
        g_mix = k.sb("g_mix_rows", [128, D], F32, ctx)
        gain = k.sem("nt_gain")
        rms = k.sem("nt_rms")
        normed = k.sem("nt_normed")
        moved = k.sem("nt_moved")
        hi_done = k.sem("nt_hi")
        lo_done = k.sem("nt_lo")
        with nc.Block() as block:
            @block.sync
            def _(sp):
                sp.dma_start(g_mix[:], k.i["g_mix"].broadcast_to([128, D])).then_inc(gain, 16)

            @block.scalar
            def _(a):
                c = k.chain(a, "scalar")
                for t, (c0, n) in enumerate(TILES):
                    c(nc.scalar.activation(junk[0:n, :], k.x[0:n, t, :], ACT.Square, accum_out=stat[0:n, 0, t:t + 1]))
                for t, (c0, n) in enumerate(TILES):
                    nc.scalar.activation(rt[0:n, t:t + 1], stat[0:n, 0, t:t + 1], ACT.Sqrt, bias=k.eps[0:n, :],
                                         scale=1.0 / D).then_inc(rms, 1)
                for t, (c0, n) in enumerate(TILES):
                    a.wait_ge(moved, t + 1)
                    for b in range(2):
                        nc.scalar.activation(k.xhi[:, 4 * b:4 * b + 4, c0:c0 + n],
                                             k.bank[2 * (t % 2) + b][:, 0:4 * n].rearrange("p (k n) -> p k n", k=4),
                                             ACT.Copy).then_inc(hi_done, 1)

            @block.vector
            def _(v):
                c = k.chain(v, "vector")
                def normalise(t):
                    c0, n = TILES[t]
                    v.wait_ge(rms, t + 1)
                    c(nc.vector.reciprocal(rr[0:n, t:t + 1], rt[0:n, t:t + 1]))
                    if t >= 2:
                        v.wait_ge(moved, t - 1)
                    nc.vector.scalar_tensor_tensor(out=xn[0:n, t % 2, :], in0=k.x[0:n, t, :], scalar=rr[0:n, t:t + 1],
                                                   in1=g_mix[0:n, :], op0=ALU.mult, op1=ALU.mult).then_inc(normed, 1)
                v.wait_ge(gain, 16)
                normalise(0)
                for t, (c0, n) in enumerate(TILES):
                    if t + 1 < 5:
                        normalise(t + 1)
                    for b in range(2):
                        v.wait_ge(hi_done, 2 * t + b + 1)
                        nc.vector.tensor_tensor(k.xlo[:, 4 * b:4 * b + 4, c0:c0 + n],
                                                k.bank[2 * (t % 2) + b][:, 0:4 * n].rearrange("p (k n) -> p k n", k=4),
                                                k.xhi[:, 4 * b:4 * b + 4, c0:c0 + n].bitcast(F32),
                                                ALU.subtract).then_inc(lo_done, 1)

            @block.tensor
            def _(pe):
                for t, (c0, n) in enumerate(TILES):
                    pe.wait_ge(normed, t + 1)
                    if t >= 2:
                        pe.wait_ge(lo_done, 2 * (t - 1))
                    for d in range(KD):
                        last = nc.tensor.transpose(k.bank[2 * (t % 2) + d // 4][:, (d % 4) * n:(d % 4) * n + n],
                                                   xn[0:n, t % 2, 128 * d:128 * d + 128], k.ident[0:n, 0:n])
                    last.then_inc(moved, 1)


class Stream:

    def __init__(self, k, name, chunks, ctx, emptier=None):
        self.k, self.chunks = k, chunks
        k.raw = k.sb(name + "_w_raw", [128, 3, KD, 128], F32, ctx)
        k.whi = k.sb(name + "_w_hi", [128, 2, KD, 128], F32R, ctx)
        k.wlo = k.sb(name + "_w_lo", [128, 2, KD, 128], F32R, ctx)
        self.loaded = [k.sem(f"{name}_loaded{s}") for s in range(3)]
        self.hi = k.sem(name + "_hi")
        self.lo = k.sem(name + "_lo")
        self.half = k.sem(name + "_half")
        self.emptier = emptier or [0] * len(chunks)
        self.emptied = [k.sem(f"{name}_emptied{e}") for e in range(max(self.emptier) + 1)]
        self.nload = [0] * 3

    def emptied_of(self, c):
        return self.emptied[self.emptier[c]]

    def wait_emptied(self, eng, c, h):
        before = sum(1 for j in range(c) if self.emptier[j] == self.emptier[c])
        eng.wait_ge(self.emptied_of(c), 2 * before + h + 1)

    def load(self, sp, c):
        k = self.k
        srcs, nk = self.chunks[c][0], self.chunks[c][1]
        if c >= 3:
            sp.wait_ge(self.lo, c - 2)
        for dst0, src in srcs:
            w = src.shape[-1]
            sp.dma_start(k.raw[:, c % 3, 0:nk, dst0:dst0 + w], src).then_inc(self.loaded[c % 3], 16)

    def loads_of(self, c):
        return 16 * sum(len(self.chunks[j][0]) for j in range(c % 3, c + 1, 3))

    def split_hi(self, a, c):
        k, nk = self.k, self.chunks[c][1]
        a.wait_ge(self.loaded[c % 3], self.loads_of(c))
        if c >= 2:
            a.wait_ge(self.half, 2 * (c - 1))
        k.nc.scalar.activation(k.whi[:, c % 2, 0:nk, :], k.raw[:, c % 3, 0:nk, :], ACT.Copy).then_inc(self.hi, 1)

    def split_lo(self, g, c):
        k, nk = self.k, self.chunks[c][1]
        g.wait_ge(self.hi, c + 1)
        k.nc.gpsimd.tensor_tensor(k.wlo[:, c % 2, 0:nk, :], k.raw[:, c % 3, 0:nk, :],
                                  k.whi[:, c % 2, 0:nk, :].bitcast(F32), ALU.subtract).then_inc(self.lo, 1)

    def product(self, pe, c, halves=(0, 1)):
        k = self.k
        _, nk, xhi, xlo = self.chunks[c]
        pe.wait_ge(self.lo, c + 1)
        for h in halves:
            if c >= 1:
                self.wait_emptied(pe, c - 1, h)
            cols = slice(h * HALF, (h + 1) * HALF)
            for d in range(nk):
                for n, (w, x) in enumerate(((k.whi, xhi), (k.whi, xlo), (k.wlo, xhi))):
                    last = k.nc.tensor.matmul(k.bank[h][:, 0:HALF], w[:, c % 2, d, :], x[:, d, cols],
                                              start=(d == 0 and n == 0), stop=(d == nk - 1 and n == 2))
            last.then_inc(self.half, 1)


def w_in_cols(k, c0, n=128):
    return k.i["w_in"][0].rearrange("(k p) n -> p k n", p=128)[:, :, c0:c0 + n]


def convolved_projections(k):
    nc = k.nc
    ctx = k.conv_ctx
    k.cT = k.sb("conv_out", [128, NCC, NT], F32, ctx)
    with ExitStack() as ctx:
        k.sT = k.sb("small_cols", [96, NT], F32, ctx)
        tmp = k.sb("small_tmp", [96, 2, NT], F32, ctx)
        cin = k.sb("conv_in", [128, 2, 3 + NS + 3 + NP], F32, ctx)
        acc = k.sb("conv_acc", [128, 2, 3 + NS + NP], F32, ctx)
        last3 = k.sb("conv_last", [128, 6, NCC], F32, ctx)
        lastT = k.sb("conv_lastT", [96, 128], F32, ctx)
        W = 3 + NS + NP
        small = [(0, w_in_cols(k, C_LOGF, H)), (32, w_in_cols(k, C_BETA, H)), (64, w_in_cols(k, C_DECAY, H))]
        chunks = [([(0, w_in_cols(k, C_CONV + 128 * c))], KD, k.xhi, k.xlo) for c in range(NCC)]
        s = Stream(k, "cv", chunks + [(small, KD, k.xhi, k.xlo)], ctx)
        staged = k.sem("cv_staged")
        summed = k.sem("cv_summed")
        act_done = k.sem("cv_silu")
        zeroed = k.sem("cv_zeroed")
        kept = k.sem("cv_kept")

        def silu(a, c):
            a.wait_ge(summed, c + 1)
            nc.scalar.activation(k.cT[:, c, 0:NS], acc[:, c % 2, 0:NS], ACT.Silu)
            nc.scalar.activation(k.cT[:, c, NS:NT], acc[:, c % 2, 3 + NS:W], ACT.Silu).then_inc(act_done, 1)

        with nc.Block() as block:
            @block.sync
            def _(sp):
                with nc.allow_non_contiguous_dma(reason="eight columns"):
                    for c in range(NCC):
                        s.load(sp, c)
                    sp.wait_ge(s.lo, NCC - 2)
                    sp.wait_ge(zeroed, 1)
                    s.load(sp, NCC)

            @block.gpsimd
            def _(g):
                for c in range(NCC):
                    s.split_lo(g, c)
                    if c == NCC - 3:
                        g.wait_ge(s.lo, NCC - 2)
                        g.memset(k.raw[:, NCC % 3], 0.0).then_inc(zeroed, 1)
                s.split_lo(g, NCC)

            @block.tensor
            def _(pe):
                for c in range(NCC + 1):
                    s.product(pe, c)

            @block.scalar
            def _(a):
                c_ = k.chain(a, "scalar")
                s.split_hi(a, 0)
                for c in range(NCC):
                    s.split_hi(a, c + 1)
                    if c >= 2:
                        a.wait_ge(summed, c - 1)
                        a.wait_ge(kept, c - 1)
                    a.wait_ge(s.half, 2 * c + 1)
                    nc.scalar.activation(cin[:, c % 2, 3:3 + NS], k.bank[0][:, 0:NS], ACT.Copy)
                    nc.scalar.activation(cin[:, c % 2, 6 + NS:6 + HALF], k.bank[0][:, NS:HALF], ACT.Copy)\
                        .then_inc(s.emptied_of(c), 1)
                    a.wait_ge(s.half, 2 * c + 2)
                    nc.scalar.activation(cin[:, c % 2, 6 + HALF:6 + NT], k.bank[1][:, 0:HALF], ACT.Copy)\
                        .then_inc(s.emptied_of(c), 1)
                    if c >= 1:
                        silu(a, c - 1)
                silu(a, NCC - 1)

            @block.vector
            def _(v):
                c_ = k.chain(v, "vector")
                for b in range(2):
                    c_(nc.vector.memset(cin[:, b, 3 + NS:6 + NS], 0.0))
                for c in range(NCC):
                    ci, ac = cin[:, c % 2], acc[:, c % 2]
                    c_(nc.vector.tensor_copy(ci[:, 0:3], k.hist[:, :, c]))
                    s.wait_emptied(v, c, 1)
                    if c >= 2:
                        v.wait_ge(act_done, c - 1)
                    c_(nc.vector.tensor_scalar(ac[:, 0:W], ci[:, 0:W], k.wconv[:, 0, c:c + 1], None, ALU.mult))
                    for w in range(1, CONV_W):
                        op = nc.vector.scalar_tensor_tensor(out=ac[:, 0:W], in0=ci[:, w:w + W],
                                                            scalar=k.wconv[:, w, c:c + 1], in1=ac[:, 0:W],
                                                            op0=ALU.mult, op1=ALU.add)
                        if w < CONV_W - 1:
                            c_(op)
                        else:
                            op.then_inc(summed, 1)
                    nc.vector.tensor_copy(last3[:, 0:3, c], ci[:, NS:NS + 3])
                    nc.vector.tensor_copy(last3[:, 3:6, c], ci[:, 3 + NT:6 + NT]).then_inc(kept, 1)
                    v.wait_ge(kept, c + 1)
                for h in range(2):
                    v.wait_ge(s.half, 2 * NCC + h + 1)
                    c_(nc.vector.tensor_scalar(k.sT[:, h * HALF:(h + 1) * HALF], k.bank[h][0:96, 0:HALF],
                                               k.sm_bias[0:96, :], k.sm_sign[0:96, :], ALU.add, ALU.mult))
        e_done, l_done, d_done, tr, trc = (k.sem("sm_" + n) for n in ("exp", "ln", "rows", "tr", "trc"))
        stored = k.sem("sm_stored")
        with nc.Block() as block:
            @block.scalar
            def _(a):
                c = k.chain(a, "scalar")
                c(nc.scalar.activation(tmp[:, 0, :], k.sT[:], ACT.Abs))
                c(nc.scalar.activation(tmp[:, 1, :], tmp[:, 0, :], ACT.Exp, scale=-1.0))
                nc.scalar.activation(tmp[:, 0, :], tmp[:, 1, :], ACT.Ln, bias=k.one[0:96, :]).then_inc(l_done, 1)

            @block.vector
            def _(v):
                c = k.chain(v, "vector")
                v.wait_ge(l_done, 1)
                c(nc.vector.scalar_tensor_tensor(out=tmp[:, 1, :], in0=k.sT[:], scalar=0.0, in1=tmp[:, 0, :],
                                                 op0=ALU.max, op1=ALU.add))
                nc.vector.tensor_scalar(k.sT[:], tmp[:, 1, :], k.sm_coef[0:96, :], None, ALU.mult).then_inc(d_done, 1)
                v.wait_ge(tr, 1)
                c(nc.vector.tensor_copy(k.smt[:, 1:5, :], k.bank[2][:, 0:384].rearrange("p (t m) -> p t m", t=4)))
                c(nc.vector.tensor_copy(k.smt[0:NS, 0, :], k.bank[3][0:NS, 0:96]))
                nc.vector.tensor_copy(lastT[:], k.bank[4][0:96, 0:128]).then_inc(trc, 1)

            @block.tensor
            def _(pe):
                pe.wait_ge(d_done, 1)
                for t, (c0, n) in enumerate(TILES):
                    out = k.bank[3][0:NS, 0:96] if t == 0 else k.bank[2][:, 96 * (t - 1):96 * t]
                    nc.tensor.transpose(out, k.sT[:, c0:c0 + n], k.ident[0:96, 0:96])
                nc.tensor.transpose(k.bank[4][0:96, 0:128], last3[:].rearrange("p a c -> p (a c)"),
                                    k.ident[:, :]).then_inc(tr, 1)

            @block.sync
            def _(sp):
                sp.wait_ge(trc, 1)
                sp.dma_start(k.o["conv_s"][0, 0].rearrange("w (c m) -> (w c) m", m=128), lastT[0:48, :]).then_inc(stored, 16)
                sp.dma_start(k.o["conv_p"][0, 0].rearrange("w (c m) -> (w c) m", m=128), lastT[48:96, :]).then_inc(stored, 16)
                sp.dma_start(k.o["logf_s"][0, 0], k.smt[0:NS, 0, 0:H]).then_inc(stored, 16)
                sp.dma_start(k.o["logf_p"][0, 0].rearrange("(t p) h -> p t h", p=128), k.smt[:, 1:5, 0:H])\
                    .then_inc(stored, 16)
                sp.wait_ge(stored, 64)
    head_norm(k, "l2", [(k.cT, c, DH ** -0.5 if c < 4 else 1.0, None) for c in range(8)], 1.0)


def head_norm(k, name, items, mean_scale, ones=None):
    nc, ones = k.nc, ones or k.head_ones
    with ExitStack() as ctx:
        sq = k.sb(name + "_sq", [128, 2, NT], F32, ctx)
        rt = k.sb(name + "_rt", [128, 2, NT], F32, ctx)
        squared, summed, rooted, scaled = (k.sem(f"{name}_{n}") for n in ("squared", "summed", "rooted", "scaled"))
        n = len(items)
        with nc.Block() as block:
            @block.gpsimd
            def _(g):
                for j, (T, c, f, gain) in enumerate(items):
                    if j >= 2:
                        g.wait_ge(summed, j - 1)
                    nc.gpsimd.tensor_tensor(sq[:, j % 2, :], T[:, c, :], T[:, c, :], ALU.mult).then_inc(squared, 1)

            @block.tensor
            def _(pe):
                for j in range(n):
                    pe.wait_ge(squared, j + 1)
                    if j >= 2:
                        pe.wait_ge(rooted, j - 1)
                    for h in range(2):
                        last = nc.tensor.matmul(k.bank[2 * (j % 2) + h][:, 0:HALF], ones[:],
                                                sq[:, j % 2, h * HALF:(h + 1) * HALF], start=True, stop=True)
                    last.then_inc(summed, 1)

            @block.scalar
            def _(a):
                for j in range(n):
                    a.wait_ge(summed, j + 1)
                    if j >= 2:
                        a.wait_ge(scaled, j - 1)
                    for h in range(2):
                        last = nc.scalar.activation(rt[:, j % 2, h * HALF:(h + 1) * HALF],
                                                    k.bank[2 * (j % 2) + h][:, 0:HALF], ACT.Sqrt,
                                                    bias=k.eps[:], scale=mean_scale)
                    last.then_inc(rooted, 1)

            @block.vector
            def _(v):
                c_ = k.chain(v, "vector")
                for j, (T, c, f, gain) in enumerate(items):
                    v.wait_ge(rooted, j + 1)
                    c_(nc.vector.reciprocal(rt[:, j % 2, :], rt[:, j % 2, :]))
                    if gain is not None:
                        c_(nc.vector.tensor_scalar(rt[:, j % 2, :], rt[:, j % 2, :], gain[:], None, ALU.mult))
                    nc.vector.scalar_tensor_tensor(out=T[:, c, :], in0=T[:, c, :], scalar=f, in1=rt[:, j % 2, :],
                                                   op0=ALU.mult, op1=ALU.mult).then_inc(scaled, 1)


def delta_net(k):
    nc = k.nc
    with ExitStack() as ctx:
        beta, G, nG, Gt, eG, egl, kf = (k.sb("g_" + n, [128, 5, H], F32, ctx)
                                        for n in ("beta", "cum", "ncum", "total", "exp", "exptot", "tail"))
        GT = k.sb("g_cols", [H, NT], F32, ctx)
        kg = k.sb("k_grown", [128, 5, WA], F32, ctx)
        kd = k.sb("k_tail", [128, 5, WA], F32, ctx)
        S = k.sb("state_p", [128, 4, DV], F32, ctx)
        Ss = k.sb("state_s", [128, 4, DV], F32, ctx)
        smask = k.sb("later_neg_s", [NS, 4, NS], F32, ctx)
        summed, cum, grown, kT, kread, loaded = (k.sem("g0_" + n) for n in ("sum", "cum", "exp", "kT", "kread", "state"))
        parts = [(slice(0, NS), slice(0, 1)), (slice(0, 128), slice(1, 5))]
        with nc.Block() as block:
            @block.sync
            def _(sp):
                for a in range(2):
                    sp.dma_start(Ss[64 * a:64 * a + 64], k.i["state_gdn"][0, 0].rearrange("(p a) k v -> a k p v", a=2)[a])\
                        .then_inc(loaded, 16)
                sp.wait_ge(loaded, 32)

            @block.tensor
            def _(pe):
                g = k.smt[:, :, 64:72]
                for t, (c0, n) in enumerate(TILES):
                    out = k.bank[1][0:n, 0:H] if t == 0 else k.bank[0][:, H * (t - 1):H * t]
                    nc.tensor.matmul(out, k.triu[0:n, 0:n], g[0:n, t, :], start=True, stop=True)
                    nc.tensor.matmul(k.bank[2][:, H * t:H * t + H], k.ones[0:n, :], g[0:n, t, :], start=True, stop=True)
                    out = k.bank[3][0:H, 0:n] if t == 0 else k.bank[4][0:H, 128 * (t - 1):128 * t]
                    last = nc.tensor.matmul(out, g[0:n, t, :], k.triu[0:n, 0:n], start=True, stop=True)
                last.then_inc(summed, 1)
                for p in range(4):
                    if p >= 2:
                        pe.wait_ge(kread, p - 1)
                    b = (5, 7)[p % 2]
                    b0 = (6, 1)[p % 2]
                    if p == 1:
                        pe.wait_ge(cum, 1)
                    for t, (c0, n) in enumerate(TILES):
                        out = k.bank[b0][0:n, 0:128] if t == 0 else k.bank[b][:, 128 * (t - 1):128 * t]
                        last = nc.tensor.transpose(out, k.cT[:, 4 + p, c0:c0 + n], k.ident[:])
                    last.then_inc(kT, 1)

            @block.vector
            def _(v):
                c = k.chain(v, "vector")
                c(nc.vector.memset(smask[:], 0.0))
                v.wait_ge(summed, 1)
                c(nc.vector.tensor_copy(G[0:NS, 0], k.bank[1][0:NS, 0:H]))
                c(nc.vector.tensor_copy(G[:, 1:5], k.bank[0][:, 0:4 * H].rearrange("p (t h) -> p t h", t=4)))
                c(nc.vector.tensor_copy(Gt[:], k.bank[2][:, 0:5 * H].rearrange("p (t h) -> p t h", t=5)))
                c(nc.vector.tensor_copy(GT[:, 0:NS], k.bank[3][0:H, 0:NS]))
                c(nc.vector.tensor_copy(GT[:, NS:NT], k.bank[4][0:H, 0:NP]))
                c(nc.vector.tensor_copy(smask[:], k.later_neg[0:NS, :, 0:NS]))
                for rows, ts in parts:
                    c(nc.vector.tensor_tensor(kf[rows, ts], Gt[rows, ts], G[rows, ts], ALU.subtract))
                    c(nc.vector.tensor_scalar(nG[rows, ts], G[rows, ts], -1.0, None, ALU.mult))
                nc.vector.memset(S[:], 0.0).then_inc(cum, 1)
                v.wait_ge(grown, 1)
                for p in range(4):
                    v.wait_ge(kT, p + 1)
                    b = (5, 7)[p % 2]
                    b0 = (6, 1)[p % 2]
                    for f, dst in ((eG, kg), (kf, kd)):
                        fac = f[:, :, 2 * p:2 * p + 2].unsqueeze(3)
                        nc.vector.tensor_tensor(
                            dst[0:NS, 0, 128 * p:128 * p + 128].rearrange("p (a c) -> p a c", a=2),
                            k.bank[b0][0:NS, 0:128].rearrange("p (a c) -> p a c", a=2),
                            fac[0:NS, 0].broadcast_to([NS, 2, 64]), ALU.mult)
                        last = nc.vector.tensor_tensor(
                            dst[:, 1:5, 128 * p:128 * p + 128].rearrange("p t (a c) -> p t a c", a=2),
                            k.bank[b][:].rearrange("p (t a c) -> p t a c", t=4, a=2),
                            fac[:, 1:5].broadcast_to([128, 4, 2, 64]), ALU.mult)
                    last.then_inc(kread, 1)

            @block.scalar
            def _(a):
                c = k.chain(a, "scalar")
                for rows, ts in parts:
                    c(nc.scalar.activation(beta[rows, ts], k.smt[rows, ts, 32:40], ACT.Exp))
                a.wait_ge(cum, 1)
                for rows, ts in parts:
                    c(nc.scalar.activation(eG[rows, ts], G[rows, ts], ACT.Exp))
                    c(nc.scalar.activation(kf[rows, ts], kf[rows, ts], ACT.Exp))
                nc.scalar.activation(egl[:], Gt[:], ACT.Exp).then_inc(grown, 1)

        def units(r, a):
            if r == 0:
                return [(2 * u + a, 0, 0) for u in range(4)]
            return [(2 * (r - 1) + a, t, TILES[t][0]) for t in range(1, 5)]

        R, A, U = range(5), range(2), range(4)
        width = lambda r: NS if r == 0 else 128
        levels = lambda r: range(5 if r == 0 else 7)
        base = lambda h: 64 * (h % 2)
        st = lambda r: Ss if r == 0 else S
        ra = [(r, a) for r in R for a in A]
        ral = [(r, l, a) for r in R for l in levels(r) for a in A]
        rua = [(r, u, a) for r in R for u in U for a in A]
        m = {n: k.marks("g_" + n, names) for n, names in dict(
            scores=ra, low=ral, grown=[x for x in ral if x[1] > 0], wt=ra, vsum=rua, upd=rua, egp=R, vT=ra,
            dec=ra, lowc=[x for x in ral if x[1] > 0], wtc=ra, outc=ra, egx=R, vtok=ra,
            mt=ra, inv=ral, vnew=rua, state=rua,
            ml=ral, qd=R).items()}
        dec, mt, at, P, X, Xt, wT, vt = (k.sb("g_" + n, [128, 2, 512], F32, ctx)
                                         for n in ("dec", "mt", "at", "low", "inv", "invT", "wT", "vt"))
        ml = k.sb("g_ml", [128, 2, 2, 512], F32, ctx)
        qd = k.sb("g_qd", [128, 512], F32, ctx)
        egp = k.sb("g_egp", [128, 512], F32, ctx)
        vn = k.sb("g_vn", [128, 2, DV], F32, ctx)
        stored = k.sem("g_stored")
        bank = lambda a, n: k.bank[4 * a + n]
        qcols = lambda r, h, t: slice(NS * (h // 2), NS * (h // 2) + NS) if r == 0 else slice(128 * (t - 1), 128 * t)
        with nc.Block() as block:
            @block.tensor
            def _(pe):
                for r in R:
                    w = width(r)
                    if r >= 1:
                        m["outc"].wait(pe, (r - 1, 0))
                    if r == 0:
                        for p in range(4):
                            last = nc.tensor.matmul(bank(0, 3)[:, NS * p:NS * p + NS], k.selpair[:, p, :], GT[:, 0:NS],
                                                    start=True, stop=True)
                    else:
                        last = nc.tensor.matmul(bank(0, 3)[:], k.selpair[:, r - 1, :], GT[:, NS:NT], start=True, stop=True)
                    m["egp"].mark(last, r)
                    for a in A:
                        for u, (h, t, c0) in enumerate(units(r, a)):
                            b, cols, o = base(h), slice(c0, c0 + w), slice(u * w, u * w + w)
                            kT_, qT_ = k.cT[b:b + 64, 4 + h // 2, cols], k.cT[b:b + 64, h // 2, cols]
                            nc.tensor.matmul(bank(a, 0)[0:w, o], kT_, kT_, start=True, stop=True)
                            nc.tensor.matmul(bank(a, 1)[0:w, o], kT_, qT_, start=True, stop=True)
                        neg = smask[:] if r == 0 else k.later_neg[:]
                        if r >= 1:
                            m["state"].wait(pe, (r - 1, 3, a))
                        nc.tensor.matmul(bank(a, 2)[0:w, 0:4 * w], k.ident[0:w, 0:w], neg, start=True, stop=False)
                        if r == 0:
                            for u, (h, t, c0) in enumerate(units(r, a)):
                                last = nc.tensor.matmul(bank(a, 2)[0:w, u * w:u * w + w], k.sel[:, h, 0:w], GT[:, 0:NS],
                                                        start=False, stop=(u == 3))
                        else:
                            last = nc.tensor.matmul(bank(a, 2)[:], k.sel[:, units(r, a)[0][0], :], GT[:, NS:NT],
                                                    start=False, stop=True)
                        m["scores"].mark(last, (r, a))
                    m["egx"].wait(pe, r)
                    for a in A:
                        if r >= 1:
                            m["outc"].wait(pe, (r - 1, a))
                        for u, (h, t, c0) in enumerate(units(r, a)):
                            last = nc.tensor.transpose(bank(a, 3)[0:w, u * 128:u * 128 + 128], k.cT[:, 8 + h, c0:c0 + w],
                                                       k.ident[:])
                        m["vT"].mark(last, (r, a))
                    for l in levels(r):
                        for a in A:
                            m["ml"].wait(pe, (r, l, a))
                            if l >= 1:
                                m["inv"].wait(pe, (r, l - 1, a))
                            for u in U:
                                o = slice(u * w, u * w + w)
                                rhs = k.ident[0:w, 0:w] if l == 0 else X[0:w, a, o]
                                last = nc.tensor.matmul(bank(a, 0)[0:w, o], ml[0:w, a, l % 2, o], rhs, start=True, stop=True)
                            m["low"].mark(last, (r, l, a))
                        if l == 0:
                            continue
                        for a in A:
                            m["lowc"].wait(pe, (r, l, a))
                            for u in U:
                                o = slice(u * w, u * w + w)
                                if l < levels(r)[-1]:
                                    nc.tensor.matmul(bank(a, 1)[0:w, o], Xt[0:w, a, o], P[0:w, a, o], start=True, stop=True)
                                last = nc.tensor.matmul(bank(a, 2)[0:w, o], P[0:w, a, o], Xt[0:w, a, o], start=True, stop=True)
                            m["grown"].mark(last, (r, l, a))
                    for a in A:
                        m["inv"].wait(pe, (r, levels(r)[-1], a))
                        for u, (h, t, c0) in enumerate(units(r, a)):
                            b = base(h)
                            last = nc.tensor.matmul(bank(a, 0)[b:b + 64, u * w:u * w + w], kg[0:w, t, 64 * h:64 * h + 64],
                                                    Xt[0:w, a, u * w:u * w + w], start=True, stop=True)
                        m["wt"].mark(last, (r, a))
                    for u in U:
                        for a in A:
                            h, t, c0 = units(r, a)[u]
                            b, o = base(h), slice(u * w, u * w + w)
                            first = r > 0 and u == 0
                            if u == 0:
                                m["wtc"].wait(pe, (r, a))
                                m["vtok"].wait(pe, (r, a))
                            elif r > 0:
                                m["state"].wait(pe, (r, u - 1, a))
                            if u > 0:
                                m["vnew"].wait(pe, (r, u - 1, a))
                            last = nc.tensor.matmul(bank(a, 1)[0:w, 0:DV], Xt[0:w, a, o], vt[0:w, a, u * DV:u * DV + DV],
                                                    start=True, stop=first)
                            if not first:
                                last = nc.tensor.matmul(bank(a, 1)[0:w, 0:DV], wT[b:b + 64, a, o],
                                                        st(r)[b:b + 64, h // 2, :], start=False, stop=True)
                            m["vsum"].mark(last, (r, u, a))
                        for a in A:
                            h, t, c0 = units(r, a)[u]
                            b, o = base(h), slice(u * w, u * w + w)
                            first = r > 0 and u == 0
                            if not first:
                                nc.tensor.matmul(bank(a, 3)[:, o], st(r)[b:b + 64, h // 2, :],
                                                 qd[b:b + 64, qcols(r, h, t)], start=True, stop=False)
                            m["vnew"].wait(pe, (r, u, a))
                            nc.tensor.matmul(bank(a, 3)[:, o], vn[0:w, a, :], at[0:w, a, o], start=first, stop=True)
                            if u > 0:
                                m["state"].wait(pe, (r, u - 1, a))
                            last = nc.tensor.matmul(bank(a, 2)[b:b + 64, 0:DV], kd[0:w, t, 64 * h:64 * h + 64],
                                                    vn[0:w, a, :], start=True, stop=True)
                            m["upd"].mark(last, (r, u, a))

            @block.scalar
            def _(s):
                for r in R:
                    w = width(r)
                    m["egp"].wait(s, r)
                    if r >= 1:
                        m["qd"].wait(s, r - 1)
                    m["egx"].mark(nc.scalar.activation(egp[:, 0:4 * w], bank(0, 3)[:, 0:4 * w], ACT.Exp), r)
                    for a in A:
                        m["scores"].wait(s, (r, a))
                        for u, (h, t, c0) in enumerate(units(r, a)):
                            o = slice(u * w, u * w + w)
                            last = nc.scalar.activation(dec[0:w, a, o], bank(a, 2)[0:w, o], ACT.Exp, bias=nG[0:w, t, h:h + 1])
                        m["dec"].mark(last, (r, a))
                    for a in A:
                        m["vT"].wait(s, (r, a))
                        m["vtok"].mark(nc.scalar.activation(vt[0:w, a, :], bank(a, 3)[0:w, :], ACT.Copy), (r, a))
                    for l in levels(r)[1:]:
                        for a in A:
                            m["low"].wait(s, (r, l, a))
                            m["lowc"].mark(nc.scalar.activation(P[0:w, a, 0:4 * w], bank(a, 0)[0:w, 0:4 * w], ACT.Copy),
                                           (r, l, a))
                    for a in A:
                        m["wt"].wait(s, (r, a))
                        b = 64 * a
                        last = nc.scalar.activation(wT[b:b + 64, a, 0:4 * w], bank(a, 0)[b:b + 64, 0:4 * w], ACT.Copy,
                                                    scale=-1.0)
                        m["wtc"].mark(last, (r, a))
                    for a in A:
                        m["upd"].wait(s, (r, 3, a))
                        if r == 0:
                            out, src = k.yb[:, a::2, 0:NS], bank(a, 3)[:, 0:128].rearrange("p (h n) -> p h n", h=4)
                        else:
                            out, src = k.yb[:, 2 * (r - 1) + a, NS:NT], bank(a, 3)[:]
                        m["outc"].mark(nc.scalar.activation(out, src, ACT.Copy), (r, a))

            @block.vector
            def _(v):
                c = k.chain(v, "vector")
                for r in R:
                    w = width(r)
                    idb = k.ident[0:w, 0:w].unsqueeze(1).broadcast_to([w, 4, w])
                    for a in A:
                        m["dec"].wait(v, (r, a))
                        for u, (h, t, c0) in enumerate(units(r, a)):
                            o = slice(u * w, u * w + w)
                            nc.vector.scalar_tensor_tensor(out=mt[0:w, a, o], in0=bank(a, 0)[0:w, o],
                                                           scalar=beta[0:w, t, h:h + 1], in1=dec[0:w, a, o],
                                                           op0=ALU.mult, op1=ALU.mult)
                        m["mt"].mark(nc.vector.tensor_tensor(at[0:w, a, 0:4 * w], bank(a, 1)[0:w, 0:4 * w],
                                                             dec[0:w, a, 0:4 * w], ALU.mult), (r, a))
                    for l in levels(r):
                        for a in A:
                            f = slice(0, 4 * w)
                            if l == 0:
                                m["low"].wait(v, (r, l, a))
                                nc.vector.tensor_tensor(X[0:w, a, f].rearrange("p (u n) -> p u n", u=4), idb,
                                                        bank(a, 0)[0:w, f].rearrange("p (u n) -> p u n", u=4), ALU.subtract)
                                last = nc.vector.tensor_tensor(Xt[0:w, a, f].rearrange("p (u n) -> p u n", u=4), idb,
                                                               ml[0:w, a, 0, f].rearrange("p (u n) -> p u n", u=4),
                                                               ALU.subtract)
                            else:
                                m["grown"].wait(v, (r, l, a))
                                if l < levels(r)[-1]:
                                    nc.vector.tensor_tensor(X[0:w, a, f], X[0:w, a, f], bank(a, 1)[0:w, f], ALU.subtract)
                                last = nc.vector.tensor_tensor(Xt[0:w, a, f], Xt[0:w, a, f], bank(a, 2)[0:w, f],
                                                               ALU.subtract)
                            m["inv"].mark(last, (r, l, a))
                    for u in U:
                        for a in A:
                            h, t, c0 = units(r, a)[u]
                            m["vsum"].wait(v, (r, u, a))
                            if u > 0:
                                m["upd"].wait(v, (r, u - 1, a))
                            m["vnew"].mark(nc.vector.tensor_scalar(vn[0:w, a, :], bank(a, 1)[0:w, 0:DV],
                                                                   beta[0:w, t, h:h + 1], None, ALU.mult), (r, u, a))
                        for a in A:
                            h, t, c0 = units(r, a)[u]
                            b = base(h)
                            m["upd"].wait(v, (r, u, a))
                            if u > 0:
                                m["state"].wait(v, (r, u - 1, a))
                            m["state"].mark(nc.vector.scalar_tensor_tensor(
                                out=st(r)[b:b + 64, h // 2, :], in0=st(r)[b:b + 64, h // 2, :],
                                scalar=egl[b:b + 64, t, h:h + 1], in1=bank(a, 2)[b:b + 64, 0:DV],
                                op0=ALU.mult, op1=ALU.add), (r, u, a))

            @block.gpsimd
            def _(g):
                for r in R:
                    w = width(r)
                    m["egx"].wait(g, r)
                    if r >= 1:
                        m["upd"].wait(g, (r - 1, 3, 1))
                    if r == 0:
                        q, e = qd[:, 0:4 * w].rearrange("p (c n) -> p c n", c=4), egp[:, 0:4 * w].rearrange("p (c n) -> p c n", c=4)
                        m["qd"].mark(nc.gpsimd.tensor_tensor(q, k.cT[:, 0:4, 0:NS], e, ALU.mult), r)
                    else:
                        m["qd"].mark(nc.gpsimd.tensor_tensor(qd[:], k.cT[:, r - 1, NS:NT], egp[:], ALU.mult), r)
                    for l in levels(r):
                        for a in A:
                            if l == 0:
                                m["mt"].wait(g, (r, a))
                            if l >= 2:
                                m["low"].wait(g, (r, l - 2, a))
                            if l == 2:
                                m["inv"].wait(g, (r, 0, a))
                            f = slice(0, 4 * w)
                            m["ml"].mark(nc.gpsimd.tensor_tensor(
                                ml[0:w, a, l % 2, f].rearrange("p (u n) -> p u n", u=4),
                                mt[0:w, a, f].rearrange("p (u n) -> p u n", u=4),
                                k.level[0:w, l, 0:w].unsqueeze(1).broadcast_to([w, 4, w]), ALU.mult), (r, l, a))

            @block.sync
            def _(sp):
                for r, src, name in ((0, Ss, "state_s"), (4, S, "state_p")):
                    m["state"].wait(sp, (r, 3, 1))
                    for a in range(2):
                        sp.dma_start(k.o[name][0, 0].rearrange("(p a) k v -> a k p v", a=2)[a], src[64 * a:64 * a + 64])\
                            .then_inc(stored, 16)
                sp.wait_ge(stored, 64)


def attention(k):
    nc = k.nc
    head_norm(k, "on", [(k.yb, h, 1.0, k.go) for h in range(H)], 1.0 / DV, k.ones)
    with ExitStack() as ctx:
        fT = k.sb("fox_cols", [128, 12, NT], F32, ctx)
        with ExitStack() as inner:
            zs = k.sb("z_silu", [128, 2, NT], F32, inner)
            chunks = [([(0, w_in_cols(k, C_FQ + 128 * c))], KD, k.xhi, k.xlo) for c in range(12)]
            chunks += [([(0, w_in_cols(k, C_Z + 128 * c))], KD, k.xhi, k.xlo) for c in range(H)]
            s = Stream(k, "fz", chunks, inner)
            gate, hi, lo = k.sem("z_gated"), k.sem("z_hi"), k.sem("z_lo")
            with nc.Block() as block:
                @block.sync
                def _(sp):
                    for c in range(20):
                        s.load(sp, c)

                @block.gpsimd
                def _(g):
                    for c in range(20):
                        s.split_lo(g, c)

                @block.tensor
                def _(pe):
                    for c in range(20):
                        s.product(pe, c)

                def high(a, h):
                    a.wait_ge(gate, h + 1)
                    nc.scalar.activation(k.ybh[:, h, :], k.yb[:, h, :], ACT.Copy).then_inc(hi, 1)

                @block.scalar
                def _(a):
                    s.split_hi(a, 0)
                    for c in range(20):
                        if c + 1 < 20:
                            s.split_hi(a, c + 1)
                        if c >= 14:
                            a.wait_ge(gate, c - 13)
                        for h in range(2):
                            cols = slice(h * HALF, (h + 1) * HALF)
                            a.wait_ge(s.half, 2 * c + h + 1)
                            out = fT[:, c, cols] if c < 12 else zs[:, c % 2, cols]
                            nc.scalar.activation(out, k.bank[h][:, 0:HALF], ACT.Copy if c < 12 else ACT.Silu)\
                                .then_inc(s.emptied_of(c), 1)
                        if c >= 13:
                            high(a, c - 13)
                    high(a, H - 1)

                @block.vector
                def _(v):
                    for h in range(H):
                        s.wait_emptied(v, 12 + h, 1)
                        nc.vector.tensor_tensor(k.yb[:, h, :], k.yb[:, h, :], zs[:, h % 2, :], ALU.mult)\
                            .then_inc(gate, 1)
                        v.wait_ge(hi, h + 1)
                        nc.vector.tensor_tensor(k.ybl[:, h, :], k.yb[:, h, :], k.ybh[:, h, :].bitcast(F32),
                                                ALU.subtract).then_inc(lo, 1)
        head_norm(k, "qk", [(fT, c, DH ** -0.5 if c < 4 else 1.0, k.gq if c < 4 else k.gk) for c in range(8)], 1.0 / DH)

        vt = k.sb("fox_v", [128, 5, WA], F32, ctx)
        vp = k.sb("fox_vpast", [128, WA], F32, ctx)
        kTs = k.sb("fox_kT_s", [128, 4, PAST + NS], F32, ctx)
        ncT = k.sb("fox_nc", [H, PAST + NS + NP], F32, ctx)
        with ExitStack() as inner:
            kt = k.sb("fox_k", [128, 2, WA], F32, inner)
            kp = k.sb("fox_kpast", [128, WA], F32, inner)
            lp = k.sb("fox_logf_past", [128, H], F32, inner)
            loaded, tr, kc, vc, rest, restc, stored = (k.sem("f1_" + n) for n in
                                                       ("loaded", "tr", "kcopy", "vcopy", "rest", "restcopy", "stored"))
            with nc.Block() as block:
                @block.sync
                def _(sp):
                    sp.dma_start(kp[:], k.i["cache_fox_k"][0, 0].rearrange("p h c -> p (h c)")).then_inc(loaded, 16)
                    sp.dma_start(vp[:], k.i["cache_fox_v"][0, 0].rearrange("p h c -> p (h c)")).then_inc(loaded, 16)
                    sp.dma_start(lp[:], k.i["cache_fox_logf"][0, 0]).then_inc(loaded, 16)
                    for t, (c0, n) in enumerate(TILES):
                        for what, src, sem in (("k", kt[0:n, t % 2, :], kc), ("v", vt[0:n, t, :], vc)):
                            sp.wait_ge(sem, t + 1)
                            dst = k.o[what + ("_s" if t == 0 else "_p")][0, 0].rearrange("t h c -> t (h c)")
                            dst = dst if t == 0 else dst[128 * (t - 1):128 * t, :]
                            sp.dma_start(dst, src).then_inc(stored, 16)
                        sp.wait_ge(stored, 32 * (t + 1))
                    sp.wait_ge(loaded, 48)

                @block.tensor
                def _(pe):
                    for t, (c0, n) in enumerate(TILES):
                        if t >= 2:
                            pe.wait_ge(kc, t - 1)
                            pe.wait_ge(vc, t - 1)
                        for part in (4, 8):
                            b = k.bank[2 * (t % 2) + (part == 8)]
                            for c in range(4):
                                last = nc.tensor.transpose(b[0:n, 128 * c:128 * c + 128], fT[:, part + c, c0:c0 + n],
                                                           k.ident[:])
                        last.then_inc(tr, 1)
                    pe.wait_ge(loaded, 48)
                    for c in range(4):
                        nc.tensor.transpose(k.bank[4][:, 128 * c:128 * c + 128], kp[:, 128 * c:128 * c + 128], k.ident[:])
                    for j in range(4):
                        nc.tensor.matmul(k.bank[5][0:H, 128 * j:NP], k.smt[:, 1 + j, 0:H], k.triu[:, 0:NP - 128 * j],
                                         start=(j == 0), stop=(j == 3))
                    nc.tensor.matmul(k.bank[6][0:H, 0:PAST + NS], lp[:], k.triu[:, 0:PAST + NS], start=True, stop=False)
                    nc.tensor.matmul(k.bank[6][0:H, PAST:PAST + NS], k.smt[0:NS, 0, 0:H], k.triu[0:NS, 0:NS],
                                     start=False, stop=True).then_inc(rest, 1)

                @block.vector
                def _(v):
                    for t, (c0, n) in enumerate(TILES):
                        v.wait_ge(tr, t + 1)
                        if t >= 2:
                            v.wait_ge(stored, 32 * (t - 1))
                        nc.vector.tensor_copy(kt[0:n, t % 2, :], k.bank[2 * (t % 2)][0:n, :]).then_inc(kc, 1)
                    v.wait_ge(rest, 1)
                    nc.vector.tensor_copy(kTs[:, :, 0:PAST], k.bank[4][:].rearrange("p (c n) -> p c n", c=4))
                    nc.vector.tensor_copy(kTs[:, :, PAST:PAST + NS], fT[:, 4:8, 0:NS])
                    nc.vector.tensor_scalar(ncT[:, 0:PAST + NS], k.bank[6][0:H, 0:PAST + NS], -1.0, None, ALU.mult)
                    nc.vector.tensor_scalar(ncT[:, PAST + NS:], k.bank[5][0:H, :], -1.0, None, ALU.mult)

                @block.scalar
                def _(a):
                    for t, (c0, n) in enumerate(TILES):
                        a.wait_ge(tr, t + 1)
                        nc.scalar.activation(vt[0:n, t, :], k.bank[2 * (t % 2) + 1][0:n, :], ACT.Copy).then_inc(vc, 1)

        fox_heads(k, fT, vt, vp, kTs, ncT)


def fox_heads(k, fT, vt, vp, kTs, ncT):
    nc = k.nc
    items = [(h, t) for h in range(H) for t in range(5)]
    J = len(items)
    base = lambda h: 64 * (h % 2)

    def sizes(t):
        n = TILES[t][1]
        blocks = [(0, PAST), (PAST, NS)] if t == 0 else [(128 * b, 128) for b in range(t)]
        return n, blocks[-1][0] + blocks[-1][1], blocks

    with ExitStack() as ctx:
        ncb = k.sb("ncb", [128, 2, PAST + NS + NP], F32, ctx)
        sc = k.sb("f_scores", [128, 2, NP], F32, ctx)
        pr = k.sb("f_probs", [128, 2, NP], F32, ctx)
        pT = k.sb("f_probsT", [128, 2, NP], F32, ctx)
        st = k.sb("f_stat", [128, 4, J], F32, ctx)
        bias, biasc, score, biased, probs, scaled, turned, turnedc, out, outh, outl = (
            k.sem("f_" + n) for n in ("bias", "biasc", "score", "biased", "probs", "scaled", "turned", "turnedc",
                                      "out", "outh", "outl"))
        with nc.Block() as block:
            @block.tensor
            def _(pe):
                def scores(j):
                    h, t = items[j]
                    n, nk, blocks = sizes(t)
                    b, c0 = base(h), TILES[t][0]
                    if t == 0:
                        if h >= 1:
                            pe.wait_ge(biasc, h)
                        nc.tensor.matmul(k.bank[6][:, 0:PAST + NS], k.sel[:, h, :], ncT[:, 0:PAST + NS],
                                         start=True, stop=True)
                        nc.tensor.matmul(k.bank[7][:], k.sel[:, h, :], ncT[:, PAST + NS:], start=True, stop=True)\
                            .then_inc(bias, 1)
                    if j >= 2:
                        pe.wait_ge(biased, j - 1)
                    keys = kTs[b:b + 64, h // 2, :] if t == 0 else fT[b:b + 64, 4 + h // 2, NS:NS + nk]
                    nc.tensor.matmul(k.bank[j % 2][0:n, 0:nk], fT[b:b + 64, h // 2, c0:c0 + n], keys, start=True, stop=False)
                    m0, mn = blocks[-1]
                    nc.tensor.matmul(k.bank[j % 2][0:n, m0:m0 + mn], k.ident[0:n, 0:n], k.causal_neg[0:n, 0:mn],
                                     start=False, stop=True).then_inc(score, 1)

                def turn(j):
                    h, t = items[j]
                    n, nk, blocks = sizes(t)
                    pe.wait_ge(scaled, j + 1)
                    if j >= 2:
                        pe.wait_ge(turnedc, j - 1)
                    for i, (m0, mn) in enumerate(blocks):
                        last = nc.tensor.transpose(k.bank[2 + j % 2][0:mn, i * n:i * n + n], pr[0:n, j % 2, m0:m0 + mn],
                                                   k.ident[0:n, 0:n])
                    last.then_inc(turned, 1)

                def values(j):
                    h, t = items[j]
                    n, nk, blocks = sizes(t)
                    b = base(h)
                    pe.wait_ge(turnedc, j + 1)
                    if j >= 2:
                        pe.wait_ge(outl, j - 1)
                    for i, (m0, mn) in enumerate(blocks):
                        hv = slice(64 * h, 64 * h + 64)
                        v = (vp[:, hv] if i == 0 else vt[0:NS, 0, hv]) if t == 0 else vt[:, 1 + i, hv]
                        last = nc.tensor.matmul(k.bank[4 + j % 2][b:b + 64, 0:n], v, pT[0:mn, j % 2, i * n:i * n + n],
                                                start=(i == 0), stop=(i == len(blocks) - 1))
                    last.then_inc(out, 1)

                for j in range(J + 2):
                    if j < J:
                        scores(j)
                    if 1 <= j <= J:
                        turn(j - 1)
                    if j >= 2:
                        values(j - 2)

            @block.vector
            def _(v):
                own = k.chain(v, "vector")

                def biases(j):
                    h, t = items[j]
                    n, nk, blocks = sizes(t)
                    v.wait_ge(score, j + 1)
                    v.wait_ge(biasc, h + 1)
                    if j >= 2:
                        v.wait_ge(probs, j - 1)
                    cols = slice(0, nk) if t == 0 else slice(PAST + NS, PAST + NS + nk)
                    own(nc.vector.tensor_tensor_reduce(out=sc[0:n, j % 2, 0:nk], in0=k.bank[j % 2][0:n, 0:nk],
                                                   in1=ncb[0:n, h % 2, cols], scale=1.0, scalar=-3e38,
                                                   op0=ALU.add, op1=ALU.max, accum_out=st[0:n, 0, j:j + 1]))
                    nc.vector.tensor_scalar(st[0:n, 1, j:j + 1], st[0:n, 0, j:j + 1], -1.0, None, ALU.mult)\
                        .then_inc(biased, 1)

                def scale(j):
                    h, t = items[j]
                    n, nk, blocks = sizes(t)
                    v.wait_ge(probs, j + 1)
                    own(nc.vector.reciprocal(st[0:n, 3, j:j + 1], st[0:n, 2, j:j + 1]))
                    nc.vector.tensor_scalar(pr[0:n, j % 2, 0:nk], pr[0:n, j % 2, 0:nk], st[0:n, 3, j:j + 1], None,
                                            ALU.mult).then_inc(scaled, 1)

                def low(j):
                    h, t = items[j]
                    n, b, c0 = TILES[t][1], base(h), TILES[t][0]
                    v.wait_ge(outh, j + 1)
                    nc.vector.tensor_tensor(k.yal[b:b + 64, h // 2, c0:c0 + n], k.bank[4 + j % 2][b:b + 64, 0:n],
                                            k.yah[b:b + 64, h // 2, c0:c0 + n].bitcast(F32), ALU.subtract)\
                        .then_inc(outl, 1)

                for j in range(J + 2):
                    if j < J:
                        biases(j)
                    if 1 <= j <= J:
                        scale(j - 1)
                    if j >= 2:
                        low(j - 2)

            @block.scalar
            def _(a):
                def spread(h):
                    a.wait_ge(bias, h + 1)
                    if h >= 2:
                        a.wait_ge(biased, 5 * (h - 1))
                    nc.scalar.activation(ncb[:, h % 2, 0:PAST + NS], k.bank[6][:, 0:PAST + NS], ACT.Copy)
                    nc.scalar.activation(ncb[:, h % 2, PAST + NS:], k.bank[7][:], ACT.Copy).then_inc(biasc, 1)

                def exps(j):
                    h, t = items[j]
                    n, nk, blocks = sizes(t)
                    a.wait_ge(biased, j + 1)
                    if j >= 2:
                        a.wait_ge(turned, j - 1)
                    nc.scalar.activation(pr[0:n, j % 2, 0:nk], sc[0:n, j % 2, 0:nk], ACT.Exp, bias=st[0:n, 1, j:j + 1],
                                         accum_out=st[0:n, 2, j:j + 1]).then_inc(probs, 1)

                def copy(j):
                    h, t = items[j]
                    n, nk, blocks = sizes(t)
                    a.wait_ge(turned, j + 1)
                    if j >= 2:
                        a.wait_ge(out, j - 1)
                    if t == 0:
                        nc.scalar.activation(pT[:, j % 2, 0:n], k.bank[2 + j % 2][:, 0:n], ACT.Copy)
                        last = nc.scalar.activation(pT[0:NS, j % 2, n:2 * n], k.bank[2 + j % 2][0:NS, n:2 * n], ACT.Copy)
                    else:
                        last = nc.scalar.activation(pT[:, j % 2, 0:nk], k.bank[2 + j % 2][:, 0:nk], ACT.Copy)
                    last.then_inc(turnedc, 1)

                def high(j):
                    h, t = items[j]
                    n, b, c0 = TILES[t][1], base(h), TILES[t][0]
                    a.wait_ge(out, j + 1)
                    nc.scalar.activation(k.yah[b:b + 64, h // 2, c0:c0 + n], k.bank[4 + j % 2][b:b + 64, 0:n], ACT.Copy)\
                        .then_inc(outh, 1)

                for j in range(J + 2):
                    if j < J:
                        if items[j][1] == 0:
                            spread(items[j][0])
                        exps(j)
                    if 1 <= j <= J:
                        copy(j - 1)
                    if j >= 2:
                        high(j - 2)


def merge_branches(k):
    nc = k.nc
    with ExitStack() as ctx:
        mh = k.sb("mix_hi", [128, KD, NT], F32R, ctx)
        ml = k.sb("mix_lo", [128, KD, NT], F32R, ctx)
        gate = k.sb("m_gate", [128, 2, NT], F32, ctx)
        part = k.sb("m_part", [128, 2, NT], F32, ctx)
        cols = lambda name, c: k.i[name][0].rearrange("(k p) n -> p k n", p=128)[:, :, 128 * c:128 * c + 128]
        chunks = []
        for c in range(KD):
            chunks += [([(0, w_in_cols(k, C_GA + 128 * c))], KD, k.xhi, k.xlo), ([(0, cols("w_br_a", c))], 4, k.yah, k.yal),
                       ([(0, w_in_cols(k, C_GB + 128 * c))], KD, k.xhi, k.xlo), ([(0, cols("w_br_b", c))], KD, k.ybh, k.ybl)]
        n4 = len(chunks)
        chunks += [([(0, cols("w_out", c))], KD, mh, ml) for c in range(KD)]
        s = Stream(k, "mg", chunks, ctx, [1 if c < n4 and c % 2 == 0 else 0 for c in range(len(chunks))])
        gated, sumd, high, low = (k.sem("m_" + n) for n in ("gated", "sum", "high", "low"))
        with nc.Block() as block:
            @block.sync
            def _(sp):
                for c in range(len(chunks)):
                    s.load(sp, c)

            @block.gpsimd
            def _(g):
                for c in range(len(chunks)):
                    s.split_lo(g, c)

            @block.tensor
            def _(pe):
                for c in range(n4):
                    s.product(pe, c)
                pe.wait_ge(low, KD)
                for c in range(n4, len(chunks)):
                    pe.wait_ge(s.lo, c + 1)
                    for h, tiles in enumerate(((0, 1, 2), (3, 4))):
                        s.wait_emptied(pe, c - 1, h)
                        for i, t in enumerate(tiles):
                            c0 = TILES[t][0]
                            for d in range(KD):
                                for n, (x, w) in enumerate(((mh, k.whi), (ml, k.whi), (mh, k.wlo))):
                                    last = nc.tensor.matmul(k.bank[h][:, 128 * i:128 * i + 128], x[:, d, c0:c0 + 128],
                                                            w[:, c % 2, d, :], start=(d == 0 and n == 0),
                                                            stop=(d == KD - 1 and n == 2))
                        last.then_inc(s.half, 1)

            @block.scalar
            def _(a):
                s.split_hi(a, 0)
                for c in range(n4 + 1):
                    if c + 1 < len(chunks) and c < n4:
                        s.split_hi(a, c + 1)
                    if c < n4 and c % 2 == 0:
                        if c >= 4:
                            s.wait_emptied(a, c - 3, 1)
                        for h in range(2):
                            a.wait_ge(s.half, 2 * c + h + 1)
                            nc.scalar.activation(gate[:, c // 2 % 2, h * HALF:(h + 1) * HALF], k.bank[h][:, 0:HALF],
                                                 ACT.Sigmoid, bias=k.bgate[:, (c // 4) + 8 * (c // 2 % 2):][:, 0:1])\
                                .then_inc(s.emptied_of(c), 1)
                    if c >= 4 and c % 4 == 0:
                        a.wait_ge(sumd, c // 4)
                        nc.scalar.activation(mh[:, c // 4 - 1, :], part[:, 0, :], ACT.Copy).then_inc(high, 1)
                for c in range(n4 + 1, len(chunks)):
                    s.split_hi(a, c)

            @block.vector
            def _(v):
                ch = k.chain(v, "vector")
                for c in range(1, n4, 2):
                    if c % 4 == 1 and c > 1:
                        v.wait_ge(low, c // 4)
                    s.wait_emptied(v, c - 1, 1)
                    for h in range(2):
                        f = slice(h * HALF, (h + 1) * HALF)
                        v.wait_ge(s.half, 2 * c + h + 1)
                        nc.vector.tensor_tensor(part[:, c // 2 % 2, f], k.bank[h][:, 0:HALF], gate[:, c // 2 % 2, f],
                                                ALU.mult).then_inc(s.emptied_of(c), 1)
                    if c % 4 == 3:
                        s.wait_emptied(v, c, 1)
                        nc.vector.tensor_tensor(part[:, 0, :], part[:, 0, :], part[:, 1, :], ALU.add).then_inc(sumd, 1)
                        v.wait_ge(high, c // 4 + 1)
                        nc.vector.tensor_tensor(ml[:, c // 4, :], part[:, 0, :], mh[:, c // 4, :].bitcast(F32),
                                                ALU.subtract).then_inc(low, 1)
                for c in range(n4, len(chunks)):
                    f = slice(128 * (c - n4), 128 * (c - n4) + 128)
                    v.wait_ge(s.half, 2 * c + 1)
                    nc.vector.tensor_tensor(k.x[0:NS, 0, f], k.x[0:NS, 0, f], k.bank[0][0:NS, 0:128], ALU.add)
                    nc.vector.tensor_tensor(k.x[:, 1:3, f], k.x[:, 1:3, f],
                                            k.bank[0][:, 128:384].rearrange("p (t n) -> p t n", t=2), ALU.add)\
                        .then_inc(s.emptied_of(c), 1)
                    v.wait_ge(s.half, 2 * c + 2)
                    nc.vector.tensor_tensor(k.x[:, 3:5, f], k.x[:, 3:5, f],
                                            k.bank[1][:, 0:256].rearrange("p (t n) -> p t n", t=2), ALU.add)\
                        .then_inc(s.emptied_of(c), 1)


def route_and_experts(k):
    nc = k.nc
    with ExitStack() as ctx:
        k.moe = ctx
        k.table = nc.dram_tensor("token_rows", [NT + 1, D], F32).ap()
        k.yblk = nc.dram_tensor("expert_rows", [NB * SLOTS, D], F32).ap()
        k.w1 = k.sb("e_w1", [128, 2, KD, FE], F32, ctx)
        k.w3 = k.sb("e_w3", [128, 2, KD, FE], F32, ctx)
        k.w2 = k.sb("e_w2", [128, 2, FE // 128, D], F32, ctx)
        k.up_loaded = [k.sem(f"up_loaded{s}") for s in range(2)]
        k.down_loaded = [k.sem(f"down_loaded{s}") for s in range(2)]
        k.idx = k.sb("slot_token", [SLOTS, NB], I32, ctx)
        k.eid = k.sb("more_expert", [1, MORE], I32, ctx)
        k.nmore = k.sb("more_blocks", [1, 1], I32, ctx)
        k.row = k.sb("token_slot", [128, 5, 2], I32, ctx)
        k.wt = k.sb("token_weight", [128, 5, 2], F32, ctx)
        with ExitStack() as k.routing:
            k.lg = k.sb("logits", [128, 5, GROUPS + NE], F32, k.routing)
            normalise_rows(k)
            choose_experts(k)
        expert_blocks(k)
        combine(k)


def load_up(k, sp, e, slot):
    for w, src in ((k.w1, k.i["w_e1"]), (k.w3, k.i["w_e3"])):
        src = src[0, e] if isinstance(e, int) else src[0, bass.ds(e, 1)].rearrange("o r n -> (o r) n")
        sp.dma_start(w[:, slot], src.rearrange("(k p) n -> p k n", p=128)).then_inc(k.up_loaded[slot], 16)


def load_down(k, sp, e, slot):
    src = k.i["w_e2"]
    src = src[0, e] if isinstance(e, int) else src[0, bass.ds(e, 1)].rearrange("o r n -> (o r) n")
    sp.dma_start(k.w2[:, slot], src.rearrange("(k p) n -> p k n", p=128)).then_inc(k.down_loaded[slot], 16)


def normalise_rows(k):
    nc = k.nc
    ctx = k.routing
    NL = GROUPS + NE
    junk = k.sb("r_sq", [128, D], F32, ctx)
    stat = k.sb("r_stat", [128, 3, 5], F32, ctx)
    xn = k.sb("r_xn", [128, 2, D], F32, ctx)
    xT = k.sb("r_xT", [128, 2, KD, 128], F32, ctx)
    gain = k.sb("g_ffn_rows", [128, D], F32, ctx)
    zero = k.sb("r_zero", [128, D], F32, ctx)
    wr = k.sb("w_router", [128, KD, NL], F32, ctx)
    br = k.sb("b_router", [128, NL], F32, ctx)
    params, zeroed, filled, rms, normed, moved, turned, scored, biased = (
        k.sem("r_" + n) for n in ("params", "zeroed", "filled", "rms", "normed", "moved", "turned", "scored", "biased"))
    stored = [k.sem(f"r_stored{s}") for s in range(2)]
    with nc.Block() as block:
        @block.sync
        def _(sp):
            with nc.allow_non_contiguous_dma(reason="router columns"):
                for dst, src in ((gain[:], k.i["g_ffn"].broadcast_to([128, D])),
                                 (wr[:, :, 0:GROUPS], k.i["w_grp"][0].rearrange("(k p) n -> p k n", p=128)),
                                 (wr[:, :, GROUPS:], k.i["w_exp"][0].rearrange("(k p) n -> p k n", p=128)),
                                 (br[:, 0:GROUPS], k.i["b_grp"].broadcast_to([128, GROUPS])),
                                 (br[:, GROUPS:], k.i["b_exp"].broadcast_to([128, NE]))):
                    sp.dma_start(dst, src).then_inc(params, 16)
            for e in range(2):
                load_up(k, sp, e, e)
                load_down(k, sp, e, e)
            for t, (c0, n) in enumerate(TILES):
                sp.wait_ge(normed, t + 1)
                sp.dma_start(k.table[c0:c0 + n, :], xn[0:n, t % 2, :]).then_inc(stored[t % 2], 16)
            sp.wait_ge(stored[0], 48)
            sp.wait_ge(stored[1], 32)

        @block.gpsimd
        def _(g):
            g.memset(zero[:], 0.0).then_inc(zeroed, 1)

        @block.scalar
        def _(a):
            c = k.chain(a, "scalar")
            for t, (c0, n) in enumerate(TILES):
                c(nc.scalar.activation(junk[0:n, :], k.x[0:n, t, :], ACT.Square, accum_out=stat[0:n, 0, t:t + 1]))
            for t, (c0, n) in enumerate(TILES):
                nc.scalar.activation(stat[0:n, 1, t:t + 1], stat[0:n, 0, t:t + 1], ACT.Sqrt, bias=k.eps[0:n, :],
                                     scale=1.0 / D).then_inc(rms, 1)
            a.wait_ge(zeroed, 1)
            a.dma_start(k.table[NT:NT + 1, :], zero[0:1, :]).then_inc(filled, 16)
            for m in range(NE * SLOTS, NB * SLOTS, 128):
                a.dma_start(k.yblk[m:m + 128, :], zero[:]).then_inc(filled, 16)
            for t, (c0, n) in enumerate(TILES):
                a.wait_ge(moved, t + 1)
                if t >= 2:
                    a.wait_ge(scored, t - 1)
                for b in range(2):
                    nc.scalar.activation(xT[:, t % 2, 4 * b:4 * b + 4, 0:n],
                                         k.bank[2 * (t % 2) + b][:, 0:4 * n].rearrange("p (k n) -> p k n", k=4),
                                         ACT.Copy).then_inc(turned, 1)
            a.wait_ge(filled, 16 * (1 + MORE * SLOTS // 128))

        @block.vector
        def _(v):
            c = k.chain(v, "vector")
            c(nc.vector.memset(k.lg[:], 0.0))
            v.wait_ge(params, 80)
            for t, (c0, n) in enumerate(TILES):
                v.wait_ge(rms, t + 1)
                c(nc.vector.reciprocal(stat[0:n, 2, t:t + 1], stat[0:n, 1, t:t + 1]))
                if t >= 2:
                    v.wait_ge(moved, t - 1)
                    v.wait_ge(stored[t % 2], 16 * (t // 2))
                nc.vector.scalar_tensor_tensor(out=xn[0:n, t % 2, :], in0=k.x[0:n, t, :], scalar=stat[0:n, 2, t:t + 1],
                                               in1=gain[0:n, :], op0=ALU.mult, op1=ALU.mult).then_inc(normed, 1)
            for t, (c0, n) in enumerate(TILES):
                v.wait_ge(scored, t + 1)
                nc.vector.tensor_tensor(k.lg[0:n, t, :], k.bank[4 + t % 2][0:n, 0:NL], br[0:n, :], ALU.add)\
                    .then_inc(biased, 1)

        @block.tensor
        def _(pe):
            pe.wait_ge(params, 80)
            for t, (c0, n) in enumerate(TILES):
                pe.wait_ge(normed, t + 1)
                if t >= 2:
                    pe.wait_ge(turned, 2 * (t - 1))
                for d in range(KD):
                    last = nc.tensor.transpose(k.bank[2 * (t % 2) + d // 4][:, (d % 4) * n:(d % 4) * n + n],
                                               xn[0:n, t % 2, 128 * d:128 * d + 128], k.ident[0:n, 0:n])
                last.then_inc(moved, 1)
                pe.wait_ge(turned, 2 * (t + 1))
                if t >= 2:
                    pe.wait_ge(biased, t - 1)
                for d in range(KD):
                    last = nc.tensor.matmul(k.bank[4 + t % 2][0:n, 0:NL], xT[:, t % 2, d, 0:n], wr[:, d, :],
                                            start=(d == 0), stop=(d == KD - 1))
                last.then_inc(scored, 1)


def choose_experts(k):
    nc = k.nc
    ctx = k.routing
    V = nc.vector
    T = lambda name, *dims, dt=F32, p=128: k.sb("c_" + name, [p] + list(dims), dt, ctx)
    iN = T("iota_i", max(NB, SLOTS), dt=I32)
    iota = T("iota", max(NB, SLOTS))
    token_i, token, valid = T("token_i", 5, dt=I32), T("token", 5), T("valid", 5)
    g8, gm, gi, gf = T("g8", 5, 8), T("gmax", 5, 8), T("gidx", 5, 8, dt=U32), T("gsel", 5)
    goh, gd, ge, gs = T("goh", 5, GROUPS), T("gdiff", 5, GROUPS), T("gexp", 5, GROUPS), T("gsum", 5)
    em, em8, ei, ef = T("em", 5, NE), T("emax", 5, 8), T("eidx", 5, 8, dt=U32), T("esel", 5, 2)
    e2, wa = T("e2", 5), T("wa", 5)
    oh, both, pre, tmp = T("oh", 2, 5, NE), T("both", 5, NE), T("pre", 5, NE), T("tmp", 2, 5, NE)
    tot, ov, oi, ob = T("tot", NE), T("over", NE), T("cum", 2, NE), T("before", NE)
    rank, obr, q, s, blk, pos = T("rank", 2, 5), T("obr", 2, 5), T("q", 2, 5), T("s", 2, 5), T("blk", 2, 5), T("pos", 2, 5)
    more = T("more", 2, 5)
    cmpj, ejf = T("cmpj", MORE, NE), T("ejf", MORE)
    r1, b1 = T("rank_oh", 10, SLOTS), T("blk_oh", 10, NB)
    made, diffs, exps, chosen, counted, coded, listed = (k.sem("c_" + n) for n in
                                                        ("made", "diffs", "exps", "chosen", "counted", "coded", "listed"))
    further = -(-NT // SLOTS)
    with nc.Block() as block:
        @block.gpsimd
        def _(g):
            g.iota(iN[:], pattern=[[1, max(NB, SLOTS)]], base=0, channel_multiplier=0).then_inc(made, 1)
            g.iota(token_i[:], pattern=[[128, 5]], base=NS - 128, channel_multiplier=1).then_inc(made, 1)
            g.wait_ge(made, 2)
            g.iota(token_i[:, 0:1], pattern=[[0, 1]], base=0, channel_multiplier=1).then_inc(made, 1)

        @block.scalar
        def _(a):
            a.wait_ge(diffs, 2)
            nc.scalar.activation(ge[:], gd[:], ACT.Exp).then_inc(exps, 1)
            nc.scalar.activation(e2[:], e2[:], ACT.Exp).then_inc(exps, 1)

        @block.tensor
        def _(pe):
            pe.wait_ge(chosen, 1)
            for t in range(5):
                nc.tensor.matmul(k.bank[0][:, NE * t:NE * t + NE], k.striu[:], both[:, t, :], start=True, stop=(t == 0))
                for u in range(t):
                    nc.tensor.matmul(k.bank[0][:, NE * t:NE * t + NE], k.ones[:], both[:, u, :], start=False,
                                     stop=(u == t - 1))
            for t in range(5):
                last = nc.tensor.matmul(k.bank[1][:, 0:NE], k.ones[:], both[:, t, :], start=(t == 0), stop=(t == 4))
            last.then_inc(counted, 1)
            pe.wait_ge(coded, 1)
            for j in range(10):
                last = nc.tensor.matmul(k.bank[2][0:SLOTS, 0:NB], r1[:, j, :], b1[:, j, :], start=(j == 0), stop=(j == 9))
            last.then_inc(listed, 1)

        @block.vector
        def _(v):
            c = k.chain(v, "vector")
            bc = lambda ap, n: ap.unsqueeze(2).broadcast_to([128, 5, n])
            c(V.memset(valid[:], 1.0))
            c(V.memset(valid[:, 0:1], 0.0))
            c(V.memset(valid[0:NS, 0:1], 1.0))
            c(V.memset(g8[:], NEG))
            v.wait_ge(made, 3)
            c(V.tensor_copy(iota[:], iN[:]))
            c(V.tensor_copy(token[:], token_i[:]))
            c(V.tensor_copy(g8[:, :, 0:GROUPS], k.lg[:, :, 0:GROUPS]))
            for t in range(5):
                c(V.max(out=gm[:, t, :], in_=g8[:, t, :]))
                c(V.max_index(out=gi[:, t, :], in_max=gm[:, t, :], in_values=g8[:, t, :]))
            c(V.tensor_copy(gf[:], gi[:, :, 0]))
            V.tensor_tensor(gd[:], k.lg[:, :, 0:GROUPS], bc(gm[:, :, 0], GROUPS), ALU.subtract).then_inc(diffs, 1)
            c(V.tensor_tensor(goh[:], iota[:, 0:GROUPS].unsqueeze(1).broadcast_to([128, 5, GROUPS]), bc(gf[:], GROUPS),
                              ALU.is_equal))
            c(V.tensor_scalar(goh[:], goh[:], -NEG, NEG, ALU.mult, ALU.add))
            c(V.tensor_tensor(em[:].rearrange("p t (g e) -> p t g e", g=GROUPS),
                              k.lg[:, :, GROUPS:].rearrange("p t (g e) -> p t g e", g=GROUPS),
                              goh[:].unsqueeze(3).broadcast_to([128, 5, GROUPS, PER_GROUP]), ALU.add))
            for t in range(5):
                c(V.max(out=em8[:, t, :], in_=em[:, t, :]))
                c(V.max_index(out=ei[:, t, :], in_max=em8[:, t, :], in_values=em[:, t, :]))
            V.tensor_tensor(e2[:], em8[:, :, 1], em8[:, :, 0], ALU.subtract).then_inc(diffs, 1)
            c(V.tensor_copy(ef[:], ei[:, :, 0:2]))
            for j in range(2):
                c(V.tensor_tensor(oh[:, j], iota[:, 0:NE].unsqueeze(1).broadcast_to([128, 5, NE]), bc(ef[:, :, j], NE),
                                  ALU.is_equal))
                c(V.tensor_tensor(oh[:, j], oh[:, j], bc(valid[:], NE), ALU.mult))
            V.tensor_tensor(both[:], oh[:, 0], oh[:, 1], ALU.add).then_inc(chosen, 1)
            v.wait_ge(exps, 2)
            c(V.tensor_reduce(gs[:], ge[:], AX.X, ALU.add))
            c(V.tensor_scalar(wa[:], e2[:], 1.0, None, ALU.add))
            c(V.tensor_tensor(gs[:], gs[:], wa[:], ALU.mult))
            c(V.reciprocal(k.wt[:, :, 0], gs[:]))
            c(V.tensor_tensor(k.wt[:, :, 1], k.wt[:, :, 0], e2[:], ALU.mult))
            v.wait_ge(counted, 1)
            c(V.tensor_copy(pre[:].rearrange("p t e -> p (t e)"), k.bank[0][:, 0:5 * NE]))
            c(V.tensor_copy(tot[:], k.bank[1][:, 0:NE]))
            c(V.memset(ov[:], 0.0))
            for m in range(1, further):
                c(V.scalar_tensor_tensor(out=ov[:], in0=tot[:], scalar=SLOTS * m + 0.5, in1=ov[:], op0=ALU.is_gt,
                                         op1=ALU.add))
            c(V.tensor_copy(oi[:, 0], ov[:]))
            cur, step = 0, 1
            while step < NE:
                c(V.tensor_copy(oi[:, 1 - cur, 0:step], oi[:, cur, 0:step]))
                c(V.tensor_tensor(oi[:, 1 - cur, step:], oi[:, cur, step:], oi[:, cur, 0:NE - step], ALU.add))
                cur, step = 1 - cur, 2 * step
            c(V.tensor_tensor(ob[:], oi[:, cur], ov[:], ALU.subtract))
            c(V.tensor_tensor(tmp[:], oh[:], pre[:].unsqueeze(1).broadcast_to([128, 2, 5, NE]), ALU.mult))
            c(V.tensor_reduce(rank[:], tmp[:], AX.X, ALU.add))
            c(V.tensor_tensor(tmp[:].rearrange("p j t e -> p (j t) e"), oh[:].rearrange("p j t e -> p (j t) e"),
                              ob[:].unsqueeze(1).broadcast_to([128, 10, NE]), ALU.mult))
            c(V.tensor_reduce(obr[:], tmp[:], AX.X, ALU.add))
            c(V.memset(q[:], 0.0))
            for m in range(1, further):
                c(V.scalar_tensor_tensor(out=q[:], in0=rank[:], scalar=SLOTS * m - 0.5, in1=q[:], op0=ALU.is_gt,
                                         op1=ALU.add))
            c(V.scalar_tensor_tensor(out=s[:], in0=q[:], scalar=-float(SLOTS), in1=rank[:], op0=ALU.mult, op1=ALU.add))
            c(V.scalar_tensor_tensor(out=blk[:], in0=q[:], scalar=NE - 1.0, in1=obr[:], op0=ALU.add, op1=ALU.add))
            c(V.tensor_scalar(more[:], q[:], 0.5, None, ALU.is_gt))
            est = ef[:].rearrange("p t j -> p j t")
            c(V.tensor_tensor(blk[:], blk[:], est, ALU.subtract))
            c(V.tensor_tensor(blk[:], blk[:], more[:], ALU.mult))
            c(V.tensor_tensor(blk[:], blk[:], est, ALU.add))
            c(V.scalar_tensor_tensor(out=pos[:], in0=blk[:], scalar=float(SLOTS), in1=s[:], op0=ALU.mult, op1=ALU.add))
            c(V.tensor_copy(k.row[:].rearrange("p t j -> p j t"), pos[:]))
            c(V.tensor_scalar(token[:], token[:], float(NT), None, ALU.subtract))
            c(V.tensor_tensor(token[:], token[:], valid[:], ALU.mult))
            for j in range(2):
                for t in range(5):
                    V.tensor_scalar(r1[:, 5 * j + t, :], iota[:, 0:SLOTS], s[:, j, t:t + 1], None, ALU.is_equal)
                    last = V.tensor_scalar(b1[:, 5 * j + t, :], iota[:, 0:NB], blk[:, j, t:t + 1], token[:, t:t + 1],
                                           ALU.is_equal, ALU.mult)
            last.then_inc(coded, 1)
            c(V.tensor_tensor(cmpj[:], oi[:, cur].unsqueeze(1).broadcast_to([128, MORE, NE]),
                              iota[:, 0:MORE].unsqueeze(2).broadcast_to([128, MORE, NE]), ALU.is_le))
            c(V.tensor_reduce(ejf[:], cmpj[:], AX.X, ALU.add))
            c(V.tensor_copy(k.eid[:], ejf[0:1, :]))
            c(V.tensor_copy(k.nmore[:], oi[0:1, cur, NE - 1:NE]))
            v.wait_ge(listed, 1)
            c(V.tensor_scalar(k.idx[:], k.bank[2][0:SLOTS, 0:NB], float(NT), None, ALU.add))


def expert_blocks(k):
    nc = k.nc
    FH, NF = FE // 2, FE // 128
    with ExitStack() as ctx:
        at = k.sb("b_index", [SLOTS, 2], I32, ctx)
        spare = k.sb("b_spare", [SLOTS, 2], F32, ctx)
        xg = k.sb("b_rows", [SLOTS, 2, D], F32, ctx)
        xT = k.sb("b_xT", [128, KD, SLOTS], F32, ctx)
        act = k.sb("b_silu", [128, FH], F32, ctx)
        hm = k.sb("b_hidden", [128, FH], F32, ctx)
        hT = k.sb("b_hiddenT", [128, 2, 128], F32, ctx)
        y = k.sb("b_y", [128, 2, D // 2], F32, ctx)
        names = ("index", "turned", "copied", "up", "silu", "hidden", "hturned", "hcopied", "down", "out")
        index, turned, copied, up, silu, hidden, hturned, hcopied, down, out = (k.sem("b_" + n) for n in names)
        gathered = [k.sem(f"b_gathered{s}") for s in range(2)]
        stored = [k.sem(f"b_stored{s}") for s in range(2)]
        lo, hi = slice(0, 64), slice(64, 128)
        sl = (lo, hi)

        def wait(eng, sem, value):
            if not isinstance(value, int) or value > 0:
                eng.wait_ge(sem, value)

        def fetch(g, b, slot, n, prev):
            wait(g, turned, prev + 1)
            nc.gpsimd.tensor_copy(at[:, slot:slot + 1], k.idx[:, bass.ds(b, 1)]).then_inc(index, 1)
            g.wait_ge(index, b + 1)
            nc.gpsimd.tensor_tensor(spare[:, 0:1], k.one[0:SLOTS, :], k.one[0:SLOTS, :], ALU.add)
            g.indirect_dma_start(out=xg[:, slot, :], out_offset=None, in_=k.table,
                                 in_offset=bass.IndirectOffsetOnAxis(ap=at[:, slot:slot + 1], axis=0))\
                .then_inc(gathered[slot], 16)
            g.wait_ge(gathered[slot], 16 * n + 16)

        def products(pe, b, slot, n, prev):
            pe.wait_ge(gathered[slot], 16 * n + 16)
            wait(pe, copied, b)
            nc.tensor.matmul(k.bank[0][:, 0:64], xg[:, slot, 0:128], k.ident[0:64, 0:64], start=True, stop=True)
            for d in range(1, KD):
                last = nc.tensor.transpose(k.bank[0][:, 64 * d:64 * d + 64], xg[:, slot, 128 * d:128 * d + 128],
                                           k.ident[0:64, 0:64])
            last.then_inc(turned, 1)
            pe.wait_ge(copied, b + 1)
            pe.wait_ge(k.up_loaded[slot], 32 * n + 32)
            wait(pe, hidden, b)
            for d in range(KD):
                for bank, w in ((1, k.w1), (2, k.w3)):
                    for a in range(2):
                        last = nc.tensor.matmul(k.bank[bank][sl[a], 0:FH], xT[:, d, :], w[:, slot, d, FH * a:FH * a + FH],
                                                start=(d == 0), stop=(d == KD - 1))
            last.then_inc(up, 1)
            pe.wait_ge(hidden, b + 1)
            for c in range(2):
                last = nc.tensor.transpose(k.bank[3][:, 128 * c:128 * c + 128], hm[:, 128 * c:128 * c + 128], k.ident[:])
            last.then_inc(hturned, 1)
            pe.wait_ge(hcopied, b + 1)
            pe.wait_ge(k.down_loaded[slot], 16 * n + 16)
            wait(pe, out, b)
            for f in range(NF):
                for a in range(2):
                    last = nc.tensor.matmul(k.bank[4][sl[a], :], hT[:, f % 2, sl[f // 2]],
                                            k.w2[:, slot, f, 512 * a:512 * a + 512], start=(f == 0), stop=(f == NF - 1))
            last.then_inc(down, 1)

        def scalar_part(a, b, slot, n, prev):
            a.wait_ge(up, b + 1)
            wait(a, hidden, b)
            nc.scalar.activation(act[:], k.bank[1][:, 0:FH], ACT.Silu).then_inc(silu, 1)
            a.wait_ge(down, b + 1)
            wait(a, stored[slot], 32 * n)
            nc.scalar.activation(y[:, slot, :], k.bank[4][:], ACT.Copy).then_inc(out, 1)
            a.wait_ge(out, b + 1)
            for h in range(2):
                a.dma_start(k.yblk[bass.ds(b * SLOTS, SLOTS), 512 * h:512 * h + 512], y[sl[h], slot, :])\
                    .then_inc(stored[slot], 16)

        def vector_part(v, b, slot, n, prev):
            v.wait_ge(turned, b + 1)
            wait(v, up, b)
            nc.vector.tensor_copy(xT[:].rearrange("p k s -> p (k s)"), k.bank[0][:]).then_inc(copied, 1)
            v.wait_ge(silu, b + 1)
            wait(v, hturned, b)
            nc.vector.tensor_tensor(hm[:], act[:], k.bank[2][:, 0:FH], ALU.mult).then_inc(hidden, 1)
            v.wait_ge(hturned, b + 1)
            wait(v, down, b)
            nc.vector.tensor_copy(hT[:].rearrange("p c s -> p (c s)"), k.bank[3][:, 0:256]).then_inc(hcopied, 1)

        def loads(sp, e, b, slot, prev):
            sp.wait_ge(up, prev + 1)
            load_up(k, sp, e, slot)
            sp.wait_ge(down, prev + 1)
            load_down(k, sp, e, slot)

        def run_blocks(eng, part):
            for s in range(2):
                part(eng, s, s, 0, s - 2)
            with eng.Fori(1, NE // 2) as i:
                for s in range(2):
                    part(eng, 2 * i + s, s, i, 2 * i + s - 2)
            n = eng.value_load(k.nmore[0:1, 0:1], min_val=0, max_val=MORE)
            with eng.If(n > 0):
                with eng.Fori(0, n) as j:
                    part(eng, j + NE, 0, j + NE // 2, j + NE - 1)
            return n

        with nc.Block() as block:
            @block.sync
            def _(sp):
                with sp.Fori(1, NE // 2) as i:
                    for s in range(2):
                        b = 2 * i + s
                        loads(sp, b, b, s, b - 2)
                n = sp.value_load(k.nmore[0:1, 0:1], min_val=0, max_val=MORE)
                with sp.If(n > 0):
                    with sp.Fori(0, n) as j:
                        e = sp.value_load(k.eid[0:1, bass.ds(j, 1)], min_val=0, max_val=NE - 1)
                        loads(sp, e, j + NE, 0, j + NE - 1)

            @block.gpsimd
            def _(g):
                run_blocks(g, fetch)

            @block.tensor
            def _(pe):
                run_blocks(pe, products)

            @block.scalar
            def _(a):
                n = run_blocks(a, scalar_part)
                a.wait_ge(stored[1], 32 * (NE // 2))
                a.wait_ge(stored[0], n * 32 + 32 * (NE // 2))
                nc.scalar.activation(spare[:, 1:2], k.one[0:SLOTS, :], ACT.Copy)

            @block.vector
            def _(v):
                run_blocks(v, vector_part)


def combine(k):
    nc = k.nc
    with ExitStack() as ctx:
        rows = k.sb("y_rows", [128, 4, D], F32, ctx)
        idx = k.sb("y_index", [128, 10], I32, ctx)
        ready = k.sem("y_ready")
        got = [k.sem(f"y_got{s}") for s in range(4)]
        added, stored = k.sem("y_added"), k.sem("y_stored")
        with nc.Block() as block:
            @block.gpsimd
            def _(g):
                nc.gpsimd.tensor_copy(idx[:], k.row[:].rearrange("p t j -> p (t j)")).then_inc(ready, 1)
                g.wait_ge(ready, 1)
                for m in range(10):
                    n = TILES[m // 2][1]
                    if m >= 4:
                        g.wait_ge(added, m - 3)
                    g.indirect_dma_start(out=rows[0:n, m % 4, :], out_offset=None, in_=k.yblk,
                                         in_offset=bass.IndirectOffsetOnAxis(ap=idx[0:n, m:m + 1], axis=0))\
                        .then_inc(got[m % 4], 16)
                for s in range(4):
                    g.wait_ge(got[s], 16 * (3 if s < 2 else 2))

            @block.vector
            def _(v):
                for m in range(10):
                    t, j = m // 2, m % 2
                    n = TILES[t][1]
                    v.wait_ge(got[m % 4], 16 * (m // 4 + 1))
                    if j:
                        v.wait_ge(added, m)
                    nc.vector.scalar_tensor_tensor(out=k.x[0:n, t, :], in0=rows[0:n, m % 4, :],
                                                   scalar=k.wt[0:n, t, j:j + 1], in1=k.x[0:n, t, :],
                                                   op0=ALU.mult, op1=ALU.add).then_inc(added, 1)

            @block.sync
            def _(sp):
                for t, (c0, n) in enumerate(TILES):
                    sp.wait_ge(added, 2 * t + 2)
                    dst = k.o["y_s"][0] if t == 0 else k.o["y_p"][0, 128 * (t - 1):128 * t, :]
                    sp.dma_start(dst, k.x[0:n, t, :]).then_inc(stored, 16)
                sp.wait_ge(stored, 80)


_INS = ["x_prompt", "x_sample", "cache_fox_k", "cache_fox_v", "cache_fox_logf", "state_gdn", "state_gdn_conv", "g_mix",
        "w_in", "b_f", "g_qnorm", "g_knorm", "w_conv", "a_log", "dt_bias", "g_onorm", "b_gate", "w_br_a", "w_br_b",
        "w_out", "g_ffn", "w_grp", "b_grp", "w_exp", "b_exp", "w_e1", "w_e3", "w_e2"]
_OUTS = {"y_p": (1, NP, D), "y_s": (1, NS, D)}
for _s, _n in (("p", NP), ("s", NS)):
    _OUTS.update({"k_" + _s: (1, 1, _n, H, DH), "v_" + _s: (1, 1, _n, H, DH), "logf_" + _s: (1, 1, _n, H),
                  "state_" + _s: (1, 1, H, DH, DV), "conv_" + _s: (1, 1, CONV_W - 1, CONV_CH)})


def kernel(**inputs):
    import numpy as _np
    import concourse.bacc as _bacc
    from concourse.bass_utils import run_bass_kernel_spmd as _run

    nc = _bacc.Bacc("TRN2", target_bir_lowering=False, num_devices=1)
    arrays, ins, outs = {}, {}, {}
    for name in _INS:
        a = _np.ascontiguousarray(inputs[name])
        arrays["in_" + name] = a
        ins[name] = nc.dram_tensor("in_" + name, a.shape, F32, kind="ExternalInput").ap()
    for name, shape in _OUTS.items():
        outs[name] = nc.dram_tensor("out_" + name, shape, F32, kind="ExternalOutput").ap()
    build(nc, ins, outs)
    r = _run(nc, [arrays], core_ids=[0])
    return tuple(r.results[0]["out_" + name] for name in _OUTS)
```

```python
from contextlib import ExitStack

import concourse.bass as bass
from concourse import mybir

DT = mybir.dt
F32, F32R, I32, U32 = DT.float32, DT.float32r, DT.int32, DT.uint32
ALU = mybir.AluOpType
ACT = mybir.ActivationFunctionType
AX = mybir.AxisListType

D = 1024
KD = D // 128
NS, NP = 32, 512
NT = NS + NP
HALF = NT // 2
TILES = [(0, NS)] + [(NS + 128 * i, 128) for i in range(NP // 128)]
H, DH = 8, 64
DV = 128
PAST = 128
WA = H * DH
CONV_CH = 2 * H * DH + H * DV
CONV_W = 4
NCC = CONV_CH // 128
NE, GROUPS, PER_GROUP, FE = 32, 4, 8, 512
SLOTS = 64
MORE = (2 * NT - 1) // SLOTS
NB = NE + MORE
EPS = 1e-6
RAWS, OPS = 4, 3
LEAD = OPS - 1
NEG = -1e30
C_FQ, C_FK, C_FV = 0, WA, 2 * WA
C_LOGF = 3 * WA
C_CONV = C_LOGF + H
C_BETA = C_CONV + CONV_CH
C_DECAY = C_BETA + H
C_Z = C_DECAY + H
C_GA = C_Z + H * DV
C_GB = C_GA + D


class Marks:

    def __init__(self, sem, names):
        self.sem, self.at, self.made = sem, {n: i + 1 for i, n in enumerate(names)}, 0

    def mark(self, ins, name):
        self.made += 1
        assert self.at[name] == self.made, (name, self.at[name], self.made)
        return ins.then_inc(self.sem, 1)

    def wait(self, eng, name):
        eng.wait_ge(self.sem, self.at[name])


class Chain:

    def __init__(self, eng, sem, start=0):
        self.eng, self.sem, self.n = eng, sem, start

    def __call__(self, ins):
        self.n += 1
        ins.then_inc(self.sem, 1)
        self.eng.wait_ge(self.sem, self.n)


class Kernel:
    def __init__(self, nc, ins, outs):
        self.nc, self.i, self.o = nc, ins, outs
        self.top = ExitStack()
        self.live = []

    def sb(self, name, shape, dt=F32, ctx=None):
        size = 4
        for n in shape[1:]:
            size *= n
        size = -(-size // 32) * 32
        at = -(-self.nc.sbuf_base // 32) * 32
        for a, b in sorted(self.live):
            if at + size <= a:
                break
            at = max(at, b)
        assert at + size <= self.nc.sbuf_top, (name, size, sorted(self.live))
        span = (at, at + size)
        self.live.append(span)
        (ctx or self.top).callback(self.live.remove, span)
        return self.nc.alloc_sbuf_tensor_at(name, shape, dt, offset=at)

    def sem(self, name, ctx=None):
        s = self.nc.alloc_semaphore(name=name)
        if ctx is None:
            self.stage_sems.append(s)
        return s

    def run(self, part):
        self.stage_sems = []
        with ExitStack() as self.stage:
            part(self)
        self.nc.clear_and_free_semaphores(self.stage_sems)
        self.nc.all_engine_barrier()

    def marks(self, name, names):
        return Marks(self.sem(name), list(names))

    def chain(self, eng, which):
        c = self.chains.get(which)
        if c is None:
            c = self.chains[which] = Chain(eng, self.sem("own_" + which, self.top))
        c.eng = eng
        return c


def build(nc, ins, outs):
    k = Kernel(nc, ins, outs)
    k.chains = {}
    with k.top:
        for which in ("vector", "scalar"):
            k.chain(None, which)
        k.gathered = [k.sem(f"b_gathered{s}", k.top) for s in range(2)]
        k.got = [k.sem(f"y_got{m}", k.top) for m in range(10)]
        k.bank = [k.top.enter_context(nc.psum_tensor(f"bank{b}", [128, 512], F32)) for b in range(8)]
        k.table = nc.dram_tensor("token_rows", [NT + 1, D], F32).ap()
        k.yblk = nc.dram_tensor("expert_rows", [NB * SLOTS, D], F32).ap()
        k.x = k.sb("x_rows", [128, 5, D])
        mix = k.top.enter_context(ExitStack())
        with ExitStack() as mixer:
            k.mixer = mixer
            mixer_tensors(k)
            conv_ctx = mixer.enter_context(ExitStack())
            k.conv_ctx = conv_ctx
            k.run(start)
            k.run(convolved_projections)
            k.run(delta_net)
            conv_ctx.close()
            k.ybh = k.sb("yb_hi", [128, H, NT], F32R, mixer)
            k.ybl = k.sb("yb_lo", [128, H, NT], F32R, mixer)
            k.run(attention)
            k.yb_ctx.close()
            k.mh = k.sb("mix_hi", [128, KD, NT], F32R, mix)
            k.ml = k.sb("mix_lo", [128, KD, NT], F32R, mix)
            k.run(gated_sum)
        with ExitStack() as k.experts, ExitStack() as k.rings, ExitStack() as k.routing:
            expert_tensors(k)
            k.run(project_out)
            mix.close()
            k.run(normalise_rows)
            k.run(choose_experts)
            k.routing.close()
            k.run(expert_blocks)
            k.rings.close()
            k.run(combine)


def start(k):
    nc, i = k.nc, k.i
    k.ident = k.sb("ident", [128, 128])
    k.ones = k.sb("ones", [128, 128])
    k.head_ones = k.sb("head_ones", [128, 128])
    k.triu = k.sb("triu", [128, 512])
    k.striu = k.sb("striu", [128, 128])
    k.later_neg = k.sb("later_neg", [128, 4, 128])
    k.causal_neg = k.sb("causal_neg", [128, 128])
    k.level = k.sb("level", [128, 7, 128])
    k.sel = k.sb("sel", [8, 8, 128])
    k.selpair = k.sb("selpair", [8, 4, 128])
    k.eps = k.sb("eps", [128, 1])
    k.one = k.sb("one", [128, 1])
    k.wconv = k.sb("wconv", [128, CONV_W, NCC])
    k.hist = k.sb("hist", [128, 3, NCC])
    k.gq = k.sb("gq", [128, 1])
    k.gk = k.sb("gk", [128, 1])
    k.go = k.sb("go", [128, 1])
    k.bgate = k.sb("bgate", [128, 16])
    k.sm_bias = k.sb("sm_bias", [128, 1])
    k.sm_sign = k.sb("sm_sign", [128, 1])
    k.sm_coef = k.sb("sm_coef", [128, 1])
    k.xi = k.sb("xor_i", [128, 128], I32, k.conv_ctx)
    k.xj = k.sb("xor_j", [128, 128], I32, k.conv_ctx)
    k.xs = k.sb("xor_s", [128, 128], I32, k.conv_ctx)
    k.junk = k.sb("nt_sq", [128, D], F32, k.stage)
    stat = k.sb("nt_stat", [128, 3, 5], F32, k.stage)
    xn = k.sb("nt_xn", [128, 2, D], F32, k.stage)
    g_mix = k.sb("g_mix_rows", [128, D], F32, k.stage)
    junk, rt, rr = k.junk, stat[:, 1], stat[:, 2]
    filled, loaded, ints, done, early = (k.sem("const_" + n) for n in ("filled", "loaded", "ints", "done", "early"))
    x_loaded = [k.sem(f"x_loaded{t}") for t in range(5)]
    gain = k.sem("nt_gain")
    rms = k.sem("nt_rms")
    normed = k.sem("nt_normed")
    moved = k.sem("nt_moved")
    hi_done = k.sem("nt_hi")
    lo_done = k.sem("nt_lo")
    with nc.Block() as block:
        @block.vector
        def _(v):
            c = k.chain(v, "vector")
            nc.vector.memset(k.eps[:], EPS)
            nc.vector.memset(k.ident[:], 0.0)
            nc.vector.memset(k.striu[:], 1.0).then_inc(early, 1)
            for t, val in ((k.sm_bias, 0.0), (k.sm_sign, 0.0), (k.sm_coef, 0.0), (k.ones, 1.0), (k.head_ones, 0.0),
                           (k.triu, 1.0), (k.later_neg, 0.0), (k.causal_neg, 0.0), (k.sel, 0.0), (k.selpair, 0.0),
                           (k.one, 1.0)):
                last = nc.vector.memset(t[tuple(slice(None) for _ in t.shape)], val)
            c(last)
            c(nc.vector.memset(k.head_ones[0:64, 0:64], 1.0))
            c(nc.vector.memset(k.head_ones[64:128, 64:128], 1.0))
            c(nc.vector.memset(k.sm_sign[0:8, :], -1.0))
            c(nc.vector.memset(k.sm_sign[32:40, :], -1.0))
            c(nc.vector.memset(k.sm_sign[64:72, :], 1.0))
            c(nc.vector.memset(k.sm_coef[0:40, :], -1.0))
            nc.vector.memset(k.sm_coef[64:72, :], -1.0).then_inc(filled, 1)

            def normalise(t):
                c0, n = TILES[t]
                v.wait_ge(rms, t + 1)
                c(nc.vector.reciprocal(rr[0:n, t:t + 1], rt[0:n, t:t + 1]))
                if t >= 2:
                    v.wait_ge(moved, t - 1)
                nc.vector.scalar_tensor_tensor(out=xn[0:n, t % 2, :], in0=k.x[0:n, t, :], scalar=rr[0:n, t:t + 1],
                                               in1=g_mix[0:n, :], op0=ALU.mult, op1=ALU.mult).then_inc(normed, 1)
            v.wait_ge(gain, 16)
            normalise(0)
            for t, (c0, n) in enumerate(TILES):
                if t + 1 < 5:
                    normalise(t + 1)
                for b in range(2):
                    v.wait_ge(hi_done, 2 * t + b + 1)
                    nc.vector.tensor_tensor(k.xlo[:, 4 * b:4 * b + 4, c0:c0 + n],
                                            k.bank[2 * (t % 2) + b][:, 0:4 * n].rearrange("p (k n) -> p k n", k=4),
                                            k.xhi[:, 4 * b:4 * b + 4, c0:c0 + n].bitcast(F32),
                                            ALU.subtract).then_inc(lo_done, 1)

        @block.gpsimd
        def _(g):
            g.wait_ge(early, 1)
            g.affine_select(out=k.ident[:], in_=k.ident[:], compare_op=ALU.not_equal, fill=1.0, base=0,
                            pattern=[[1, 128]], channel_multiplier=-1).then_inc(ints, 1)
            g.affine_select(out=k.striu[:], in_=k.striu[:], compare_op=ALU.is_gt, fill=0.0, base=0,
                            pattern=[[1, 128]], channel_multiplier=-1).then_inc(ints, 1)
            g.iota(k.xi[:], pattern=[[1, 128]], base=0, channel_multiplier=0).then_inc(ints, 1)
            g.iota(k.xj[:], pattern=[[0, 128]], base=0, channel_multiplier=1).then_inc(ints, 1)
            g.wait_ge(filled, 1)
            g.affine_select(out=k.triu[:], in_=k.triu[:], compare_op=ALU.is_ge, fill=0.0, base=0,
                            pattern=[[1, 512]], channel_multiplier=-1).then_inc(done, 1)
            g.affine_select(out=k.later_neg[:], in_=k.later_neg[:], compare_op=ALU.is_ge, fill=NEG, base=0,
                            pattern=[[0, 4], [1, 128]], channel_multiplier=-1).then_inc(done, 1)
            g.affine_select(out=k.causal_neg[:], in_=k.causal_neg[:], compare_op=ALU.is_ge, fill=NEG, base=0,
                            pattern=[[-1, 128]], channel_multiplier=1).then_inc(done, 1)
            g.affine_select(out=k.sel[:], in_=k.sel[:], compare_op=ALU.not_equal, fill=1.0, base=0,
                            pattern=[[-1, 8], [0, 128]], channel_multiplier=1).then_inc(done, 1)
            g.affine_select(out=k.selpair[:].rearrange("r p (a m) -> r p a m", a=2),
                            in_=k.selpair[:].rearrange("r p (a m) -> r p a m", a=2),
                            compare_op=ALU.not_equal, fill=1.0, base=0,
                            pattern=[[-2, 4], [-1, 2], [0, 64]], channel_multiplier=1).then_inc(done, 1)
            g.wait_ge(ints, 4)
            g.wait_ge(done, 5)

        @block.sync
        def _(sp):
            for t, (c0, n) in enumerate(TILES):
                src = i["x_sample"][0] if t == 0 else i["x_prompt"][0, 128 * (t - 1):128 * t, :]
                sp.dma_start(k.x[0:n, t, :], src).then_inc(x_loaded[t], 16)
                if t == 0:
                    sp.dma_start(g_mix[:], i["g_mix"].broadcast_to([128, D])).then_inc(gain, 16)
            sp.wait_ge(filled, 1)
            with nc.allow_non_contiguous_dma(reason="small parameters"):
                loads = [
                    (k.gq[0:64, :], i["g_qnorm"].rearrange("o c -> c o")),
                    (k.gq[64:128, :], i["g_qnorm"].rearrange("o c -> c o")),
                    (k.gk[0:64, :], i["g_knorm"].rearrange("o c -> c o")),
                    (k.gk[64:128, :], i["g_knorm"].rearrange("o c -> c o")),
                    (k.go[:], i["g_onorm"].rearrange("o c -> c o")),
                    (k.bgate[:], i["b_gate"][0].rearrange("(c p) -> p c", p=128)),
                    (k.sm_bias[0:8, :], i["b_f"].rearrange("o c -> c o")),
                    (k.sm_bias[64:72, :], i["dt_bias"].rearrange("o c -> c o")),
                    (k.sm_coef[64:72, :], i["a_log"].rearrange("o c -> c o")),
                ]
                for w in range(CONV_W):
                    loads.append((k.wconv[:, w, :], i["w_conv"][0, w].rearrange("(c p) -> p c", p=128)))
                for w in range(3):
                    loads.append((k.hist[:, w, :], i["state_gdn_conv"][0, 0, w].rearrange("(c p) -> p c", p=128)))
                for dst, src in loads:
                    sp.dma_start(dst, src).then_inc(loaded, 16)
            sp.wait_ge(loaded, 16 * len(loads))

        @block.scalar
        def _(a):
            c = k.chain(a, "scalar")
            a.wait_ge(early, 1)
            for t, (c0, n) in enumerate(TILES):
                a.wait_ge(x_loaded[t], 16)
                c(nc.scalar.activation(junk[0:n, :], k.x[0:n, t, :], ACT.Square, accum_out=stat[0:n, 0, t:t + 1]))
                nc.scalar.activation(rt[0:n, t:t + 1], stat[0:n, 0, t:t + 1], ACT.Sqrt, bias=k.eps[0:n, :],
                                     scale=1.0 / D).then_inc(rms, 1)
            for t, (c0, n) in enumerate(TILES):
                a.wait_ge(moved, t + 1)
                for b in range(2):
                    nc.scalar.activation(k.xhi[:, 4 * b:4 * b + 4, c0:c0 + n],
                                         k.bank[2 * (t % 2) + b][:, 0:4 * n].rearrange("p (k n) -> p k n", k=4),
                                         ACT.Copy).then_inc(hi_done, 1)

        @block.tensor
        def _(pe):
            pe.wait_ge(ints, 1)
            for t, (c0, n) in enumerate(TILES):
                pe.wait_ge(normed, t + 1)
                if t >= 2:
                    pe.wait_ge(lo_done, 2 * (t - 1))
                for d in range(KD):
                    last = nc.tensor.transpose(k.bank[2 * (t % 2) + d // 4][:, (d % 4) * n:(d % 4) * n + n],
                                               xn[0:n, t % 2, 128 * d:128 * d + 128], k.ident[0:n, 0:n])
                last.then_inc(moved, 1)


def levels_of_inversion(k, v):
    nc = k.nc
    c = k.chain(v, "vector")
    c(nc.vector.tensor_tensor(k.xs[:], k.xi[:], k.xj[:], ALU.bitwise_xor))
    for l in range(7):
        c(nc.vector.tensor_scalar(k.xi[:], k.xs[:], l, None, ALU.logical_shift_right))
        c(nc.vector.tensor_scalar(k.level[:, l, :], k.xi[:], 1, None, ALU.is_equal))
    for l in range(7):
        c(nc.vector.tensor_tensor(k.level[:, l, :], k.level[:, l, :], k.striu[:], ALU.mult))


def mixer_tensors(k):
    ctx = k.mixer
    k.xhi = k.sb("xhi", [128, KD, NT], F32R, ctx)
    k.xlo = k.sb("xlo", [128, KD, NT], F32R, ctx)
    k.yb_ctx = ctx.enter_context(ExitStack())
    k.yb = k.sb("yb", [128, H, NT], F32, k.yb_ctx)
    k.smt = k.sb("small_rows", [128, 5, 96], F32, ctx)


class Stream:

    def __init__(self, k, name, chunks, ctx, emptier=None, raws=RAWS):
        self.k, self.chunks, self.raws = k, chunks, raws
        k.raw = k.sb(name + "_w_raw", [128, raws, KD, 128], F32, ctx)
        k.whi = k.sb(name + "_w_hi", [128, OPS, KD, 128], F32R, ctx)
        k.wlo = k.sb(name + "_w_lo", [128, OPS, KD, 128], F32R, ctx)
        self.loaded = [k.sem(f"{name}_loaded{s}") for s in range(raws)]
        self.hi = k.sem(name + "_hi")
        self.lo = k.sem(name + "_lo")
        self.half = k.sem(name + "_half")
        self.emptier = emptier or [0] * len(chunks)
        self.emptied = [k.sem(f"{name}_emptied{e}") for e in range(max(self.emptier) + 1)]

    def emptied_of(self, c):
        return self.emptied[self.emptier[c]]

    def bank(self, c, h):
        return self.k.bank[2 * (c % 2) + h]

    def wait_emptied(self, eng, c, h):
        before = sum(1 for j in range(c) if self.emptier[j] == self.emptier[c])
        eng.wait_ge(self.emptied_of(c), 2 * before + h + 1)

    def load(self, sp, c):
        k = self.k
        srcs, nk = self.chunks[c][0], self.chunks[c][1]
        if c >= self.raws:
            sp.wait_ge(self.lo, c - self.raws + 1)
        for dst0, src in srcs:
            w = src.shape[-1]
            sp.dma_start(k.raw[:, c % self.raws, 0:nk, dst0:dst0 + w], src).then_inc(self.loaded[c % self.raws], 16)

    def loads_of(self, c):
        return 16 * sum(len(self.chunks[j][0]) for j in range(c % self.raws, c + 1, self.raws))

    def split_hi(self, a, c):
        k, nk = self.k, self.chunks[c][1]
        a.wait_ge(self.loaded[c % self.raws], self.loads_of(c))
        if c >= OPS:
            a.wait_ge(self.half, 2 * (c - OPS + 1))
        k.nc.scalar.activation(k.whi[:, c % OPS, 0:nk, :], k.raw[:, c % self.raws, 0:nk, :], ACT.Copy).then_inc(self.hi, 1)

    def split_lo(self, g, c):
        k, nk = self.k, self.chunks[c][1]
        g.wait_ge(self.hi, c + 1)
        k.nc.gpsimd.tensor_tensor(k.wlo[:, c % OPS, 0:nk, :], k.raw[:, c % self.raws, 0:nk, :],
                                  k.whi[:, c % OPS, 0:nk, :].bitcast(F32), ALU.subtract).then_inc(self.lo, 1)

    def product(self, pe, c, halves=(0, 1)):
        k = self.k
        nk, xhi, xlo = self.chunks[c][1:]
        pe.wait_ge(self.lo, c + 1)
        for h in halves:
            if c >= 2:
                self.wait_emptied(pe, c - 2, h)
            cols = slice(h * HALF, (h + 1) * HALF)
            for d in range(nk):
                for n, (w, x) in enumerate(((k.whi, xhi), (k.whi, xlo), (k.wlo, xhi))):
                    last = k.nc.tensor.matmul(self.bank(c, h)[:, 0:HALF], w[:, c % OPS, d, :], x[:, d, cols],
                                              start=(d == 0 and n == 0), stop=(d == nk - 1 and n == 2))
            last.then_inc(self.half, 1)


def w_in_cols(k, c0, n=128):
    return k.i["w_in"][0].rearrange("(k p) n -> p k n", p=128)[:, :, c0:c0 + n]


def convolved_projections(k):
    nc = k.nc
    ctx = k.conv_ctx
    k.cT = k.sb("conv_out", [128, NCC, NT], F32, ctx)
    with ExitStack() as ctx:
        k.sT = k.sb("small_cols", [96, NT], F32, ctx)
        tmp = k.sb("small_tmp", [96, 2, NT], F32, ctx)
        cin = k.sb("conv_in", [128, 2, 3 + NS + 3 + NP], F32, ctx)
        acc = k.sb("conv_acc", [128, 2, 3 + NS + NP], F32, ctx)
        last3 = k.sb("conv_last", [128, 6, NCC], F32, ctx)
        lastT = k.sb("conv_lastT", [96, 128], F32, ctx)
        W = 3 + NS + NP
        small = [(0, w_in_cols(k, C_LOGF, H)), (32, w_in_cols(k, C_BETA, H)), (64, w_in_cols(k, C_DECAY, H))]
        chunks = [([(0, w_in_cols(k, C_CONV + 128 * c))], KD, k.xhi, k.xlo) for c in range(NCC)]
        s = Stream(k, "cv", chunks + [(small, KD, k.xhi, k.xlo)], ctx)
        staged = k.sem("cv_staged")
        summed = k.sem("cv_summed")
        act_done = k.sem("cv_silu")
        zeroed = k.sem("cv_zeroed")
        kept = k.sem("cv_kept")

        norms = Norms(k, "l2", [(k.cT, c, DH ** -0.5 if c < 4 else 1.0, k.head_ones, 1.0,
                                 lambda g, c=c: g.wait_ge(act_done, c + 1)) for c in range(8)], ctx)
        group_at = {5: (0, 1), 7: (2, 3), 9: (4, 5), 11: (6, 7)}

        def silu(a, c):
            a.wait_ge(summed, c + 1)
            nc.scalar.activation(k.cT[:, c, 0:NS], acc[:, c % 2, 0:NS], ACT.Silu)
            nc.scalar.activation(k.cT[:, c, NS:NT], acc[:, c % 2, 3 + NS:W], ACT.Silu).then_inc(act_done, 1)

        with nc.Block() as block:
            @block.sync
            def _(sp):
                with nc.allow_non_contiguous_dma(reason="eight columns"):
                    for c in range(NCC):
                        s.load(sp, c)
                    sp.wait_ge(s.lo, NCC - RAWS + 1)
                    sp.wait_ge(zeroed, 1)
                    s.load(sp, NCC)

            @block.gpsimd
            def _(g):
                for c in range(NCC):
                    s.split_lo(g, c)
                    if 4 <= c < 12:
                        norms.square(g, c - 4)
                    if c == NCC - RAWS:
                        g.wait_ge(s.lo, NCC - RAWS + 1)
                        g.memset(k.raw[:, NCC % RAWS], 0.0).then_inc(zeroed, 1)
                s.split_lo(g, NCC)

            @block.tensor
            def _(pe):
                for c in range(NCC + 1):
                    s.product(pe, c)
                    norms.sums(pe, group_at.get(c, ()))

            @block.scalar
            def _(a):
                c_ = k.chain(a, "scalar")
                for c in range(LEAD):
                    s.split_hi(a, c)
                c_(nc.scalar.activation(k.sm_coef[64:72, :], k.sm_coef[64:72, :], ACT.Exp))
                c_(nc.scalar.activation(k.sm_coef[64:72, :], k.sm_coef[64:72, :], ACT.Copy, scale=-1.0))
                c_(nc.scalar.activation(k.gq[:], k.gq[:], ACT.Copy, scale=DH ** -0.5))
                for c in range(NCC):
                    if c + LEAD <= NCC:
                        s.split_hi(a, c + LEAD)
                    if c >= 2:
                        a.wait_ge(summed, c - 1)
                        a.wait_ge(kept, c - 1)
                    a.wait_ge(s.half, 2 * c + 1)
                    nc.scalar.activation(cin[:, c % 2, 3:3 + NS], s.bank(c, 0)[:, 0:NS], ACT.Copy)
                    nc.scalar.activation(cin[:, c % 2, 6 + NS:6 + HALF], s.bank(c, 0)[:, NS:HALF], ACT.Copy)\
                        .then_inc(s.emptied_of(c), 1)
                    a.wait_ge(s.half, 2 * c + 2)
                    nc.scalar.activation(cin[:, c % 2, 6 + HALF:6 + NT], s.bank(c, 1)[:, 0:HALF], ACT.Copy)\
                        .then_inc(s.emptied_of(c), 1)
                    if c >= 1:
                        silu(a, c - 1)
                    norms.roots(a, group_at.get(c - 1, ()))
                silu(a, NCC - 1)

            @block.vector
            def _(v):
                c_ = k.chain(v, "vector")
                levels_of_inversion(k, v)
                for b in range(2):
                    c_(nc.vector.memset(cin[:, b, 3 + NS:6 + NS], 0.0))
                for c in range(NCC):
                    ci, ac = cin[:, c % 2], acc[:, c % 2]
                    c_(nc.vector.tensor_copy(ci[:, 0:3], k.hist[:, :, c]))
                    s.wait_emptied(v, c, 1)
                    if c >= 2:
                        v.wait_ge(act_done, c - 1)
                    c_(nc.vector.tensor_scalar(ac[:, 0:W], ci[:, 0:W], k.wconv[:, 0, c:c + 1], None, ALU.mult))
                    for w in range(1, CONV_W):
                        op = nc.vector.scalar_tensor_tensor(out=ac[:, 0:W], in0=ci[:, w:w + W],
                                                            scalar=k.wconv[:, w, c:c + 1], in1=ac[:, 0:W],
                                                            op0=ALU.mult, op1=ALU.add)
                        if w < CONV_W - 1:
                            c_(op)
                        else:
                            op.then_inc(summed, 1)
                    nc.vector.tensor_copy(last3[:, 0:3, c], ci[:, NS:NS + 3])
                    nc.vector.tensor_copy(last3[:, 3:6, c], ci[:, 3 + NT:6 + NT]).then_inc(kept, 1)
                    v.wait_ge(kept, c + 1)
                    norms.scale(v, group_at.get(c - 1, ()))
                for h in range(2):
                    v.wait_ge(s.half, 2 * NCC + h + 1)
                    c_(nc.vector.tensor_scalar(k.sT[:, h * HALF:(h + 1) * HALF], s.bank(NCC, h)[0:96, 0:HALF],
                                               k.sm_bias[0:96, :], k.sm_sign[0:96, :], ALU.add, ALU.mult))
        e_done, l_done, d_done, tr, trc = (k.sem("sm_" + n) for n in ("exp", "ln", "rows", "tr", "trc"))
        stored = k.sem("sm_stored")
        with nc.Block() as block:
            @block.scalar
            def _(a):
                c = k.chain(a, "scalar")
                c(nc.scalar.activation(tmp[:, 0, :], k.sT[:], ACT.Abs))
                c(nc.scalar.activation(tmp[:, 1, :], tmp[:, 0, :], ACT.Exp, scale=-1.0))
                nc.scalar.activation(tmp[:, 0, :], tmp[:, 1, :], ACT.Ln, bias=k.one[0:96, :]).then_inc(l_done, 1)

            @block.vector
            def _(v):
                c = k.chain(v, "vector")
                v.wait_ge(l_done, 1)
                c(nc.vector.scalar_tensor_tensor(out=tmp[:, 1, :], in0=k.sT[:], scalar=0.0, in1=tmp[:, 0, :],
                                                 op0=ALU.max, op1=ALU.add))
                nc.vector.tensor_scalar(k.sT[:], tmp[:, 1, :], k.sm_coef[0:96, :], None, ALU.mult).then_inc(d_done, 1)
                v.wait_ge(tr, 1)
                c(nc.vector.tensor_copy(k.smt[:, 1:5, :], k.bank[2][:, 0:384].rearrange("p (t m) -> p t m", t=4)))
                c(nc.vector.tensor_copy(k.smt[0:NS, 0, :], k.bank[3][0:NS, 0:96]))
                nc.vector.tensor_copy(lastT[:], k.bank[4][0:96, 0:128]).then_inc(trc, 1)

            @block.tensor
            def _(pe):
                pe.wait_ge(d_done, 1)
                for t, (c0, n) in enumerate(TILES):
                    out = k.bank[3][0:NS, 0:96] if t == 0 else k.bank[2][:, 96 * (t - 1):96 * t]
                    nc.tensor.transpose(out, k.sT[:, c0:c0 + n], k.ident[0:96, 0:96])
                nc.tensor.transpose(k.bank[4][0:96, 0:128], last3[:].rearrange("p a c -> p (a c)"),
                                    k.ident[:, :]).then_inc(tr, 1)

            @block.sync
            def _(sp):
                sp.wait_ge(trc, 1)
                sp.dma_start(k.o["conv_s"][0, 0].rearrange("w (c m) -> (w c) m", m=128), lastT[0:48, :]).then_inc(stored, 16)
                sp.dma_start(k.o["conv_p"][0, 0].rearrange("w (c m) -> (w c) m", m=128), lastT[48:96, :]).then_inc(stored, 16)
                sp.dma_start(k.o["logf_s"][0, 0], k.smt[0:NS, 0, 0:H]).then_inc(stored, 16)
                sp.dma_start(k.o["logf_p"][0, 0].rearrange("(t p) h -> p t h", p=128), k.smt[:, 1:5, 0:H])\
                    .then_inc(stored, 16)
                sp.wait_ge(stored, 64)


class Norms:

    def __init__(self, k, name, items, ctx):
        self.k, self.items = k, items
        self.sq = k.sb(name + "_sq", [128, 4, NT], F32, ctx)
        self.rt = k.sb(name + "_rt", [128, 4, NT], F32, ctx)
        self.squared, self.summed, self.logged, self.rooted, self.scaled = (
            k.sem(f"{name}_{n}") for n in ("squared", "summed", "logged", "rooted", "scaled"))

    def square(self, g, j):
        T, c = self.items[j][0:2]
        self.items[j][5](g)
        if j >= 4:
            g.wait_ge(self.summed, j - 3)
        self.k.nc.gpsimd.tensor_tensor(self.sq[:, j % 4, :], T[:, c, :], T[:, c, :], ALU.mult).then_inc(self.squared, 1)

    def sums(self, pe, group):
        k = self.k
        for j in group:
            pe.wait_ge(self.squared, j + 1)
            if j >= 2:
                pe.wait_ge(self.logged, j - 1)
            for h in range(2):
                last = k.nc.tensor.matmul(k.bank[4 + 2 * (j % 2) + h][:, 0:HALF], self.items[j][3][:],
                                          self.sq[:, j % 4, h * HALF:(h + 1) * HALF], start=True, stop=True)
            last.then_inc(self.summed, 1)

    def roots(self, a, group):
        k = self.k
        for j in group:
            a.wait_ge(self.summed, j + 1)
            if j >= 4:
                a.wait_ge(self.scaled, j - 3)
            for h in range(2):
                last = k.nc.scalar.activation(self.rt[:, j % 4, h * HALF:(h + 1) * HALF],
                                              k.bank[4 + 2 * (j % 2) + h][:, 0:HALF], ACT.Ln,
                                              bias=k.eps[:], scale=self.items[j][4])
            last.then_inc(self.logged, 1)
        for j in group:
            a.wait_ge(self.logged, j + 1)
            k.nc.scalar.activation(self.rt[:, j % 4, :], self.rt[:, j % 4, :], ACT.Exp, scale=-0.5).then_inc(self.rooted, 1)

    def scale(self, v, group):
        for j in group:
            T, c, f = self.items[j][0:3]
            v.wait_ge(self.rooted, j + 1)
            self.k.nc.vector.scalar_tensor_tensor(out=T[:, c, :], in0=T[:, c, :], scalar=f, in1=self.rt[:, j % 4, :],
                                                  op0=ALU.mult, op1=ALU.mult).then_inc(self.scaled, 1)


def delta_net(k):
    nc = k.nc
    with ExitStack() as ctx:
        beta, G, nG, Gt, eG, egl, kf = (k.sb("g_" + n, [128, 5, H], F32, ctx)
                                        for n in ("beta", "cum", "ncum", "total", "exp", "exptot", "tail"))
        GT = k.sb("g_cols", [H, NT], F32, ctx)
        kg = k.sb("k_grown", [128, 5, WA], F32, ctx)
        kd = k.sb("k_tail", [128, 5, WA], F32, ctx)
        S = k.sb("state_p", [128, 4, DV], F32, ctx)
        Ss = k.sb("state_s", [128, 4, DV], F32, ctx)
        smask = k.sb("later_neg_s", [NS, 4, NS], F32, ctx)
        summed, cum, grown, kT, kread, loaded = (k.sem("g0_" + n) for n in ("sum", "cum", "exp", "kT", "kread", "state"))
        parts = [(slice(0, NS), slice(0, 1)), (slice(0, 128), slice(1, 5))]
        with nc.Block() as block:
            @block.sync
            def _(sp):
                for a in range(2):
                    sp.dma_start(Ss[64 * a:64 * a + 64], k.i["state_gdn"][0, 0].rearrange("(p a) k v -> a k p v", a=2)[a])\
                        .then_inc(loaded, 16)
                sp.wait_ge(loaded, 32)

            @block.tensor
            def _(pe):
                g = k.smt[:, :, 64:72]
                for t, (c0, n) in enumerate(TILES):
                    out = k.bank[1][0:n, 0:H] if t == 0 else k.bank[0][:, H * (t - 1):H * t]
                    nc.tensor.matmul(out, k.triu[0:n, 0:n], g[0:n, t, :], start=True, stop=True)
                    nc.tensor.matmul(k.bank[2][:, H * t:H * t + H], k.ones[0:n, :], g[0:n, t, :], start=True, stop=True)
                    out = k.bank[3][0:H, 0:n] if t == 0 else k.bank[4][0:H, 128 * (t - 1):128 * t]
                    last = nc.tensor.matmul(out, g[0:n, t, :], k.triu[0:n, 0:n], start=True, stop=True)
                last.then_inc(summed, 1)
                for p in range(4):
                    if p >= 2:
                        pe.wait_ge(kread, p - 1)
                    b = (5, 7)[p % 2]
                    b0 = (6, 1)[p % 2]
                    if p == 1:
                        pe.wait_ge(cum, 1)
                    for t, (c0, n) in enumerate(TILES):
                        out = k.bank[b0][0:n, 0:128] if t == 0 else k.bank[b][:, 128 * (t - 1):128 * t]
                        last = nc.tensor.transpose(out, k.cT[:, 4 + p, c0:c0 + n], k.ident[:])
                    last.then_inc(kT, 1)

            @block.vector
            def _(v):
                c = k.chain(v, "vector")
                c(nc.vector.memset(smask[:], 0.0))
                v.wait_ge(summed, 1)
                c(nc.vector.tensor_copy(G[0:NS, 0], k.bank[1][0:NS, 0:H]))
                c(nc.vector.tensor_copy(G[:, 1:5], k.bank[0][:, 0:4 * H].rearrange("p (t h) -> p t h", t=4)))
                c(nc.vector.tensor_copy(Gt[:], k.bank[2][:, 0:5 * H].rearrange("p (t h) -> p t h", t=5)))
                c(nc.vector.tensor_copy(GT[:, 0:NS], k.bank[3][0:H, 0:NS]))
                c(nc.vector.tensor_copy(GT[:, NS:NT], k.bank[4][0:H, 0:NP]))
                c(nc.vector.tensor_copy(smask[:], k.later_neg[0:NS, :, 0:NS]))
                for rows, ts in parts:
                    c(nc.vector.tensor_tensor(kf[rows, ts], Gt[rows, ts], G[rows, ts], ALU.subtract))
                    c(nc.vector.tensor_scalar(nG[rows, ts], G[rows, ts], -1.0, None, ALU.mult))
                nc.vector.memset(S[:], 0.0).then_inc(cum, 1)
                v.wait_ge(grown, 1)
                for p in range(4):
                    v.wait_ge(kT, p + 1)
                    b = (5, 7)[p % 2]
                    b0 = (6, 1)[p % 2]
                    for f, dst in ((eG, kg), (kf, kd)):
                        fac = f[:, :, 2 * p:2 * p + 2].unsqueeze(3)
                        nc.vector.tensor_tensor(
                            dst[0:NS, 0, 128 * p:128 * p + 128].rearrange("p (a c) -> p a c", a=2),
                            k.bank[b0][0:NS, 0:128].rearrange("p (a c) -> p a c", a=2),
                            fac[0:NS, 0].broadcast_to([NS, 2, 64]), ALU.mult)
                        last = nc.vector.tensor_tensor(
                            dst[:, 1:5, 128 * p:128 * p + 128].rearrange("p t (a c) -> p t a c", a=2),
                            k.bank[b][:].rearrange("p (t a c) -> p t a c", t=4, a=2),
                            fac[:, 1:5].broadcast_to([128, 4, 2, 64]), ALU.mult)
                    last.then_inc(kread, 1)

            @block.scalar
            def _(a):
                c = k.chain(a, "scalar")
                for rows, ts in parts:
                    c(nc.scalar.activation(beta[rows, ts], k.smt[rows, ts, 32:40], ACT.Exp))
                a.wait_ge(cum, 1)
                for rows, ts in parts:
                    c(nc.scalar.activation(eG[rows, ts], G[rows, ts], ACT.Exp))
                    c(nc.scalar.activation(kf[rows, ts], kf[rows, ts], ACT.Exp))
                nc.scalar.activation(egl[:], Gt[:], ACT.Exp).then_inc(grown, 1)

        def units(r, a):
            if r == 0:
                return [(2 * u + a, 0, 0) for u in range(4)]
            return [(2 * (r - 1) + a, t, TILES[t][0]) for t in range(1, 5)]

        R, A, U = range(5), range(2), range(4)
        width = lambda r: NS if r == 0 else 128
        levels = lambda r: range(5 if r == 0 else 7)
        base = lambda h: 64 * (h % 2)
        st = lambda r: Ss if r == 0 else S
        ra = [(r, a) for r in R for a in A]
        ral = [(r, l, a) for r in R for l in levels(r) for a in A]
        rua = [(r, u, a) for r in R for u in U for a in A]
        m = {n: k.marks("g_" + n, names) for n, names in dict(
            scores=ra, low=ral, grown=[x for x in ral if x[1] > 0], wt=ra, vsum=rua, upd=rua, egp=R, vT=ra,
            dec=ra, lowc=[x for x in ral if x[1] > 0], wtc=ra, outc=ra, egx=R, vtok=ra,
            mt=ra, inv=ral, vnew=rua, state=rua,
            ml=ral, qd=R).items()}
        dec, mt, at, P, X, Xt, wT, vt = (k.sb("g_" + n, [128, 2, 512], F32, ctx)
                                         for n in ("dec", "mt", "at", "low", "inv", "invT", "wT", "vt"))
        ml = k.sb("g_ml", [128, 2, 2, 512], F32, ctx)
        qd = k.sb("g_qd", [128, 512], F32, ctx)
        egp = k.sb("g_egp", [128, 512], F32, ctx)
        vn = k.sb("g_vn", [128, 2, DV], F32, ctx)
        stored, zeroed, filled = k.sem("g_stored"), k.sem("g_zeroed"), k.sem("g_filled")
        zero = k.sb("g_zero", [128, D], F32, ctx)
        bank = lambda a, n: k.bank[4 * a + n]
        qcols = lambda r, h, t: slice(NS * (h // 2), NS * (h // 2) + NS) if r == 0 else slice(128 * (t - 1), 128 * t)
        with nc.Block() as block:
            @block.tensor
            def _(pe):
                for r in R:
                    w = width(r)
                    if r >= 1:
                        m["outc"].wait(pe, (r - 1, 0))
                    if r == 0:
                        for p in range(4):
                            last = nc.tensor.matmul(bank(0, 3)[:, NS * p:NS * p + NS], k.selpair[:, p, :], GT[:, 0:NS],
                                                    start=True, stop=True)
                    else:
                        last = nc.tensor.matmul(bank(0, 3)[:], k.selpair[:, r - 1, :], GT[:, NS:NT], start=True, stop=True)
                    m["egp"].mark(last, r)
                    for a in A:
                        for u, (h, t, c0) in enumerate(units(r, a)):
                            b, cols, o = base(h), slice(c0, c0 + w), slice(u * w, u * w + w)
                            kT_, qT_ = k.cT[b:b + 64, 4 + h // 2, cols], k.cT[b:b + 64, h // 2, cols]
                            nc.tensor.matmul(bank(a, 0)[0:w, o], kT_, kT_, start=True, stop=True)
                            nc.tensor.matmul(bank(a, 1)[0:w, o], kT_, qT_, start=True, stop=True)
                        neg = smask[:] if r == 0 else k.later_neg[:]
                        if r >= 1:
                            m["state"].wait(pe, (r - 1, 3, a))
                        nc.tensor.matmul(bank(a, 2)[0:w, 0:4 * w], k.ident[0:w, 0:w], neg, start=True, stop=False)
                        if r == 0:
                            for u, (h, t, c0) in enumerate(units(r, a)):
                                last = nc.tensor.matmul(bank(a, 2)[0:w, u * w:u * w + w], k.sel[:, h, 0:w], GT[:, 0:NS],
                                                        start=False, stop=(u == 3))
                        else:
                            last = nc.tensor.matmul(bank(a, 2)[:], k.sel[:, units(r, a)[0][0], :], GT[:, NS:NT],
                                                    start=False, stop=True)
                        m["scores"].mark(last, (r, a))
                    m["egx"].wait(pe, r)
                    for a in A:
                        if r >= 1:
                            m["outc"].wait(pe, (r - 1, a))
                        for u, (h, t, c0) in enumerate(units(r, a)):
                            last = nc.tensor.transpose(bank(a, 3)[0:w, u * 128:u * 128 + 128], k.cT[:, 8 + h, c0:c0 + w],
                                                       k.ident[:])
                        m["vT"].mark(last, (r, a))
                    for l in levels(r):
                        for a in A:
                            m["ml"].wait(pe, (r, l, a))
                            if l >= 1:
                                m["inv"].wait(pe, (r, l - 1, a))
                            for u in U:
                                o = slice(u * w, u * w + w)
                                rhs = k.ident[0:w, 0:w] if l == 0 else X[0:w, a, o]
                                last = nc.tensor.matmul(bank(a, 0)[0:w, o], ml[0:w, a, l % 2, o], rhs, start=True, stop=True)
                            m["low"].mark(last, (r, l, a))
                        if l == 0:
                            continue
                        for a in A:
                            m["lowc"].wait(pe, (r, l, a))
                            for u in U:
                                o = slice(u * w, u * w + w)
                                if l < levels(r)[-1]:
                                    nc.tensor.matmul(bank(a, 1)[0:w, o], Xt[0:w, a, o], P[0:w, a, o], start=True, stop=True)
                                last = nc.tensor.matmul(bank(a, 2)[0:w, o], P[0:w, a, o], Xt[0:w, a, o], start=True, stop=True)
                            m["grown"].mark(last, (r, l, a))
                    for a in A:
                        m["inv"].wait(pe, (r, levels(r)[-1], a))
                        for u, (h, t, c0) in enumerate(units(r, a)):
                            b = base(h)
                            last = nc.tensor.matmul(bank(a, 0)[b:b + 64, u * w:u * w + w], kg[0:w, t, 64 * h:64 * h + 64],
                                                    Xt[0:w, a, u * w:u * w + w], start=True, stop=True)
                        m["wt"].mark(last, (r, a))
                    for u in U:
                        for a in A:
                            h, t, c0 = units(r, a)[u]
                            b, o = base(h), slice(u * w, u * w + w)
                            first = r > 0 and u == 0
                            if u == 0:
                                m["wtc"].wait(pe, (r, a))
                                m["vtok"].wait(pe, (r, a))
                            elif r > 0:
                                m["state"].wait(pe, (r, u - 1, a))
                            if u > 0:
                                m["vnew"].wait(pe, (r, u - 1, a))
                            last = nc.tensor.matmul(bank(a, 1)[0:w, 0:DV], Xt[0:w, a, o], vt[0:w, a, u * DV:u * DV + DV],
                                                    start=True, stop=first)
                            if not first:
                                last = nc.tensor.matmul(bank(a, 1)[0:w, 0:DV], wT[b:b + 64, a, o],
                                                        st(r)[b:b + 64, h // 2, :], start=False, stop=True)
                            m["vsum"].mark(last, (r, u, a))
                        for a in A:
                            h, t, c0 = units(r, a)[u]
                            b, o = base(h), slice(u * w, u * w + w)
                            first = r > 0 and u == 0
                            if not first:
                                nc.tensor.matmul(bank(a, 3)[:, o], st(r)[b:b + 64, h // 2, :],
                                                 qd[b:b + 64, qcols(r, h, t)], start=True, stop=False)
                            m["vnew"].wait(pe, (r, u, a))
                            nc.tensor.matmul(bank(a, 3)[:, o], vn[0:w, a, :], at[0:w, a, o], start=first, stop=True)
                            if u > 0:
                                m["state"].wait(pe, (r, u - 1, a))
                            last = nc.tensor.matmul(bank(a, 2)[b:b + 64, 0:DV], kd[0:w, t, 64 * h:64 * h + 64],
                                                    vn[0:w, a, :], start=True, stop=True)
                            m["upd"].mark(last, (r, u, a))

            @block.scalar
            def _(s):
                for r in R:
                    w = width(r)
                    m["egp"].wait(s, r)
                    if r >= 1:
                        m["qd"].wait(s, r - 1)
                    m["egx"].mark(nc.scalar.activation(egp[:, 0:4 * w], bank(0, 3)[:, 0:4 * w], ACT.Exp), r)
                    for a in A:
                        m["scores"].wait(s, (r, a))
                        for u, (h, t, c0) in enumerate(units(r, a)):
                            o = slice(u * w, u * w + w)
                            last = nc.scalar.activation(dec[0:w, a, o], bank(a, 2)[0:w, o], ACT.Exp, bias=nG[0:w, t, h:h + 1])
                        m["dec"].mark(last, (r, a))
                    for a in A:
                        m["vT"].wait(s, (r, a))
                        m["vtok"].mark(nc.scalar.activation(vt[0:w, a, :], bank(a, 3)[0:w, :], ACT.Copy), (r, a))
                    for l in levels(r)[1:]:
                        for a in A:
                            m["low"].wait(s, (r, l, a))
                            m["lowc"].mark(nc.scalar.activation(P[0:w, a, 0:4 * w], bank(a, 0)[0:w, 0:4 * w], ACT.Copy),
                                           (r, l, a))
                    for a in A:
                        m["wt"].wait(s, (r, a))
                        b = 64 * a
                        last = nc.scalar.activation(wT[b:b + 64, a, 0:4 * w], bank(a, 0)[b:b + 64, 0:4 * w], ACT.Copy,
                                                    scale=-1.0)
                        m["wtc"].mark(last, (r, a))
                    for a in A:
                        m["upd"].wait(s, (r, 3, a))
                        if r == 0:
                            out, src = k.yb[:, a::2, 0:NS], bank(a, 3)[:, 0:128].rearrange("p (h n) -> p h n", h=4)
                        else:
                            out, src = k.yb[:, 2 * (r - 1) + a, NS:NT], bank(a, 3)[:]
                        m["outc"].mark(nc.scalar.activation(out, src, ACT.Copy), (r, a))

            @block.vector
            def _(v):
                nc.vector.memset(zero[:], 0.0).then_inc(zeroed, 1)
                for r in R:
                    w = width(r)
                    idb = k.ident[0:w, 0:w].unsqueeze(1).broadcast_to([w, 4, w])
                    for a in A:
                        m["dec"].wait(v, (r, a))
                        for u, (h, t, c0) in enumerate(units(r, a)):
                            o = slice(u * w, u * w + w)
                            nc.vector.scalar_tensor_tensor(out=mt[0:w, a, o], in0=bank(a, 0)[0:w, o],
                                                           scalar=beta[0:w, t, h:h + 1], in1=dec[0:w, a, o],
                                                           op0=ALU.mult, op1=ALU.mult)
                        m["mt"].mark(nc.vector.tensor_tensor(at[0:w, a, 0:4 * w], bank(a, 1)[0:w, 0:4 * w],
                                                             dec[0:w, a, 0:4 * w], ALU.mult), (r, a))
                    for l in levels(r):
                        for a in A:
                            f = slice(0, 4 * w)
                            if l == 0:
                                m["low"].wait(v, (r, l, a))
                                nc.vector.tensor_tensor(X[0:w, a, f].rearrange("p (u n) -> p u n", u=4), idb,
                                                        bank(a, 0)[0:w, f].rearrange("p (u n) -> p u n", u=4), ALU.subtract)
                                last = nc.vector.tensor_tensor(Xt[0:w, a, f].rearrange("p (u n) -> p u n", u=4), idb,
                                                               ml[0:w, a, 0, f].rearrange("p (u n) -> p u n", u=4),
                                                               ALU.subtract)
                            else:
                                m["grown"].wait(v, (r, l, a))
                                if l < levels(r)[-1]:
                                    nc.vector.tensor_tensor(X[0:w, a, f], X[0:w, a, f], bank(a, 1)[0:w, f], ALU.subtract)
                                last = nc.vector.tensor_tensor(Xt[0:w, a, f], Xt[0:w, a, f], bank(a, 2)[0:w, f],
                                                               ALU.subtract)
                            m["inv"].mark(last, (r, l, a))
                    for u in U:
                        for a in A:
                            h, t, c0 = units(r, a)[u]
                            m["vsum"].wait(v, (r, u, a))
                            if u > 0:
                                m["upd"].wait(v, (r, u - 1, a))
                            m["vnew"].mark(nc.vector.tensor_scalar(vn[0:w, a, :], bank(a, 1)[0:w, 0:DV],
                                                                   beta[0:w, t, h:h + 1], None, ALU.mult), (r, u, a))
                        for a in A:
                            h, t, c0 = units(r, a)[u]
                            b = base(h)
                            m["upd"].wait(v, (r, u, a))
                            if u > 0:
                                m["state"].wait(v, (r, u - 1, a))
                            m["state"].mark(nc.vector.scalar_tensor_tensor(
                                out=st(r)[b:b + 64, h // 2, :], in0=st(r)[b:b + 64, h // 2, :],
                                scalar=egl[b:b + 64, t, h:h + 1], in1=bank(a, 2)[b:b + 64, 0:DV],
                                op0=ALU.mult, op1=ALU.add), (r, u, a))

            @block.gpsimd
            def _(g):
                for r in R:
                    w = width(r)
                    m["egx"].wait(g, r)
                    if r >= 1:
                        m["upd"].wait(g, (r - 1, 3, 1))
                    if r == 0:
                        q, e = qd[:, 0:4 * w].rearrange("p (c n) -> p c n", c=4), egp[:, 0:4 * w].rearrange("p (c n) -> p c n", c=4)
                        m["qd"].mark(nc.gpsimd.tensor_tensor(q, k.cT[:, 0:4, 0:NS], e, ALU.mult), r)
                    else:
                        m["qd"].mark(nc.gpsimd.tensor_tensor(qd[:], k.cT[:, r - 1, NS:NT], egp[:], ALU.mult), r)
                    for l in levels(r):
                        for a in A:
                            if l == 0:
                                m["mt"].wait(g, (r, a))
                            if l >= 2:
                                m["low"].wait(g, (r, l - 2, a))
                            if l == 2:
                                m["inv"].wait(g, (r, 0, a))
                            f = slice(0, 4 * w)
                            m["ml"].mark(nc.gpsimd.tensor_tensor(
                                ml[0:w, a, l % 2, f].rearrange("p (u n) -> p u n", u=4),
                                mt[0:w, a, f].rearrange("p (u n) -> p u n", u=4),
                                k.level[0:w, l, 0:w].unsqueeze(1).broadcast_to([w, 4, w]), ALU.mult), (r, l, a))

            @block.sync
            def _(sp):
                sp.wait_ge(zeroed, 1)
                sp.dma_start(k.table[NT:NT + 1, :], zero[0:1, :]).then_inc(filled, 16)
                for row in range(NE * SLOTS, NB * SLOTS, 128):
                    sp.dma_start(k.yblk[row:row + 128, :], zero[:]).then_inc(filled, 16)
                sp.wait_ge(filled, 16 * (1 + MORE * SLOTS // 128))
                for r, src, name in ((0, Ss, "state_s"), (4, S, "state_p")):
                    m["state"].wait(sp, (r, 3, 1))
                    for a in range(2):
                        sp.dma_start(k.o[name][0, 0].rearrange("(p a) k v -> a k p v", a=2)[a], src[64 * a:64 * a + 64])\
                            .then_inc(stored, 16)
                sp.wait_ge(stored, 64)


def attention(k):
    nc = k.nc
    with ExitStack() as ctx:
        fT = k.sb("fox_cols", [128, 12, NT], F32, ctx)
        with ExitStack() as inner:
            zs = k.sb("z_silu", [128, 2, NT], F32, inner)
            chunks = [([(0, w_in_cols(k, C_FQ + 128 * c))], KD, k.xhi, k.xlo) for c in range(12)]
            chunks += [([(0, w_in_cols(k, C_Z + 128 * c))], KD, k.xhi, k.xlo) for c in range(H)]
            s = Stream(k, "fz", chunks, inner, [0] * 12 + [1] * 8, raws=3)
            norms = Norms(k, "hn", [(k.yb, h, k.go[:], k.ones, 1.0 / DV, lambda g: None) for h in range(H)] +
                          [(fT, c, (k.gq if c < 4 else k.gk)[:], k.head_ones, 1.0 / DH,
                            lambda g, c=c: s.wait_emptied(g, c, 1)) for c in range(8)], inner)
            group_at = {2 * g + 1: (2 * g, 2 * g + 1) for g in range(8)}
            gate, hi, lo = k.sem("z_gated"), k.sem("z_hi"), k.sem("z_lo")
            with nc.Block() as block:
                @block.sync
                def _(sp):
                    for c in range(20):
                        s.load(sp, c)

                @block.gpsimd
                def _(g):
                    for c in range(20):
                        s.split_lo(g, c)
                        if c >= 2 and c < 18:
                            norms.square(g, c - 2)

                @block.tensor
                def _(pe):
                    for c in range(20):
                        s.product(pe, c)
                        norms.sums(pe, group_at.get(c, ()))

                def high(a, h):
                    a.wait_ge(gate, h + 1)
                    nc.scalar.activation(k.ybh[:, h, :], k.yb[:, h, :], ACT.Copy).then_inc(hi, 1)

                @block.scalar
                def _(a):
                    for c in range(LEAD):
                        s.split_hi(a, c)
                    for c in range(20):
                        if c + LEAD < 20:
                            s.split_hi(a, c + LEAD)
                        if c >= 14:
                            a.wait_ge(gate, c - 13)
                        for h in range(2 if c >= 12 else 0):
                            a.wait_ge(s.half, 2 * c + h + 1)
                            nc.scalar.activation(zs[:, c % 2, h * HALF:(h + 1) * HALF], s.bank(c, h)[:, 0:HALF],
                                                 ACT.Silu).then_inc(s.emptied_of(c), 1)
                        norms.roots(a, group_at.get(c - 1, ()))
                        if c >= 13:
                            high(a, c - 13)
                    high(a, H - 1)

                @block.vector
                def _(v):
                    for c in range(12):
                        for h in range(2):
                            v.wait_ge(s.half, 2 * c + h + 1)
                            nc.vector.tensor_copy(fT[:, c, h * HALF:(h + 1) * HALF], s.bank(c, h)[:, 0:HALF])\
                                .then_inc(s.emptied_of(c), 1)
                        norms.scale(v, group_at.get(c - 2, ()))
                    for h in range(H):
                        norms.scale(v, group_at.get(10 + h, ()))
                        s.wait_emptied(v, 12 + h, 1)
                        if h == 0:
                            v.wait_ge(norms.scaled, H)
                        nc.vector.tensor_tensor(k.yb[:, h, :], k.yb[:, h, :], zs[:, h % 2, :], ALU.mult)\
                            .then_inc(gate, 1)
                        v.wait_ge(hi, h + 1)
                        nc.vector.tensor_tensor(k.ybl[:, h, :], k.yb[:, h, :], k.ybh[:, h, :].bitcast(F32),
                                                ALU.subtract).then_inc(lo, 1)
        k.yah = k.sb("ya_hi", [128, 4, NT], F32R, k.mixer)
        k.yal = k.sb("ya_lo", [128, 4, NT], F32R, k.mixer)
        vt = k.sb("fox_v", [128, 5, WA], F32, ctx)
        vp = k.sb("fox_vpast", [128, WA], F32, ctx)
        kTs = k.sb("fox_kT_s", [128, 4, PAST + NS], F32, ctx)
        ncT = k.sb("fox_nc", [H, PAST + NS + NP], F32, ctx)
        with ExitStack() as inner:
            kt = k.sb("fox_k", [128, 2, WA], F32, inner)
            kp = k.sb("fox_kpast", [128, WA], F32, inner)
            lp = k.sb("fox_logf_past", [128, H], F32, inner)
            loaded, tr, kc, vc, rest, restc, stored = (k.sem("f1_" + n) for n in
                                                       ("loaded", "tr", "kcopy", "vcopy", "rest", "restcopy", "stored"))
            with nc.Block() as block:
                @block.sync
                def _(sp):
                    sp.dma_start(kp[:], k.i["cache_fox_k"][0, 0].rearrange("p h c -> p (h c)")).then_inc(loaded, 16)
                    sp.dma_start(vp[:], k.i["cache_fox_v"][0, 0].rearrange("p h c -> p (h c)")).then_inc(loaded, 16)
                    sp.dma_start(lp[:], k.i["cache_fox_logf"][0, 0]).then_inc(loaded, 16)
                    for t, (c0, n) in enumerate(TILES):
                        for what, src, sem in (("k", kt[0:n, t % 2, :], kc), ("v", vt[0:n, t, :], vc)):
                            sp.wait_ge(sem, t + 1)
                            dst = k.o[what + ("_s" if t == 0 else "_p")][0, 0].rearrange("t h c -> t (h c)")
                            dst = dst if t == 0 else dst[128 * (t - 1):128 * t, :]
                            sp.dma_start(dst, src).then_inc(stored, 16)
                        sp.wait_ge(stored, 32 * (t + 1))
                    sp.wait_ge(loaded, 48)

                @block.tensor
                def _(pe):
                    for t, (c0, n) in enumerate(TILES):
                        if t >= 2:
                            pe.wait_ge(kc, t - 1)
                            pe.wait_ge(vc, t - 1)
                        for part in (4, 8):
                            b = k.bank[2 * (t % 2) + (part == 8)]
                            for c in range(4):
                                last = nc.tensor.transpose(b[0:n, 128 * c:128 * c + 128], fT[:, part + c, c0:c0 + n],
                                                           k.ident[:])
                        last.then_inc(tr, 1)
                    pe.wait_ge(loaded, 48)
                    for c in range(4):
                        nc.tensor.transpose(k.bank[4][:, 128 * c:128 * c + 128], kp[:, 128 * c:128 * c + 128], k.ident[:])
                    for j in range(4):
                        nc.tensor.matmul(k.bank[5][0:H, 128 * j:NP], k.smt[:, 1 + j, 0:H], k.triu[:, 0:NP - 128 * j],
                                         start=(j == 0), stop=(j == 3))
                    nc.tensor.matmul(k.bank[6][0:H, 0:PAST + NS], lp[:], k.triu[:, 0:PAST + NS], start=True, stop=False)
                    nc.tensor.matmul(k.bank[6][0:H, PAST:PAST + NS], k.smt[0:NS, 0, 0:H], k.triu[0:NS, 0:NS],
                                     start=False, stop=True).then_inc(rest, 1)

                @block.vector
                def _(v):
                    for t, (c0, n) in enumerate(TILES):
                        v.wait_ge(tr, t + 1)
                        if t >= 2:
                            v.wait_ge(stored, 32 * (t - 1))
                        nc.vector.tensor_copy(kt[0:n, t % 2, :], k.bank[2 * (t % 2)][0:n, :]).then_inc(kc, 1)
                    v.wait_ge(rest, 1)
                    nc.vector.tensor_copy(kTs[:, :, 0:PAST], k.bank[4][:].rearrange("p (c n) -> p c n", c=4))
                    nc.vector.tensor_copy(kTs[:, :, PAST:PAST + NS], fT[:, 4:8, 0:NS])
                    nc.vector.tensor_scalar(ncT[:, 0:PAST + NS], k.bank[6][0:H, 0:PAST + NS], -1.0, None, ALU.mult)
                    nc.vector.tensor_scalar(ncT[:, PAST + NS:], k.bank[5][0:H, :], -1.0, None, ALU.mult)

                @block.scalar
                def _(a):
                    for t, (c0, n) in enumerate(TILES):
                        a.wait_ge(tr, t + 1)
                        nc.scalar.activation(vt[0:n, t, :], k.bank[2 * (t % 2) + 1][0:n, :], ACT.Copy).then_inc(vc, 1)

        fox_heads(k, fT, vt, vp, kTs, ncT)


def fox_heads(k, fT, vt, vp, kTs, ncT):
    nc = k.nc
    items = [(h, t) for h in range(H) for t in range(5)]
    J = len(items)
    base = lambda h: 64 * (h % 2)

    def sizes(t):
        n = TILES[t][1]
        blocks = [(0, PAST), (PAST, NS)] if t == 0 else [(128 * b, 128) for b in range(t)]
        return n, blocks[-1][0] + blocks[-1][1], blocks

    with ExitStack() as ctx:
        ncb = k.sb("ncb", [128, 2, PAST + NS + NP], F32, ctx)
        sc = k.sb("f_scores", [128, 2, NP], F32, ctx)
        pr = k.sb("f_probs", [128, 3, NP], F32, ctx)
        pT = k.sb("f_probsT", [128, 2, NP], F32, ctx)
        st = k.sb("f_stat", [128, 4, J], F32, ctx)
        bias, biasc, score, biased, probs, scaled, turned, turnedc, out, outh, outl = (
            k.sem("f_" + n) for n in ("bias", "biasc", "score", "biased", "probs", "scaled", "turned", "turnedc",
                                      "out", "outh", "outl"))
        with nc.Block() as block:
            @block.tensor
            def _(pe):
                def scores(j):
                    h, t = items[j]
                    n, nk, blocks = sizes(t)
                    b, c0 = base(h), TILES[t][0]
                    if t == 0:
                        if h >= 1:
                            pe.wait_ge(biasc, h)
                        nc.tensor.matmul(k.bank[6][:, 0:PAST + NS], k.sel[:, h, :], ncT[:, 0:PAST + NS],
                                         start=True, stop=True)
                        nc.tensor.matmul(k.bank[7][:], k.sel[:, h, :], ncT[:, PAST + NS:], start=True, stop=True)\
                            .then_inc(bias, 1)
                    if j >= 2:
                        pe.wait_ge(biased, j - 1)
                    keys = kTs[b:b + 64, h // 2, :] if t == 0 else fT[b:b + 64, 4 + h // 2, NS:NS + nk]
                    nc.tensor.matmul(k.bank[j % 2][0:n, 0:nk], fT[b:b + 64, h // 2, c0:c0 + n], keys, start=True, stop=False)
                    m0, mn = blocks[-1]
                    nc.tensor.matmul(k.bank[j % 2][0:n, m0:m0 + mn], k.ident[0:n, 0:n], k.causal_neg[0:n, 0:mn],
                                     start=False, stop=True).then_inc(score, 1)

                def turn(j):
                    h, t = items[j]
                    n, nk, blocks = sizes(t)
                    pe.wait_ge(scaled, j + 1)
                    if j >= 2:
                        pe.wait_ge(turnedc, j - 1)
                    for i, (m0, mn) in enumerate(blocks):
                        last = nc.tensor.transpose(k.bank[2 + j % 2][0:mn, i * n:i * n + n], pr[0:n, j % 3, m0:m0 + mn],
                                                   k.ident[0:n, 0:n])
                    last.then_inc(turned, 1)

                def values(j):
                    h, t = items[j]
                    n, nk, blocks = sizes(t)
                    b = base(h)
                    pe.wait_ge(turnedc, j + 1)
                    if j >= 2:
                        pe.wait_ge(outl, j - 1)
                    for i, (m0, mn) in enumerate(blocks):
                        hv = slice(64 * h, 64 * h + 64)
                        v = (vp[:, hv] if i == 0 else vt[0:NS, 0, hv]) if t == 0 else vt[:, 1 + i, hv]
                        last = nc.tensor.matmul(k.bank[4 + j % 2][b:b + 64, 0:n], v, pT[0:mn, j % 2, i * n:i * n + n],
                                                start=(i == 0), stop=(i == len(blocks) - 1))
                    last.then_inc(out, 1)

                for j in range(J + 3):
                    if j < J:
                        scores(j)
                    if 2 <= j < J + 2:
                        turn(j - 2)
                    if j >= 3:
                        values(j - 3)

            @block.vector
            def _(v):
                own = k.chain(v, "vector")

                def biases(j):
                    h, t = items[j]
                    n, nk, blocks = sizes(t)
                    v.wait_ge(score, j + 1)
                    v.wait_ge(biasc, h + 1)
                    if j >= 2:
                        v.wait_ge(probs, j - 1)
                    cols = slice(0, nk) if t == 0 else slice(PAST + NS, PAST + NS + nk)
                    own(nc.vector.tensor_tensor_reduce(out=sc[0:n, j % 2, 0:nk], in0=k.bank[j % 2][0:n, 0:nk],
                                                   in1=ncb[0:n, h % 2, cols], scale=1.0, scalar=-3e38,
                                                   op0=ALU.add, op1=ALU.max, accum_out=st[0:n, 0, j:j + 1]))
                    nc.vector.tensor_scalar(st[0:n, 1, j:j + 1], st[0:n, 0, j:j + 1], -1.0, None, ALU.mult)\
                        .then_inc(biased, 1)

                def scale(j):
                    h, t = items[j]
                    n, nk, blocks = sizes(t)
                    v.wait_ge(probs, j + 1)
                    own(nc.vector.reciprocal(st[0:n, 3, j:j + 1], st[0:n, 2, j:j + 1]))
                    nc.vector.tensor_scalar(pr[0:n, j % 3, 0:nk], pr[0:n, j % 3, 0:nk], st[0:n, 3, j:j + 1], None,
                                            ALU.mult).then_inc(scaled, 1)

                def low(j):
                    h, t = items[j]
                    n, b, c0 = TILES[t][1], base(h), TILES[t][0]
                    v.wait_ge(outh, j + 1)
                    nc.vector.tensor_tensor(k.yal[b:b + 64, h // 2, c0:c0 + n], k.bank[4 + j % 2][b:b + 64, 0:n],
                                            k.yah[b:b + 64, h // 2, c0:c0 + n].bitcast(F32), ALU.subtract)\
                        .then_inc(outl, 1)

                for j in range(J + 4):
                    if j < J:
                        biases(j)
                    if 1 <= j <= J:
                        scale(j - 1)
                    if j >= 4:
                        low(j - 4)

            @block.scalar
            def _(a):
                def spread(h):
                    a.wait_ge(bias, h + 1)
                    if h >= 2:
                        a.wait_ge(biased, 5 * (h - 1))
                    nc.scalar.activation(ncb[:, h % 2, 0:PAST + NS], k.bank[6][:, 0:PAST + NS], ACT.Copy)
                    nc.scalar.activation(ncb[:, h % 2, PAST + NS:], k.bank[7][:], ACT.Copy).then_inc(biasc, 1)

                def exps(j):
                    h, t = items[j]
                    n, nk, blocks = sizes(t)
                    a.wait_ge(biased, j + 1)
                    if j >= 3:
                        a.wait_ge(turned, j - 2)
                    nc.scalar.activation(pr[0:n, j % 3, 0:nk], sc[0:n, j % 2, 0:nk], ACT.Exp, bias=st[0:n, 1, j:j + 1],
                                         accum_out=st[0:n, 2, j:j + 1]).then_inc(probs, 1)

                def copy(j):
                    h, t = items[j]
                    n, nk, blocks = sizes(t)
                    a.wait_ge(turned, j + 1)
                    if j >= 2:
                        a.wait_ge(out, j - 1)
                    if t == 0:
                        nc.scalar.activation(pT[:, j % 2, 0:n], k.bank[2 + j % 2][:, 0:n], ACT.Copy)
                        last = nc.scalar.activation(pT[0:NS, j % 2, n:2 * n], k.bank[2 + j % 2][0:NS, n:2 * n], ACT.Copy)
                    else:
                        last = nc.scalar.activation(pT[:, j % 2, 0:nk], k.bank[2 + j % 2][:, 0:nk], ACT.Copy)
                    last.then_inc(turnedc, 1)

                def high(j):
                    h, t = items[j]
                    n, b, c0 = TILES[t][1], base(h), TILES[t][0]
                    a.wait_ge(out, j + 1)
                    nc.scalar.activation(k.yah[b:b + 64, h // 2, c0:c0 + n], k.bank[4 + j % 2][b:b + 64, 0:n], ACT.Copy)\
                        .then_inc(outh, 1)

                for j in range(J + 4):
                    if j < J:
                        if items[j][1] == 0:
                            spread(items[j][0])
                        exps(j)
                    if 2 <= j < J + 2:
                        copy(j - 2)
                    if j >= 4:
                        high(j - 4)


def gated_sum(k):
    nc = k.nc
    mh, ml = k.mh, k.ml
    with ExitStack() as ctx:
        gate = k.sb("m_gate", [128, 2, NT], F32, ctx)
        part = k.sb("m_part", [128, 2, NT], F32, ctx)
        cols = lambda name, c: k.i[name][0].rearrange("(k p) n -> p k n", p=128)[:, :, 128 * c:128 * c + 128]
        chunks = []
        for c in range(KD):
            chunks += [([(0, w_in_cols(k, C_GA + 128 * c))], KD, k.xhi, k.xlo), ([(0, cols("w_br_a", c))], 4, k.yah, k.yal),
                       ([(0, w_in_cols(k, C_GB + 128 * c))], KD, k.xhi, k.xlo), ([(0, cols("w_br_b", c))], KD, k.ybh, k.ybl)]
        n = len(chunks)
        s = Stream(k, "mg", chunks, ctx, [1 if c % 2 == 0 else 0 for c in range(n)])
        sumd, high, low = (k.sem("m_" + x) for x in ("sum", "high", "low"))
        with nc.Block() as block:
            @block.sync
            def _(sp):
                for c in range(n):
                    s.load(sp, c)

            @block.gpsimd
            def _(g):
                for c in range(n):
                    s.split_lo(g, c)

            @block.tensor
            def _(pe):
                for c in range(n):
                    s.product(pe, c)

            @block.scalar
            def _(a):
                def high_part(j):
                    a.wait_ge(sumd, j + 1)
                    nc.scalar.activation(mh[:, j, :], part[:, 0, :], ACT.Copy).then_inc(high, 1)

                for c in range(LEAD):
                    s.split_hi(a, c)
                for c in range(n):
                    if c + LEAD < n:
                        s.split_hi(a, c + LEAD)
                    if c % 2 == 0:
                        if c >= 4:
                            s.wait_emptied(a, c - 3, 1)
                        for h in range(2):
                            a.wait_ge(s.half, 2 * c + h + 1)
                            nc.scalar.activation(gate[:, c // 2 % 2, h * HALF:(h + 1) * HALF], s.bank(c, h)[:, 0:HALF],
                                                 ACT.Sigmoid, bias=k.bgate[:, (c // 4) + 8 * (c // 2 % 2):][:, 0:1])\
                                .then_inc(s.emptied_of(c), 1)
                    if c >= 4 and c % 4 == 0:
                        high_part(c // 4 - 1)
                high_part(KD - 1)

            @block.vector
            def _(v):
                for c in range(1, n, 2):
                    if c % 4 == 1 and c > 1:
                        v.wait_ge(low, c // 4)
                    s.wait_emptied(v, c - 1, 1)
                    for h in range(2):
                        f = slice(h * HALF, (h + 1) * HALF)
                        v.wait_ge(s.half, 2 * c + h + 1)
                        nc.vector.tensor_tensor(part[:, c // 2 % 2, f], s.bank(c, h)[:, 0:HALF], gate[:, c // 2 % 2, f],
                                                ALU.mult).then_inc(s.emptied_of(c), 1)
                    if c % 4 == 3:
                        s.wait_emptied(v, c, 1)
                        nc.vector.tensor_tensor(part[:, 0, :], part[:, 0, :], part[:, 1, :], ALU.add).then_inc(sumd, 1)
                        v.wait_ge(high, c // 4 + 1)
                        nc.vector.tensor_tensor(ml[:, c // 4, :], part[:, 0, :], mh[:, c // 4, :].bitcast(F32),
                                                ALU.subtract).then_inc(low, 1)


def project_out(k):
    nc = k.nc
    mh, ml = k.mh, k.ml
    with ExitStack() as ctx:
        raw = k.sb("o_raw", [128, 4, 512], F32, ctx)
        whi = k.sb("o_hi", [128, 3, 512], F32R, ctx)
        wlo = k.sb("o_lo", [128, 3, 512], F32R, ctx)
        loaded = [k.sem(f"o_loaded{s}") for s in range(4)]
        hi, lo, used, done, added = (k.sem("o_" + n) for n in ("hi", "lo", "used", "done", "added"))
        n = 2 * KD
        bank = lambda a, t: k.bank[(5 * a + t) % 8]
        with nc.Block() as block:
            @block.sync
            def _(sp):
                for j in range(n):
                    if j >= 4:
                        sp.wait_ge(lo, j - 3)
                    sp.dma_start(raw[:, j % 4, :], k.i["w_out"][0, 128 * (j % KD):128 * (j % KD) + 128,
                                                               512 * (j // KD):512 * (j // KD) + 512])\
                        .then_inc(loaded[j % 4], 16)
                    if j == 3:
                        load_router(k, sp)
                    e = (j - 4) // 6
                    if j in (5, 11):
                        load_up(k, sp, e, e)
                    elif j in (8, 14):
                        load_down(k, sp, e, e)

            @block.gpsimd
            def _(g):
                for j in range(n):
                    g.wait_ge(hi, j + 1)
                    nc.gpsimd.tensor_tensor(wlo[:, j % 3, :], raw[:, j % 4, :], whi[:, j % 3, :].bitcast(F32),
                                            ALU.subtract).then_inc(lo, 1)

            @block.scalar
            def _(a):
                for j in range(n):
                    a.wait_ge(loaded[j % 4], 16 * (j // 4 + 1))
                    if j >= 3:
                        a.wait_ge(used, j - 2)
                    nc.scalar.activation(whi[:, j % 3, :], raw[:, j % 4, :], ACT.Copy).then_inc(hi, 1)

            @block.tensor
            def _(pe):
                for j in range(n):
                    a, d = j // KD, j % KD
                    pe.wait_ge(lo, j + 1)
                    for t, (c0, _) in enumerate(TILES):
                        if a == 1 and d == 0 and t >= 3:
                            pe.wait_ge(added, t - 2)
                        for i, (x, w) in enumerate(((mh, whi), (mh, wlo), (ml, whi))):
                            last = nc.tensor.matmul(bank(a, t)[:], x[:, d, c0:c0 + 128], w[:, j % 3, :],
                                                    start=(d == 0 and i == 0), stop=(d == KD - 1 and i == 2))
                        if d == KD - 1 and t < 4:
                            last.then_inc(done, 1)
                    last.then_inc(used, 1)

            @block.vector
            def _(v):
                for a in range(2):
                    for t, (_, rows) in enumerate(TILES):
                        if t < 4:
                            v.wait_ge(done, 4 * a + t + 1)
                        else:
                            v.wait_ge(used, KD * (a + 1))
                        f = slice(512 * a, 512 * a + 512)
                        nc.vector.tensor_tensor(k.x[0:rows, t, f], k.x[0:rows, t, f], bank(a, t)[0:rows, :], ALU.add)\
                            .then_inc(added, 1)


def expert_tensors(k):
    nc, ctx = k.nc, k.experts
    sem = lambda name: k.sem(name, ctx)
    k.w1 = k.sb("e_w1", [128, 2, KD, FE], F32, k.rings)
    k.w3 = k.sb("e_w3", [128, 2, KD, FE], F32, k.rings)
    k.w2 = k.sb("e_w2", [128, 2, FE // 128, D], F32, k.rings)
    k.up_loaded = [sem(f"up_loaded{s}") for s in range(2)]
    k.down_loaded = [sem(f"down_loaded{s}") for s in range(2)]
    k.router_loaded = sem("router_loaded")
    k.idx = k.sb("slot_token", [SLOTS, NB], I32, ctx)
    k.eid = k.sb("more_expert", [1, MORE], I32, ctx)
    k.nmore = k.sb("more_blocks", [1, 1], I32, ctx)
    k.row = k.sb("token_slot", [128, 5, 2], I32, ctx)
    k.wt = k.sb("token_weight", [128, 5, 2], F32, ctx)
    k.lg = k.sb("logits", [128, 5, GROUPS + NE], F32, k.routing)
    k.gain = k.sb("g_ffn_rows", [128, D], F32, k.routing)
    k.wr = k.sb("w_router", [128, KD, GROUPS + NE], F32, k.routing)
    k.br = k.sb("b_router", [128, GROUPS + NE], F32, k.routing)


def load_router(k, sp):
    with k.nc.allow_non_contiguous_dma(reason="router columns"):
        for dst, src in ((k.gain[:], k.i["g_ffn"].broadcast_to([128, D])),
                         (k.wr[:, :, 0:GROUPS], k.i["w_grp"][0].rearrange("(k p) n -> p k n", p=128)),
                         (k.wr[:, :, GROUPS:], k.i["w_exp"][0].rearrange("(k p) n -> p k n", p=128)),
                         (k.br[:, 0:GROUPS], k.i["b_grp"].broadcast_to([128, GROUPS])),
                         (k.br[:, GROUPS:], k.i["b_exp"].broadcast_to([128, NE]))):
            sp.dma_start(dst, src).then_inc(k.router_loaded, 16)


def load_up(k, sp, e, slot):
    for w, src in ((k.w1, k.i["w_e1"]), (k.w3, k.i["w_e3"])):
        src = src[0, e] if isinstance(e, int) else src[0, bass.ds(e, 1)].rearrange("o r n -> (o r) n")
        sp.dma_start(w[:, slot], src.rearrange("(k p) n -> p k n", p=128)).then_inc(k.up_loaded[slot], 16)


def load_down(k, sp, e, slot):
    src = k.i["w_e2"]
    src = src[0, e] if isinstance(e, int) else src[0, bass.ds(e, 1)].rearrange("o r n -> (o r) n")
    sp.dma_start(k.w2[:, slot], src.rearrange("(k p) n -> p k n", p=128)).then_inc(k.down_loaded[slot], 16)


def normalise_rows(k):
    nc = k.nc
    ctx = k.routing
    NL = GROUPS + NE
    junk = k.sb("r_sq", [128, D], F32, ctx)
    stat = k.sb("r_stat", [128, 3, 5], F32, ctx)
    xn = k.sb("r_xn", [128, 2, D], F32, ctx)
    xT = k.sb("r_xT", [128, 2, KD, 128], F32, ctx)
    rms, normed, moved, turned, scored, biased = (k.sem("r_" + n) for n in
                                                  ("rms", "normed", "moved", "turned", "scored", "biased"))
    stored = [k.sem(f"r_stored{s}") for s in range(2)]
    with nc.Block() as block:
        @block.sync
        def _(sp):
            for t, (c0, n) in enumerate(TILES):
                sp.wait_ge(normed, t + 1)
                sp.dma_start(k.table[c0:c0 + n, :], xn[0:n, t % 2, :]).then_inc(stored[t % 2], 16)
            sp.wait_ge(stored[0], 48)
            sp.wait_ge(stored[1], 32)

        @block.scalar
        def _(a):
            c = k.chain(a, "scalar")
            for t, (c0, n) in enumerate(TILES):
                c(nc.scalar.activation(junk[0:n, :], k.x[0:n, t, :], ACT.Square, accum_out=stat[0:n, 0, t:t + 1]))
            for t, (c0, n) in enumerate(TILES):
                nc.scalar.activation(stat[0:n, 1, t:t + 1], stat[0:n, 0, t:t + 1], ACT.Sqrt, bias=k.eps[0:n, :],
                                     scale=1.0 / D).then_inc(rms, 1)
            for t, (c0, n) in enumerate(TILES):
                a.wait_ge(moved, t + 1)
                if t >= 2:
                    a.wait_ge(scored, t - 1)
                for b in range(2):
                    nc.scalar.activation(xT[:, t % 2, 4 * b:4 * b + 4, 0:n],
                                         k.bank[2 * (t % 2) + b][:, 0:4 * n].rearrange("p (k n) -> p k n", k=4),
                                         ACT.Copy).then_inc(turned, 1)

        @block.vector
        def _(v):
            c = k.chain(v, "vector")
            c(nc.vector.memset(k.lg[:], 0.0))
            v.wait_ge(k.router_loaded, 80)
            for t, (c0, n) in enumerate(TILES):
                v.wait_ge(rms, t + 1)
                c(nc.vector.reciprocal(stat[0:n, 2, t:t + 1], stat[0:n, 1, t:t + 1]))
                if t >= 2:
                    v.wait_ge(moved, t - 1)
                    v.wait_ge(stored[t % 2], 16 * (t // 2))
                nc.vector.scalar_tensor_tensor(out=xn[0:n, t % 2, :], in0=k.x[0:n, t, :], scalar=stat[0:n, 2, t:t + 1],
                                               in1=k.gain[0:n, :], op0=ALU.mult, op1=ALU.mult).then_inc(normed, 1)
            for t, (c0, n) in enumerate(TILES):
                v.wait_ge(scored, t + 1)
                nc.vector.tensor_tensor(k.lg[0:n, t, :], k.bank[4 + t % 2][0:n, 0:NL], k.br[0:n, :], ALU.add)\
                    .then_inc(biased, 1)

        def score(pe, t):
            n = TILES[t][1]
            pe.wait_ge(turned, 2 * (t + 1))
            if t >= 2:
                pe.wait_ge(biased, t - 1)
            for d in range(KD):
                last = nc.tensor.matmul(k.bank[4 + t % 2][0:n, 0:NL], xT[:, t % 2, d, 0:n], k.wr[:, d, :],
                                        start=(d == 0), stop=(d == KD - 1))
            last.then_inc(scored, 1)

        @block.tensor
        def _(pe):
            pe.wait_ge(k.router_loaded, 80)
            for t, (c0, n) in enumerate(TILES):
                pe.wait_ge(normed, t + 1)
                if t >= 2:
                    pe.wait_ge(turned, 2 * (t - 1))
                for d in range(KD):
                    last = nc.tensor.transpose(k.bank[2 * (t % 2) + d // 4][:, (d % 4) * n:(d % 4) * n + n],
                                               xn[0:n, t % 2, 128 * d:128 * d + 128], k.ident[0:n, 0:n])
                last.then_inc(moved, 1)
                if t >= 1:
                    score(pe, t - 1)
            score(pe, 4)


def choose_experts(k):
    nc = k.nc
    ctx = k.routing
    V = nc.vector
    T = lambda name, *dims, dt=F32, p=128: k.sb("c_" + name, [p] + list(dims), dt, ctx)
    iN = T("iota_i", max(NB, SLOTS), dt=I32)
    iota = T("iota", max(NB, SLOTS))
    token_i, token, valid = T("token_i", 5, dt=I32), T("token", 5), T("valid", 5)
    g8, gm, gi, gf = T("g8", 5, 8), T("gmax", 5, 8), T("gidx", 5, 8, dt=U32), T("gsel", 5)
    goh, gd, ge, gs = T("goh", 5, GROUPS), T("gdiff", 5, GROUPS), T("gexp", 5, GROUPS), T("gsum", 5)
    em, em8, ei, ef = T("em", 5, NE), T("emax", 5, 8), T("eidx", 5, 8, dt=U32), T("esel", 5, 2)
    e2, wa = T("e2", 5), T("wa", 5)
    oh, both, pre, tmp = T("oh", 2, 5, NE), T("both", 5, NE), T("pre", 5, NE), T("tmp", 2, 5, NE)
    tot, ov, oi, ob = T("tot", NE), T("over", NE), T("cum", 2, NE), T("before", NE)
    run = T("run", 6, NE)
    rank, obr, q, s, blk, pos = T("rank", 2, 5), T("obr", 2, 5), T("q", 2, 5), T("s", 2, 5), T("blk", 2, 5), T("pos", 2, 5)
    more = T("more", 2, 5)
    cmpj, ejf = T("cmpj", MORE, NE), T("ejf", MORE)
    r1, b1 = T("rank_oh", 10, SLOTS), T("blk_oh", 10, NB)
    made, diffs, exps, chosen, counted, coded, listed = (k.sem("c_" + n) for n in
                                                        ("made", "diffs", "exps", "chosen", "counted", "coded", "listed"))
    further = -(-NT // SLOTS)
    with nc.Block() as block:
        @block.gpsimd
        def _(g):
            g.iota(iN[:], pattern=[[1, max(NB, SLOTS)]], base=0, channel_multiplier=0).then_inc(made, 1)
            g.iota(token_i[:], pattern=[[128, 5]], base=NS - 128, channel_multiplier=1).then_inc(made, 1)
            g.wait_ge(made, 2)
            g.iota(token_i[:, 0:1], pattern=[[0, 1]], base=0, channel_multiplier=1).then_inc(made, 1)

        @block.scalar
        def _(a):
            a.wait_ge(diffs, 2)
            nc.scalar.activation(ge[:], gd[:], ACT.Exp).then_inc(exps, 1)
            nc.scalar.activation(e2[:], e2[:], ACT.Exp).then_inc(exps, 1)

        @block.tensor
        def _(pe):
            pe.wait_ge(chosen, 1)
            nc.tensor.matmul(k.bank[0][:, 0:5 * NE], k.striu[:], both[:].rearrange("p t e -> p (t e)"), start=True, stop=False)
            nc.tensor.matmul(k.bank[0][:, 0:5 * NE], k.ones[:], run[:, 0:5].rearrange("p t e -> p (t e)"), start=False, stop=True)
            nc.tensor.matmul(k.bank[1][:, 0:NE], k.ones[:], run[:, 5, :], start=True, stop=True).then_inc(counted, 1)
            pe.wait_ge(coded, 1)
            for j in range(10):
                last = nc.tensor.matmul(k.bank[2][0:SLOTS, 0:NB], r1[:, j, :], b1[:, j, :], start=(j == 0), stop=(j == 9))
            last.then_inc(listed, 1)

        @block.vector
        def _(v):
            c = k.chain(v, "vector")
            bc = lambda ap, n: ap.unsqueeze(2).broadcast_to([128, 5, n])
            c(V.memset(valid[:], 1.0))
            c(V.memset(valid[:, 0:1], 0.0))
            c(V.memset(valid[0:NS, 0:1], 1.0))
            c(V.memset(g8[:], NEG))
            v.wait_ge(made, 3)
            c(V.tensor_copy(iota[:], iN[:]))
            c(V.tensor_copy(token[:], token_i[:]))
            c(V.tensor_copy(g8[:, :, 0:GROUPS], k.lg[:, :, 0:GROUPS]))
            for t in range(5):
                c(V.max(out=gm[:, t, :], in_=g8[:, t, :]))
                c(V.max_index(out=gi[:, t, :], in_max=gm[:, t, :], in_values=g8[:, t, :]))
            c(V.tensor_copy(gf[:], gi[:, :, 0]))
            V.tensor_tensor(gd[:], k.lg[:, :, 0:GROUPS], bc(gm[:, :, 0], GROUPS), ALU.subtract).then_inc(diffs, 1)
            c(V.tensor_tensor(goh[:], iota[:, 0:GROUPS].unsqueeze(1).broadcast_to([128, 5, GROUPS]), bc(gf[:], GROUPS),
                              ALU.is_equal))
            c(V.tensor_scalar(goh[:], goh[:], -NEG, NEG, ALU.mult, ALU.add))
            c(V.tensor_tensor(em[:].rearrange("p t (g e) -> p t g e", g=GROUPS),
                              k.lg[:, :, GROUPS:].rearrange("p t (g e) -> p t g e", g=GROUPS),
                              goh[:].unsqueeze(3).broadcast_to([128, 5, GROUPS, PER_GROUP]), ALU.add))
            for t in range(5):
                c(V.max(out=em8[:, t, :], in_=em[:, t, :]))
                c(V.max_index(out=ei[:, t, :], in_max=em8[:, t, :], in_values=em[:, t, :]))
            V.tensor_tensor(e2[:], em8[:, :, 1], em8[:, :, 0], ALU.subtract).then_inc(diffs, 1)
            c(V.tensor_copy(ef[:], ei[:, :, 0:2]))
            for j in range(2):
                c(V.tensor_tensor(oh[:, j], iota[:, 0:NE].unsqueeze(1).broadcast_to([128, 5, NE]), bc(ef[:, :, j], NE),
                                  ALU.is_equal))
                c(V.tensor_tensor(oh[:, j], oh[:, j], bc(valid[:], NE), ALU.mult))
            c(V.tensor_tensor(both[:], oh[:, 0], oh[:, 1], ALU.add))
            c(V.memset(run[:, 0, :], 0.0))
            for t in range(5):
                op = V.tensor_tensor(run[:, t + 1, :], run[:, t, :], both[:, t, :], ALU.add)
                if t < 4:
                    c(op)
            op.then_inc(chosen, 1)
            v.wait_ge(exps, 2)
            c(V.tensor_reduce(gs[:], ge[:], AX.X, ALU.add))
            c(V.tensor_scalar(wa[:], e2[:], 1.0, None, ALU.add))
            c(V.tensor_tensor(gs[:], gs[:], wa[:], ALU.mult))
            c(V.reciprocal(k.wt[:, :, 0], gs[:]))
            c(V.tensor_tensor(k.wt[:, :, 1], k.wt[:, :, 0], e2[:], ALU.mult))
            v.wait_ge(counted, 1)
            c(V.tensor_copy(pre[:].rearrange("p t e -> p (t e)"), k.bank[0][:, 0:5 * NE]))
            c(V.tensor_copy(tot[:], k.bank[1][:, 0:NE]))
            c(V.memset(ov[:], 0.0))
            for m in range(1, further):
                c(V.scalar_tensor_tensor(out=ov[:], in0=tot[:], scalar=SLOTS * m + 0.5, in1=ov[:], op0=ALU.is_gt,
                                         op1=ALU.add))
            c(V.tensor_copy(oi[:, 0], ov[:]))
            cur, step = 0, 1
            while step < NE:
                c(V.tensor_copy(oi[:, 1 - cur, 0:step], oi[:, cur, 0:step]))
                c(V.tensor_tensor(oi[:, 1 - cur, step:], oi[:, cur, step:], oi[:, cur, 0:NE - step], ALU.add))
                cur, step = 1 - cur, 2 * step
            c(V.tensor_tensor(ob[:], oi[:, cur], ov[:], ALU.subtract))
            c(V.tensor_tensor(tmp[:], oh[:], pre[:].unsqueeze(1).broadcast_to([128, 2, 5, NE]), ALU.mult))
            c(V.tensor_reduce(rank[:], tmp[:], AX.X, ALU.add))
            c(V.tensor_tensor(tmp[:].rearrange("p j t e -> p (j t) e"), oh[:].rearrange("p j t e -> p (j t) e"),
                              ob[:].unsqueeze(1).broadcast_to([128, 10, NE]), ALU.mult))
            c(V.tensor_reduce(obr[:], tmp[:], AX.X, ALU.add))
            c(V.memset(q[:], 0.0))
            for m in range(1, further):
                c(V.scalar_tensor_tensor(out=q[:], in0=rank[:], scalar=SLOTS * m - 0.5, in1=q[:], op0=ALU.is_gt,
                                         op1=ALU.add))
            c(V.scalar_tensor_tensor(out=s[:], in0=q[:], scalar=-float(SLOTS), in1=rank[:], op0=ALU.mult, op1=ALU.add))
            c(V.scalar_tensor_tensor(out=blk[:], in0=q[:], scalar=NE - 1.0, in1=obr[:], op0=ALU.add, op1=ALU.add))
            c(V.tensor_scalar(more[:], q[:], 0.5, None, ALU.is_gt))
            est = ef[:].rearrange("p t j -> p j t")
            c(V.tensor_tensor(blk[:], blk[:], est, ALU.subtract))
            c(V.tensor_tensor(blk[:], blk[:], more[:], ALU.mult))
            c(V.tensor_tensor(blk[:], blk[:], est, ALU.add))
            c(V.scalar_tensor_tensor(out=pos[:], in0=blk[:], scalar=float(SLOTS), in1=s[:], op0=ALU.mult, op1=ALU.add))
            c(V.tensor_copy(k.row[:].rearrange("p t j -> p j t"), pos[:]))
            c(V.tensor_scalar(token[:], token[:], float(NT), None, ALU.subtract))
            c(V.tensor_tensor(token[:], token[:], valid[:], ALU.mult))
            for j in range(2):
                for t in range(5):
                    V.tensor_scalar(r1[:, 5 * j + t, :], iota[:, 0:SLOTS], s[:, j, t:t + 1], None, ALU.is_equal)
                    last = V.tensor_scalar(b1[:, 5 * j + t, :], iota[:, 0:NB], blk[:, j, t:t + 1], token[:, t:t + 1],
                                           ALU.is_equal, ALU.mult)
            last.then_inc(coded, 1)
            c(V.tensor_tensor(cmpj[:], oi[:, cur].unsqueeze(1).broadcast_to([128, MORE, NE]),
                              iota[:, 0:MORE].unsqueeze(2).broadcast_to([128, MORE, NE]), ALU.is_le))
            c(V.tensor_reduce(ejf[:], cmpj[:], AX.X, ALU.add))
            c(V.tensor_copy(k.eid[:], ejf[0:1, :]))
            c(V.tensor_copy(k.nmore[:], oi[0:1, cur, NE - 1:NE]))
            v.wait_ge(listed, 1)
            c(V.tensor_scalar(k.idx[:], k.bank[2][0:SLOTS, 0:NB], float(NT), None, ALU.add))


def expert_blocks(k):
    nc = k.nc
    FH, NF = FE // 2, FE // 128
    with ExitStack() as ctx:
        at = k.sb("b_index", [SLOTS, 2], I32, ctx)
        spare = k.sb("b_spare", [SLOTS, 2], F32, ctx)
        xg = k.sb("b_rows", [SLOTS, 2, D], F32, ctx)
        xT = k.sb("b_xT", [128, KD, SLOTS], F32, ctx)
        act = k.sb("b_silu", [128, FH], F32, ctx)
        hm = k.sb("b_hidden", [128, FH], F32, ctx)
        hT = k.sb("b_hiddenT", [128, 2, 128], F32, ctx)
        y = k.sb("b_y", [128, 2, D // 2], F32, ctx)
        names = ("index", "turned", "copied", "up", "silu", "hidden", "hturned", "hcopied", "down", "out")
        index, turned, copied, up, silu, hidden, hturned, hcopied, down, out = (k.sem("b_" + n) for n in names)
        gathered = k.gathered
        stored = [k.sem(f"b_stored{s}") for s in range(2)]
        lo, hi = slice(0, 64), slice(64, 128)
        sl = (lo, hi)

        def wait(eng, sem, value):
            if not isinstance(value, int) or value > 0:
                eng.wait_ge(sem, value)

        def fetch(g, b, slot, n, prev):
            wait(g, turned, prev + 1)
            nc.gpsimd.tensor_copy(at[:, slot:slot + 1], k.idx[:, bass.ds(b, 1)]).then_inc(index, 1)
            g.wait_ge(index, b + 1)
            nc.gpsimd.tensor_tensor(spare[:, 0:1], k.one[0:SLOTS, :], k.one[0:SLOTS, :], ALU.add)
            g.indirect_dma_start(out=xg[:, slot, :], out_offset=None, in_=k.table,
                                 in_offset=bass.IndirectOffsetOnAxis(ap=at[:, slot:slot + 1], axis=0))\
                .then_inc(gathered[slot], 16)
            g.wait_ge(gathered[slot], 16 * n + 16)

        def products(pe, b, slot, n, prev):
            pe.wait_ge(gathered[slot], 16 * n + 16)
            wait(pe, copied, b)
            nc.tensor.matmul(k.bank[0][:, 0:64], xg[:, slot, 0:128], k.ident[0:64, 0:64], start=True, stop=True)
            for d in range(1, KD):
                last = nc.tensor.transpose(k.bank[0][:, 64 * d:64 * d + 64], xg[:, slot, 128 * d:128 * d + 128],
                                           k.ident[0:64, 0:64])
            last.then_inc(turned, 1)
            pe.wait_ge(copied, b + 1)
            pe.wait_ge(k.up_loaded[slot], 32 * n + 32)
            wait(pe, hidden, b)
            for d in range(KD):
                for bank, w in ((1, k.w1), (2, k.w3)):
                    for a in range(2):
                        last = nc.tensor.matmul(k.bank[bank][sl[a], 0:FH], xT[:, d, :], w[:, slot, d, FH * a:FH * a + FH],
                                                start=(d == 0), stop=(d == KD - 1))
            last.then_inc(up, 1)
            pe.wait_ge(hidden, b + 1)
            for c in range(2):
                last = nc.tensor.transpose(k.bank[3][:, 128 * c:128 * c + 128], hm[:, 128 * c:128 * c + 128], k.ident[:])
            last.then_inc(hturned, 1)
            pe.wait_ge(hcopied, b + 1)
            pe.wait_ge(k.down_loaded[slot], 16 * n + 16)
            wait(pe, out, b)
            for f in range(NF):
                for a in range(2):
                    last = nc.tensor.matmul(k.bank[4][sl[a], :], hT[:, f % 2, sl[f // 2]],
                                            k.w2[:, slot, f, 512 * a:512 * a + 512], start=(f == 0), stop=(f == NF - 1))
            last.then_inc(down, 1)

        def scalar_part(a, b, slot, n, prev):
            a.wait_ge(up, b + 1)
            wait(a, hidden, b)
            nc.scalar.activation(act[:], k.bank[1][:, 0:FH], ACT.Silu).then_inc(silu, 1)
            a.wait_ge(down, b + 1)
            wait(a, stored[slot], 32 * n)
            nc.scalar.activation(y[:, slot, :], k.bank[4][:], ACT.Copy).then_inc(out, 1)
            a.wait_ge(out, b + 1)
            for h in range(2):
                a.dma_start(k.yblk[bass.ds(b * SLOTS, SLOTS), 512 * h:512 * h + 512], y[sl[h], slot, :])\
                    .then_inc(stored[slot], 16)

        def vector_part(v, b, slot, n, prev):
            v.wait_ge(turned, b + 1)
            wait(v, up, b)
            nc.vector.tensor_copy(xT[:].rearrange("p k s -> p (k s)"), k.bank[0][:]).then_inc(copied, 1)
            v.wait_ge(silu, b + 1)
            wait(v, hturned, b)
            nc.vector.tensor_tensor(hm[:], act[:], k.bank[2][:, 0:FH], ALU.mult).then_inc(hidden, 1)
            v.wait_ge(hturned, b + 1)
            wait(v, down, b)
            nc.vector.tensor_copy(hT[:].rearrange("p c s -> p (c s)"), k.bank[3][:, 0:256]).then_inc(hcopied, 1)

        def loads(sp, e, b, slot, prev):
            sp.wait_ge(up, prev + 1)
            load_up(k, sp, e, slot)
            sp.wait_ge(down, prev + 1)
            load_down(k, sp, e, slot)

        def run_blocks(eng, part):
            for s in range(2):
                part(eng, s, s, 0, s - 2)
            with eng.Fori(1, NE // 2) as i:
                for s in range(2):
                    part(eng, 2 * i + s, s, i, 2 * i + s - 2)
            n = eng.value_load(k.nmore[0:1, 0:1], min_val=0, max_val=MORE)
            with eng.If(n > 0):
                with eng.Fori(0, n) as j:
                    part(eng, j + NE, 0, j + NE // 2, j + NE - 1)
            return n

        with nc.Block() as block:
            @block.sync
            def _(sp):
                with sp.Fori(1, NE // 2) as i:
                    for s in range(2):
                        b = 2 * i + s
                        loads(sp, b, b, s, b - 2)
                n = sp.value_load(k.nmore[0:1, 0:1], min_val=0, max_val=MORE)
                with sp.If(n > 0):
                    with sp.Fori(0, n) as j:
                        e = sp.value_load(k.eid[0:1, bass.ds(j, 1)], min_val=0, max_val=NE - 1)
                        loads(sp, e, j + NE, 0, j + NE - 1)

            @block.gpsimd
            def _(g):
                run_blocks(g, fetch)

            @block.tensor
            def _(pe):
                run_blocks(pe, products)

            @block.scalar
            def _(a):
                n = run_blocks(a, scalar_part)
                a.wait_ge(stored[1], 32 * (NE // 2))
                a.wait_ge(stored[0], n * 32 + 32 * (NE // 2))
                nc.scalar.activation(spare[:, 1:2], k.one[0:SLOTS, :], ACT.Copy)

            @block.vector
            def _(v):
                run_blocks(v, vector_part)


def combine(k):
    nc = k.nc
    with ExitStack() as ctx:
        rows = k.sb("y_rows", [128, 10, D], F32, ctx)
        idx = k.sb("y_index", [128, 10], I32, ctx)
        ready = k.sem("y_ready")
        got = k.got
        added, stored = k.sem("y_added"), k.sem("y_stored")
        with nc.Block() as block:
            @block.gpsimd
            def _(g):
                nc.gpsimd.tensor_copy(idx[:], k.row[:].rearrange("p t j -> p (t j)")).then_inc(ready, 1)
                g.wait_ge(ready, 1)
                for m in range(10):
                    n = TILES[m // 2][1]
                    g.indirect_dma_start(out=rows[0:n, m, :], out_offset=None, in_=k.yblk,
                                         in_offset=bass.IndirectOffsetOnAxis(ap=idx[0:n, m:m + 1], axis=0))\
                        .then_inc(got[m], 16)
                for m in range(10):
                    g.wait_ge(got[m], 16)

            @block.vector
            def _(v):
                for m in range(10):
                    t, j = m // 2, m % 2
                    n = TILES[t][1]
                    v.wait_ge(got[m], 16)
                    if j:
                        v.wait_ge(added, m)
                    nc.vector.scalar_tensor_tensor(out=k.x[0:n, t, :], in0=rows[0:n, m, :],
                                                   scalar=k.wt[0:n, t, j:j + 1], in1=k.x[0:n, t, :],
                                                   op0=ALU.mult, op1=ALU.add).then_inc(added, 1)

            @block.sync
            def _(sp):
                for t, (c0, n) in enumerate(TILES):
                    sp.wait_ge(added, 2 * t + 2)
                    dst = k.o["y_s"][0] if t == 0 else k.o["y_p"][0, 128 * (t - 1):128 * t, :]
                    sp.dma_start(dst, k.x[0:n, t, :]).then_inc(stored, 16)
                sp.wait_ge(stored, 80)


_INS = ["x_prompt", "x_sample", "cache_fox_k", "cache_fox_v", "cache_fox_logf", "state_gdn", "state_gdn_conv", "g_mix",
        "w_in", "b_f", "g_qnorm", "g_knorm", "w_conv", "a_log", "dt_bias", "g_onorm", "b_gate", "w_br_a", "w_br_b",
        "w_out", "g_ffn", "w_grp", "b_grp", "w_exp", "b_exp", "w_e1", "w_e3", "w_e2"]
_OUTS = {"y_p": (1, NP, D), "y_s": (1, NS, D)}
for _s, _n in (("p", NP), ("s", NS)):
    _OUTS.update({"k_" + _s: (1, 1, _n, H, DH), "v_" + _s: (1, 1, _n, H, DH), "logf_" + _s: (1, 1, _n, H),
                  "state_" + _s: (1, 1, H, DH, DV), "conv_" + _s: (1, 1, CONV_W - 1, CONV_CH)})


def kernel(**inputs):
    import numpy as _np
    import concourse.bacc as _bacc
    from concourse.bass_utils import run_bass_kernel_spmd as _run

    nc = _bacc.Bacc("TRN2", target_bir_lowering=False, num_devices=1)
    arrays, ins, outs = {}, {}, {}
    for name in _INS:
        a = _np.ascontiguousarray(inputs[name])
        arrays["in_" + name] = a
        ins[name] = nc.dram_tensor("in_" + name, a.shape, F32, kind="ExternalInput").ap()
    for name, shape in _OUTS.items():
        outs[name] = nc.dram_tensor("out_" + name, shape, F32, kind="ExternalOutput").ap()
    build(nc, ins, outs)
    r = _run(nc, [arrays], core_ids=[0])
    return tuple(r.results[0]["out_" + name] for name in _OUTS)
```

```python
from contextlib import ExitStack

import concourse.bass as bass
from concourse import mybir

DT = mybir.dt
F32, F32R, I32, U32 = DT.float32, DT.float32r, DT.int32, DT.uint32
ALU = mybir.AluOpType
ACT = mybir.ActivationFunctionType
AX = mybir.AxisListType

D = 1024
KD = D // 128
NS, NP = 32, 512
NT = NS + NP
HALF = NT // 2
TILES = [(0, NS)] + [(NS + 128 * i, 128) for i in range(NP // 128)]
H, DH = 8, 64
DV = 128
PAST = 128
WA = H * DH
CONV_CH = 2 * H * DH + H * DV
CONV_W = 4
NCC = CONV_CH // 128
NE, GROUPS, PER_GROUP, FE = 32, 4, 8, 512
SLOTS = 64
MORE = (2 * NT - 1) // SLOTS
NB = NE + MORE
RING = 3
EPS = 1e-6
RAWS, OPS = 4, 3
LEAD = OPS - 1
NEG = -1e30
C_FQ, C_FK, C_FV = 0, WA, 2 * WA
C_LOGF = 3 * WA
C_CONV = C_LOGF + H
C_BETA = C_CONV + CONV_CH
C_DECAY = C_BETA + H
C_Z = C_DECAY + H
C_GA = C_Z + H * DV
C_GB = C_GA + D


class Marks:

    def __init__(self, sem, names):
        self.sem, self.at, self.made = sem, {n: i + 1 for i, n in enumerate(names)}, 0

    def mark(self, ins, name):
        self.made += 1
        assert self.at[name] == self.made, (name, self.at[name], self.made)
        return ins.then_inc(self.sem, 1)

    def wait(self, eng, name):
        eng.wait_ge(self.sem, self.at[name])


class Chain:

    def __init__(self, eng, sem, start=0):
        self.eng, self.sem, self.n = eng, sem, start

    def __call__(self, ins):
        self.n += 1
        ins.then_inc(self.sem, 1)
        self.eng.wait_ge(self.sem, self.n)


class Kernel:
    def __init__(self, nc, ins, outs):
        self.nc, self.i, self.o = nc, ins, outs
        self.top = ExitStack()
        self.live = []

    def sb(self, name, shape, dt=F32, ctx=None):
        size = 4
        for n in shape[1:]:
            size *= n
        size = -(-size // 32) * 32
        at = -(-self.nc.sbuf_base // 32) * 32
        for a, b in sorted(self.live):
            if at + size <= a:
                break
            at = max(at, b)
        assert at + size <= self.nc.sbuf_top, (name, size, sorted(self.live))
        span = (at, at + size)
        self.live.append(span)
        (ctx or self.top).callback(self.live.remove, span)
        return self.nc.alloc_sbuf_tensor_at(name, shape, dt, offset=at)

    def sem(self, name, ctx=None):
        s = self.nc.alloc_semaphore(name=name)
        if ctx is None:
            self.stage_sems.append(s)
        return s

    def run(self, part):
        self.stage_sems = []
        with ExitStack() as self.stage:
            part(self)
        self.nc.clear_and_free_semaphores(self.stage_sems)
        self.nc.all_engine_barrier()

    def marks(self, name, names):
        return Marks(self.sem(name), list(names))

    def chain(self, eng, which):
        c = self.chains.get(which)
        if c is None:
            c = self.chains[which] = Chain(eng, self.sem("own_" + which, self.top))
        c.eng = eng
        return c


def build(nc, ins, outs):
    k = Kernel(nc, ins, outs)
    k.chains = {}
    with k.top:
        for which in ("vector", "scalar"):
            k.chain(None, which)
        k.gathered = [k.sem(f"b_gathered{s}", k.top) for s in range(RING)]
        k.got = [k.sem(f"y_got{m}", k.top) for m in range(10)]
        k.late = k.sem("late_stores", k.top)
        k.bank = [k.top.enter_context(nc.psum_tensor(f"bank{b}", [128, 512], F32)) for b in range(8)]
        k.table = nc.dram_tensor("token_rows", [NT + 1, D], F32).ap()
        k.yblk = nc.dram_tensor("expert_rows", [NB * SLOTS, D], F32).ap()
        k.x = k.sb("x_rows", [128, 5, D])
        mix = k.top.enter_context(ExitStack())
        with ExitStack() as mixer:
            k.mixer = mixer
            mixer_tensors(k)
            conv_ctx = mixer.enter_context(ExitStack())
            k.conv_ctx = conv_ctx
            k.xor_ctx = conv_ctx.enter_context(ExitStack())
            with ExitStack() as k.stream_ctx:
                small = [(0, w_in_cols(k, C_LOGF, H)), (32, w_in_cols(k, C_BETA, H)), (64, w_in_cols(k, C_DECAY, H))]
                convolved = [[(0, w_in_cols(k, C_CONV + 128 * c))] for c in range(NCC)]
                k.first_stream = Stream(k, "cv", [(w, KD, k.xhi, k.xlo) for w in [small] + convolved], k.stream_ctx,
                                        [1] + [0] * NCC, sems=k.top)
                k.run(start)
                k.run(convolved_projections)
            k.xor_ctx.close()
            k.run(delta_net)
            conv_ctx.close()
            k.ybh = k.sb("yb_hi", [128, H, NT], F32R, mixer)
            k.ybl = k.sb("yb_lo", [128, H, NT], F32R, mixer)
            k.run(attention)
            k.mh = k.sb("mix_hi", [128, KD, NT], F32R, mix)
            k.ml = k.sb("mix_lo", [128, KD, NT], F32R, mix)
            k.run(gated_sum)
        with ExitStack() as k.experts, ExitStack() as k.rings, ExitStack() as k.routing:
            expert_tensors(k)
            k.run(project_out)
            mix.close()
            weight_slot(k)
            k.run(normalise_rows)
            k.run(choose_experts)
            k.routing.close()
            k.run(expert_blocks)
            k.rings.close()
            k.run(combine)


def start(k):
    nc, i = k.nc, k.i
    k.ident = k.sb("ident", [128, 128])
    k.ones = k.sb("ones", [128, 128])
    k.head_ones = k.sb("head_ones", [128, 128], F32, k.mixer)
    k.triu = k.sb("triu", [128, 512], F32, k.mixer)
    k.striu = k.sb("striu", [128, 128])
    k.later_neg = k.sb("later_neg", [128, 128], F32, k.mixer)
    k.causal_neg = k.sb("causal_neg", [128, 128], F32, k.mixer)
    k.level = k.sb("level", [128, 7, 128], F32, k.mixer)
    k.sel = k.sb("sel", [8, 8, 128], F32, k.mixer)
    k.selpair = k.sb("selpair", [8, 4, 128], F32, k.mixer)
    k.eps = k.sb("eps", [128, 1])
    k.one = k.sb("one", [128, 1])
    k.wconv = k.sb("wconv", [128, CONV_W, NCC], F32, k.mixer)
    k.hist = k.sb("hist", [128, 3, NCC], F32, k.mixer)
    k.gq = k.sb("gq", [128, 1], F32, k.mixer)
    k.gk = k.sb("gk", [128, 1], F32, k.mixer)
    k.go = k.sb("go", [128, 1], F32, k.mixer)
    k.bgate = k.sb("bgate", [128, 16], F32, k.mixer)
    k.lastT = k.sb("conv_lastT", [96, 128], F32, k.mixer)
    k.sm_bias = k.sb("sm_bias", [128, 1], F32, k.mixer)
    k.sm_sign = k.sb("sm_sign", [128, 1], F32, k.mixer)
    k.sm_coef = k.sb("sm_coef", [128, 1], F32, k.mixer)
    k.xi = k.sb("xor_i", [128, 128], I32, k.xor_ctx)
    k.xj = k.sb("xor_j", [128, 128], I32, k.xor_ctx)
    k.junk = k.sb("nt_sq", [128, D], F32, k.stage)
    stat = k.sb("nt_stat", [128, 3, 5], F32, k.stage)
    xn = k.sb("nt_xn", [128, 2, D], F32, k.stage)
    g_mix = k.sb("g_mix_rows", [128, D], F32, k.stage)
    junk, rt, rr = k.junk, stat[:, 1], stat[:, 2]
    filled, loaded, ints, done, early = (k.sem("const_" + n) for n in ("filled", "loaded", "ints", "done", "early"))
    x_loaded = [k.sem(f"x_loaded{t}") for t in range(5)]
    gain, zeroed = k.sem("nt_gain"), k.sem("nt_zeroed")
    rms = k.sem("nt_rms")
    normed = k.sem("nt_normed")
    moved = k.sem("nt_moved")
    hi_done = k.sem("nt_hi")
    lo_done = k.sem("nt_lo")
    with nc.Block() as block:
        @block.vector
        def _(v):
            c = k.chain(v, "vector")
            nc.vector.memset(k.eps[:], EPS)
            nc.vector.memset(k.ident[:], 0.0)
            nc.vector.memset(k.striu[:], 1.0).then_inc(early, 1)
            for t, val in ((k.sm_bias, 0.0), (k.sm_sign, 0.0), (k.sm_coef, 0.0), (k.ones, 1.0), (k.head_ones, 0.0),
                           (k.triu, 1.0), (k.later_neg, 0.0), (k.causal_neg, 0.0), (k.sel, 0.0), (k.selpair, 0.0),
                           (k.one, 1.0)):
                last = nc.vector.memset(t[tuple(slice(None) for _ in t.shape)], val)
            c(last)
            c(nc.vector.memset(k.head_ones[0:64, 0:64], 1.0))
            c(nc.vector.memset(k.head_ones[64:128, 64:128], 1.0))
            c(nc.vector.memset(k.sm_sign[0:8, :], -1.0))
            c(nc.vector.memset(k.sm_sign[32:40, :], -1.0))
            c(nc.vector.memset(k.sm_sign[64:72, :], 1.0))
            c(nc.vector.memset(k.sm_coef[0:40, :], -1.0))
            nc.vector.memset(k.sm_coef[64:72, :], -1.0).then_inc(filled, 1)

            def normalise(t):
                c0, n = TILES[t]
                v.wait_ge(rms, t + 1)
                c(nc.vector.reciprocal(rr[0:n, t:t + 1], rt[0:n, t:t + 1]))
                if t >= 2:
                    v.wait_ge(moved, t - 1)
                nc.vector.scalar_tensor_tensor(out=xn[0:n, t % 2, :], in0=k.x[0:n, t, :], scalar=rr[0:n, t:t + 1],
                                               in1=g_mix[0:n, :], op0=ALU.mult, op1=ALU.mult).then_inc(normed, 1)
            v.wait_ge(gain, 16)
            normalise(0)
            for t, (c0, n) in enumerate(TILES):
                if t + 1 < 5:
                    normalise(t + 1)
                for b in range(2):
                    v.wait_ge(hi_done, 2 * t + b + 1)
                    nc.vector.tensor_tensor(k.xlo[:, 4 * b:4 * b + 4, c0:c0 + n],
                                            k.bank[2 * (t % 2) + b][:, 0:4 * n].rearrange("p (k n) -> p k n", k=4),
                                            k.xhi[:, 4 * b:4 * b + 4, c0:c0 + n].bitcast(F32),
                                            ALU.subtract).then_inc(lo_done, 1)

        @block.gpsimd
        def _(g):
            g.wait_ge(early, 1)
            g.affine_select(out=k.ident[:], in_=k.ident[:], compare_op=ALU.not_equal, fill=1.0, base=0,
                            pattern=[[1, 128]], channel_multiplier=-1).then_inc(ints, 1)
            g.affine_select(out=k.striu[:], in_=k.striu[:], compare_op=ALU.is_gt, fill=0.0, base=0,
                            pattern=[[1, 128]], channel_multiplier=-1).then_inc(ints, 1)
            g.iota(k.xi[:], pattern=[[1, 128]], base=0, channel_multiplier=0).then_inc(ints, 1)
            g.iota(k.xj[:], pattern=[[0, 128]], base=0, channel_multiplier=1).then_inc(ints, 1)
            g.memset(k.raw[:, 0], 0.0).then_inc(zeroed, 1)
            g.wait_ge(filled, 1)
            g.affine_select(out=k.triu[:], in_=k.triu[:], compare_op=ALU.is_ge, fill=0.0, base=0,
                            pattern=[[1, 512]], channel_multiplier=-1).then_inc(done, 1)
            g.affine_select(out=k.later_neg[:], in_=k.later_neg[:], compare_op=ALU.is_ge, fill=NEG, base=0,
                            pattern=[[1, 128]], channel_multiplier=-1).then_inc(done, 1)
            g.affine_select(out=k.causal_neg[:], in_=k.causal_neg[:], compare_op=ALU.is_ge, fill=NEG, base=0,
                            pattern=[[-1, 128]], channel_multiplier=1).then_inc(done, 1)
            g.affine_select(out=k.sel[:], in_=k.sel[:], compare_op=ALU.not_equal, fill=1.0, base=0,
                            pattern=[[-1, 8], [0, 128]], channel_multiplier=1).then_inc(done, 1)
            g.affine_select(out=k.selpair[:].rearrange("r p (a m) -> r p a m", a=2),
                            in_=k.selpair[:].rearrange("r p (a m) -> r p a m", a=2),
                            compare_op=ALU.not_equal, fill=1.0, base=0,
                            pattern=[[-2, 4], [-1, 2], [0, 64]], channel_multiplier=1).then_inc(done, 1)
            g.wait_ge(ints, 4)
            g.wait_ge(done, 5)

        @block.sync
        def _(sp):
            for t, (c0, n) in enumerate(TILES):
                src = i["x_sample"][0] if t == 0 else i["x_prompt"][0, 128 * (t - 1):128 * t, :]
                sp.dma_start(k.x[0:n, t, :], src).then_inc(x_loaded[t], 16)
                if t == 0:
                    sp.dma_start(g_mix[:], i["g_mix"].broadcast_to([128, D])).then_inc(gain, 16)
            sp.wait_ge(filled, 1)
            with nc.allow_non_contiguous_dma(reason="small parameters"):
                loads = [
                    (k.gq[0:64, :], i["g_qnorm"].rearrange("o c -> c o")),
                    (k.gq[64:128, :], i["g_qnorm"].rearrange("o c -> c o")),
                    (k.gk[0:64, :], i["g_knorm"].rearrange("o c -> c o")),
                    (k.gk[64:128, :], i["g_knorm"].rearrange("o c -> c o")),
                    (k.go[:], i["g_onorm"].rearrange("o c -> c o")),
                    (k.bgate[:], i["b_gate"][0].rearrange("(c p) -> p c", p=128)),
                    (k.sm_bias[0:8, :], i["b_f"].rearrange("o c -> c o")),
                    (k.sm_bias[64:72, :], i["dt_bias"].rearrange("o c -> c o")),
                    (k.sm_coef[64:72, :], i["a_log"].rearrange("o c -> c o")),
                ]
                for w in range(CONV_W):
                    loads.append((k.wconv[:, w, :], i["w_conv"][0, w].rearrange("(c p) -> p c", p=128)))
                for w in range(3):
                    loads.append((k.hist[:, w, :], i["state_gdn_conv"][0, 0, w].rearrange("(c p) -> p c", p=128)))
                for dst, src in loads:
                    sp.dma_start(dst, src).then_inc(loaded, 16)
                sp.wait_ge(zeroed, 1)
                for j in range(RAWS):
                    k.first_stream.load(sp, j)
            sp.wait_ge(loaded, 16 * len(loads))

        @block.scalar
        def _(a):
            c = k.chain(a, "scalar")
            a.wait_ge(early, 1)
            for t, (c0, n) in enumerate(TILES):
                a.wait_ge(x_loaded[t], 16)
                c(nc.scalar.activation(junk[0:n, :], k.x[0:n, t, :], ACT.Square, accum_out=stat[0:n, 0, t:t + 1]))
                nc.scalar.activation(rt[0:n, t:t + 1], stat[0:n, 0, t:t + 1], ACT.Sqrt, bias=k.eps[0:n, :],
                                     scale=1.0 / D).then_inc(rms, 1)
            for t, (c0, n) in enumerate(TILES):
                a.wait_ge(moved, t + 1)
                for b in range(2):
                    nc.scalar.activation(k.xhi[:, 4 * b:4 * b + 4, c0:c0 + n],
                                         k.bank[2 * (t % 2) + b][:, 0:4 * n].rearrange("p (k n) -> p k n", k=4),
                                         ACT.Copy).then_inc(hi_done, 1)

        @block.tensor
        def _(pe):
            pe.wait_ge(ints, 1)
            for t, (c0, n) in enumerate(TILES):
                pe.wait_ge(normed, t + 1)
                if t >= 2:
                    pe.wait_ge(lo_done, 2 * (t - 1))
                for d in range(KD):
                    last = nc.tensor.transpose(k.bank[2 * (t % 2) + d // 4][:, (d % 4) * n:(d % 4) * n + n],
                                               xn[0:n, t % 2, 128 * d:128 * d + 128], k.ident[0:n, 0:n])
                last.then_inc(moved, 1)


def levels_of_inversion(k, v):
    nc = k.nc
    c = k.chain(v, "vector")
    c(nc.vector.tensor_tensor(k.xj[:], k.xi[:], k.xj[:], ALU.bitwise_xor))
    for l in range(7):
        c(nc.vector.tensor_scalar(k.xi[:], k.xj[:], l, None, ALU.logical_shift_right))
        c(nc.vector.tensor_scalar(k.level[:, l, :], k.xi[:], 1, None, ALU.is_equal))
    for l in range(7):
        c(nc.vector.tensor_tensor(k.level[:, l, :], k.level[:, l, :], k.striu[:], ALU.mult))


def mixer_tensors(k):
    ctx = k.mixer
    k.xhi = k.sb("xhi", [128, KD, NT], F32R, ctx)
    k.xlo = k.sb("xlo", [128, KD, NT], F32R, ctx)
    k.yb_ctx = ctx.enter_context(ExitStack())
    k.yb = k.sb("yb", [128, H, NT], F32, k.yb_ctx)
    k.smt = k.sb("small_rows", [128, 5, 96], F32, ctx)


class Stream:

    def __init__(self, k, name, chunks, ctx, emptier=None, raws=RAWS, sems=None):
        self.k, self.chunks, self.raws = k, chunks, raws
        k.raw = k.sb(name + "_w_raw", [128, raws, KD, 128], F32, ctx)
        k.whi = k.sb(name + "_w_hi", [128, OPS, KD, 128], F32R, ctx)
        k.wlo = k.sb(name + "_w_lo", [128, OPS, KD, 128], F32R, ctx)
        self.loaded = [k.sem(f"{name}_loaded{s}", sems) for s in range(raws)]
        self.hi = k.sem(name + "_hi", sems)
        self.lo = k.sem(name + "_lo", sems)
        self.half = k.sem(name + "_half", sems)
        self.emptier = emptier or [0] * len(chunks)
        self.emptied = [k.sem(f"{name}_emptied{e}", sems) for e in range(max(self.emptier) + 1)]

    def emptied_of(self, c):
        return self.emptied[self.emptier[c]]

    def bank(self, c, h):
        return self.k.bank[2 * (c % 2) + h]

    def wait_emptied(self, eng, c, h):
        before = sum(1 for j in range(c) if self.emptier[j] == self.emptier[c])
        eng.wait_ge(self.emptied_of(c), 2 * before + h + 1)

    def load(self, sp, c):
        k = self.k
        srcs, nk = self.chunks[c][0], self.chunks[c][1]
        if c >= self.raws:
            sp.wait_ge(self.lo, c - self.raws + 1)
        for dst0, src in srcs:
            w = src.shape[-1]
            sp.dma_start(k.raw[:, c % self.raws, 0:nk, dst0:dst0 + w], src).then_inc(self.loaded[c % self.raws], 16)

    def loads_of(self, c):
        return 16 * sum(len(self.chunks[j][0]) for j in range(c % self.raws, c + 1, self.raws))

    def split_hi(self, a, c):
        k, nk = self.k, self.chunks[c][1]
        a.wait_ge(self.loaded[c % self.raws], self.loads_of(c))
        if c >= OPS:
            a.wait_ge(self.half, 2 * (c - OPS + 1))
        k.nc.scalar.activation(k.whi[:, c % OPS, 0:nk, :], k.raw[:, c % self.raws, 0:nk, :], ACT.Copy).then_inc(self.hi, 1)

    def split_lo(self, g, c):
        k, nk = self.k, self.chunks[c][1]
        g.wait_ge(self.hi, c + 1)
        k.nc.gpsimd.tensor_tensor(k.wlo[:, c % OPS, 0:nk, :], k.raw[:, c % self.raws, 0:nk, :],
                                  k.whi[:, c % OPS, 0:nk, :].bitcast(F32), ALU.subtract).then_inc(self.lo, 1)

    def product(self, pe, c, halves=(0, 1)):
        k = self.k
        nk, xhi, xlo = self.chunks[c][1:]
        pe.wait_ge(self.lo, c + 1)
        for h in halves:
            if c >= 2:
                self.wait_emptied(pe, c - 2, h)
            cols = slice(h * HALF, (h + 1) * HALF)
            for d in range(nk):
                for n, (w, x) in enumerate(((k.whi, xhi), (k.whi, xlo), (k.wlo, xhi))):
                    last = k.nc.tensor.matmul(self.bank(c, h)[:, 0:HALF], w[:, c % OPS, d, :], x[:, d, cols],
                                              start=(d == 0 and n == 0), stop=(d == nk - 1 and n == 2))
            last.then_inc(self.half, 1)


def w_in_cols(k, c0, n=128):
    return k.i["w_in"][0].rearrange("(k p) n -> p k n", p=128)[:, :, c0:c0 + n]


def convolved_projections(k):
    nc = k.nc
    ctx = k.conv_ctx
    k.cT = k.sb("conv_out", [128, NCC, NT], F32, ctx)
    with ExitStack() as ctx:
        k.sT = k.sb("small_cols", [96, NT], F32, ctx)
        tmp = k.sb("small_tmp", [96, 2, NT], F32, ctx)
        cin = k.sb("conv_in", [128, 2, 3 + NS + 3 + NP], F32, ctx)
        acc = k.sb("conv_acc", [128, 2, 3 + NS + NP], F32, ctx)
        last3 = k.sb("conv_last", [128, 6, NCC], F32, ctx)
        lastT = k.lastT
        W = 3 + NS + NP
        s = k.first_stream
        summed = k.sem("cv_summed")
        act_done = k.sem("cv_silu")
        logged, rows, turned, copied = (k.sem("sm_" + n) for n in ("logged", "rows", "turned", "copied"))
        last_turned, last_copied = k.sem("cv_last_turned"), k.sem("cv_last_copied")
        kept = k.sem("cv_kept")

        norms = Norms(k, "l2", [(k.cT, c, DH ** -0.5 if c < 4 else 1.0, k.head_ones, 1.0,
                                 lambda g, c=c: g.wait_ge(act_done, c + 1)) for c in range(8)], ctx)
        group_at = {5: (0, 1), 7: (2, 3), 9: (4, 5), 11: (6, 7)}

        def silu(a, c):
            a.wait_ge(summed, c + 1)
            nc.scalar.activation(k.cT[:, c, 0:NS], acc[:, c % 2, 0:NS], ACT.Silu)
            nc.scalar.activation(k.cT[:, c, NS:NT], acc[:, c % 2, 3 + NS:W], ACT.Silu).then_inc(act_done, 1)

        with nc.Block() as block:
            @block.sync
            def _(sp):
                for j in range(RAWS, NCC + 1):
                    s.load(sp, j)
                sp.wait_ge(copied, 1)
                sp.dma_start(k.o["logf_s"][0, 0], k.smt[0:NS, 0, 0:H]).then_inc(k.late, 16)
                sp.dma_start(k.o["logf_p"][0, 0].rearrange("(t p) h -> p t h", p=128), k.smt[:, 1:5, 0:H])\
                    .then_inc(k.late, 16)
                sp.wait_ge(last_copied, 1)
                sp.dma_start(k.o["conv_s"][0, 0].rearrange("w (c m) -> (w c) m", m=128), lastT[0:48, :]).then_inc(k.late, 16)
                sp.dma_start(k.o["conv_p"][0, 0].rearrange("w (c m) -> (w c) m", m=128), lastT[48:96, :]).then_inc(k.late, 16)

            @block.gpsimd
            def _(g):
                s.split_lo(g, 0)
                for c in range(NCC):
                    s.split_lo(g, c + 1)
                    if 4 <= c < 12:
                        norms.square(g, c - 4)

            @block.tensor
            def _(pe):
                s.product(pe, 0)
                for c in range(NCC):
                    s.product(pe, c + 1)
                    if c == 3:
                        pe.wait_ge(rows, 1)
                        for t, (c0, n) in enumerate(TILES):
                            out = k.bank[5][0:NS, 0:96] if t == 0 else k.bank[4][:, 96 * (t - 1):96 * t]
                            last = nc.tensor.transpose(out, k.sT[:, c0:c0 + n], k.ident[0:96, 0:96])
                        last.then_inc(turned, 1)
                    if c in group_at:
                        pe.wait_ge(copied, 1)
                        norms.sums(pe, group_at[c])
                pe.wait_ge(norms.logged, 8)
                pe.wait_ge(kept, NCC)
                nc.tensor.transpose(k.bank[4][0:96, 0:128], last3[:].rearrange("p a c -> p (a c)"), k.ident[:, :])\
                    .then_inc(last_turned, 1)

            @block.scalar
            def _(a):
                c_ = k.chain(a, "scalar")
                for j in range(LEAD):
                    s.split_hi(a, j)
                c_(nc.scalar.activation(k.sm_coef[64:72, :], k.sm_coef[64:72, :], ACT.Exp))
                c_(nc.scalar.activation(k.sm_coef[64:72, :], k.sm_coef[64:72, :], ACT.Copy, scale=-1.0))
                c_(nc.scalar.activation(k.gq[:], k.gq[:], ACT.Copy, scale=DH ** -0.5))
                s.split_hi(a, LEAD)
                for c in range(NCC):
                    if c + 1 + LEAD <= NCC:
                        s.split_hi(a, c + 1 + LEAD)
                    if c >= 2:
                        a.wait_ge(summed, c - 1)
                        a.wait_ge(kept, c - 1)
                    a.wait_ge(s.half, 2 * c + 3)
                    nc.scalar.activation(cin[:, c % 2, 3:3 + NS], s.bank(c + 1, 0)[:, 0:NS], ACT.Copy)
                    nc.scalar.activation(cin[:, c % 2, 6 + NS:6 + HALF], s.bank(c + 1, 0)[:, NS:HALF], ACT.Copy)\
                        .then_inc(s.emptied_of(c + 1), 1)
                    a.wait_ge(s.half, 2 * c + 4)
                    nc.scalar.activation(cin[:, c % 2, 6 + HALF:6 + NT], s.bank(c + 1, 1)[:, 0:HALF], ACT.Copy)\
                        .then_inc(s.emptied_of(c + 1), 1)
                    if c >= 1:
                        silu(a, c - 1)
                    if c == 1:
                        s.wait_emptied(a, 0, 1)
                        c_(nc.scalar.activation(tmp[:, 0, :], k.sT[:], ACT.Abs))
                        c_(nc.scalar.activation(tmp[:, 1, :], tmp[:, 0, :], ACT.Exp, scale=-1.0))
                        nc.scalar.activation(tmp[:, 0, :], tmp[:, 1, :], ACT.Ln, bias=k.one[0:96, :]).then_inc(logged, 1)
                    norms.roots(a, group_at.get(c - 1, ()))
                silu(a, NCC - 1)

            @block.vector
            def _(v):
                c_ = k.chain(v, "vector")
                levels_of_inversion(k, v)
                for h in range(2):
                    v.wait_ge(s.half, h + 1)
                    c_(nc.vector.tensor_scalar(k.sT[:, h * HALF:(h + 1) * HALF], s.bank(0, h)[0:96, 0:HALF],
                                               k.sm_bias[0:96, :], k.sm_sign[0:96, :], ALU.add, ALU.mult))
                for b in range(2):
                    nc.vector.memset(cin[:, b, 3 + NS:6 + NS], 0.0).then_inc(s.emptied_of(0), 1)
                s.wait_emptied(v, 0, 1)
                for c in range(NCC):
                    if c == 3:
                        v.wait_ge(logged, 1)
                        c_(nc.vector.scalar_tensor_tensor(out=tmp[:, 1, :], in0=k.sT[:], scalar=0.0, in1=tmp[:, 0, :],
                                                          op0=ALU.max, op1=ALU.add))
                        nc.vector.tensor_scalar(k.sT[:], tmp[:, 1, :], k.sm_coef[0:96, :], None, ALU.mult).then_inc(rows, 1)
                    if c == 5:
                        v.wait_ge(turned, 1)
                        c_(nc.vector.tensor_copy(k.smt[:, 1:5, :], k.bank[4][:, 0:384].rearrange("p (t m) -> p t m", t=4)))
                        nc.vector.tensor_copy(k.smt[0:NS, 0, :], k.bank[5][0:NS, 0:96]).then_inc(copied, 1)
                    ci, ac = cin[:, c % 2], acc[:, c % 2]
                    c_(nc.vector.tensor_copy(ci[:, 0:3], k.hist[:, :, c]))
                    s.wait_emptied(v, c + 1, 1)
                    if c >= 2:
                        v.wait_ge(act_done, c - 1)
                    c_(nc.vector.tensor_scalar(ac[:, 0:W], ci[:, 0:W], k.wconv[:, 0, c:c + 1], None, ALU.mult))
                    for w in range(1, CONV_W):
                        op = nc.vector.scalar_tensor_tensor(out=ac[:, 0:W], in0=ci[:, w:w + W],
                                                            scalar=k.wconv[:, w, c:c + 1], in1=ac[:, 0:W],
                                                            op0=ALU.mult, op1=ALU.add)
                        if w < CONV_W - 1:
                            c_(op)
                        else:
                            op.then_inc(summed, 1)
                    nc.vector.tensor_copy(last3[:, 0:3, c], ci[:, NS:NS + 3])
                    nc.vector.tensor_copy(last3[:, 3:6, c], ci[:, 3 + NT:6 + NT]).then_inc(kept, 1)
                    v.wait_ge(kept, c + 1)
                    norms.scale(v, group_at.get(c - 1, ()))
                v.wait_ge(last_turned, 1)
                nc.vector.tensor_copy(lastT[:], k.bank[4][0:96, 0:128]).then_inc(last_copied, 1)


class Norms:

    def __init__(self, k, name, items, ctx):
        self.k, self.items = k, items
        self.sq = k.sb(name + "_sq", [128, 4, NT], F32, ctx)
        self.rt = k.sb(name + "_rt", [128, 4, NT], F32, ctx)
        self.squared, self.summed, self.logged, self.rooted, self.scaled = (
            k.sem(f"{name}_{n}") for n in ("squared", "summed", "logged", "rooted", "scaled"))

    def square(self, g, j):
        T, c = self.items[j][0:2]
        self.items[j][5](g)
        if j >= 4:
            g.wait_ge(self.summed, j - 3)
        self.k.nc.gpsimd.tensor_tensor(self.sq[:, j % 4, :], T[:, c, :], T[:, c, :], ALU.mult).then_inc(self.squared, 1)

    def sums(self, pe, group):
        k = self.k
        for j in group:
            pe.wait_ge(self.squared, j + 1)
            if j >= 2:
                pe.wait_ge(self.logged, j - 1)
            for h in range(2):
                last = k.nc.tensor.matmul(k.bank[4 + 2 * (j % 2) + h][:, 0:HALF], self.items[j][3][:],
                                          self.sq[:, j % 4, h * HALF:(h + 1) * HALF], start=True, stop=True)
            last.then_inc(self.summed, 1)

    def roots(self, a, group):
        k = self.k
        for j in group:
            a.wait_ge(self.summed, j + 1)
            if j >= 4:
                a.wait_ge(self.scaled, j - 3)
            for h in range(2):
                last = k.nc.scalar.activation(self.rt[:, j % 4, h * HALF:(h + 1) * HALF],
                                              k.bank[4 + 2 * (j % 2) + h][:, 0:HALF], ACT.Ln,
                                              bias=k.eps[:], scale=self.items[j][4])
            last.then_inc(self.logged, 1)
        for j in group:
            a.wait_ge(self.logged, j + 1)
            k.nc.scalar.activation(self.rt[:, j % 4, :], self.rt[:, j % 4, :], ACT.Exp, scale=-0.5).then_inc(self.rooted, 1)

    def scale(self, v, group):
        for j in group:
            T, c, f = self.items[j][0:3]
            v.wait_ge(self.rooted, j + 1)
            self.k.nc.vector.scalar_tensor_tensor(out=T[:, c, :], in0=T[:, c, :], scalar=f, in1=self.rt[:, j % 4, :],
                                                  op0=ALU.mult, op1=ALU.mult).then_inc(self.scaled, 1)


def delta_net(k):
    nc = k.nc
    with ExitStack() as ctx:
        beta, G, nG, Gt, eG, egl, kf = (k.sb("g_" + n, [128, 5, H], F32, ctx)
                                        for n in ("beta", "cum", "ncum", "total", "exp", "exptot", "tail"))
        GT = k.sb("g_cols", [H, NT], F32, ctx)
        kg = k.sb("k_grown", [128, 5, WA], F32, ctx)
        kd = k.sb("k_tail", [128, 5, WA], F32, ctx)
        S = k.sb("state_p", [128, 4, DV], F32, ctx)
        Ss = k.sb("state_s", [128, 4, DV], F32, ctx)
        stored = k.sem("g_stored")
        smask = k.sb("later_neg_s", [NS, 4, NS], F32, ctx)
        identr = k.sb("ident_r", [128, 128], F32R, ctx)
        negr = k.sb("later_neg_r", [128, 128], F32R, ctx)
        selr = k.sb("sel_r", [H, H, 128], F32R, ctx)
        selpr = k.sb("selpair_r", [H, 4, 128], F32R, ctx)
        GTh = k.sb("g_cols_hi", [H, NP], F32R, ctx)
        GTl = k.sb("g_cols_lo", [H, NP], F32R, ctx)
        summed, cum, grown, kT, kread, loaded = (k.sem("g0_" + n) for n in ("sum", "cum", "exp", "kT", "kread", "state"))
        parts = [(slice(0, NS), slice(0, 1)), (slice(0, 128), slice(1, 5))]
        with nc.Block() as block:
            @block.sync
            def _(sp):
                for a in range(2):
                    sp.dma_start(Ss[64 * a:64 * a + 64], k.i["state_gdn"][0, 0].rearrange("(p a) k v -> a k p v", a=2)[a])\
                        .then_inc(loaded, 16)
                sp.wait_ge(loaded, 32)

            @block.tensor
            def _(pe):
                g = k.smt[:, :, 64:72]
                for t, (c0, n) in enumerate(TILES):
                    out = k.bank[1][0:n, 0:H] if t == 0 else k.bank[0][:, H * (t - 1):H * t]
                    nc.tensor.matmul(out, k.triu[0:n, 0:n], g[0:n, t, :], start=True, stop=True)
                    nc.tensor.matmul(k.bank[2][:, H * t:H * t + H], k.ones[0:n, :], g[0:n, t, :], start=True, stop=True)
                    out = k.bank[3][0:H, 0:n] if t == 0 else k.bank[4][0:H, 128 * (t - 1):128 * t]
                    last = nc.tensor.matmul(out, g[0:n, t, :], k.triu[0:n, 0:n], start=True, stop=True)
                last.then_inc(summed, 1)
                for p in range(4):
                    if p >= 2:
                        pe.wait_ge(kread, p - 1)
                    b = (5, 7)[p % 2]
                    b0 = (6, 1)[p % 2]
                    if p == 1:
                        pe.wait_ge(cum, 1)
                    for t, (c0, n) in enumerate(TILES):
                        out = k.bank[b0][0:n, 0:128] if t == 0 else k.bank[b][:, 128 * (t - 1):128 * t]
                        last = nc.tensor.transpose(out, k.cT[:, 4 + p, c0:c0 + n], k.ident[:])
                    last.then_inc(kT, 1)

            @block.vector
            def _(v):
                c = k.chain(v, "vector")
                c(nc.vector.memset(smask[:], 0.0))
                v.wait_ge(summed, 1)
                c(nc.vector.tensor_copy(G[0:NS, 0], k.bank[1][0:NS, 0:H]))
                c(nc.vector.tensor_copy(G[:, 1:5], k.bank[0][:, 0:4 * H].rearrange("p (t h) -> p t h", t=4)))
                c(nc.vector.tensor_copy(Gt[:], k.bank[2][:, 0:5 * H].rearrange("p (t h) -> p t h", t=5)))
                c(nc.vector.tensor_copy(GT[:, 0:NS], k.bank[3][0:H, 0:NS]))
                c(nc.vector.tensor_copy(GT[:, NS:NT], k.bank[4][0:H, 0:NP]))
                c(nc.vector.tensor_copy(smask[:], k.later_neg[0:NS, 0:NS].unsqueeze(1).broadcast_to([NS, 4, NS])))
                c(nc.vector.tensor_copy(GTh[:], GT[:, NS:NT]))
                nc.vector.tensor_tensor(GTl[:], GT[:, NS:NT], GTh[:].bitcast(F32), ALU.subtract)
                for dst, src in ((identr, k.ident), (negr, k.later_neg), (selr, k.sel), (selpr, k.selpair)):
                    full = tuple(slice(None) for _ in dst.shape)
                    nc.vector.tensor_copy(dst[full], src[full])
                for rows, ts in parts:
                    c(nc.vector.tensor_tensor(kf[rows, ts], Gt[rows, ts], G[rows, ts], ALU.subtract))
                    c(nc.vector.tensor_scalar(nG[rows, ts], G[rows, ts], -1.0, None, ALU.mult))
                nc.vector.memset(S[:], 0.0).then_inc(cum, 1)
                v.wait_ge(grown, 1)
                for p in range(4):
                    v.wait_ge(kT, p + 1)
                    b = (5, 7)[p % 2]
                    b0 = (6, 1)[p % 2]
                    for f, dst in ((eG, kg), (kf, kd)):
                        fac = f[:, :, 2 * p:2 * p + 2].unsqueeze(3)
                        nc.vector.tensor_tensor(
                            dst[0:NS, 0, 128 * p:128 * p + 128].rearrange("p (a c) -> p a c", a=2),
                            k.bank[b0][0:NS, 0:128].rearrange("p (a c) -> p a c", a=2),
                            fac[0:NS, 0].broadcast_to([NS, 2, 64]), ALU.mult)
                        last = nc.vector.tensor_tensor(
                            dst[:, 1:5, 128 * p:128 * p + 128].rearrange("p t (a c) -> p t a c", a=2),
                            k.bank[b][:].rearrange("p (t a c) -> p t a c", t=4, a=2),
                            fac[:, 1:5].broadcast_to([128, 4, 2, 64]), ALU.mult)
                    last.then_inc(kread, 1)

            @block.scalar
            def _(a):
                c = k.chain(a, "scalar")
                for rows, ts in parts:
                    c(nc.scalar.activation(beta[rows, ts], k.smt[rows, ts, 32:40], ACT.Exp))
                a.wait_ge(cum, 1)
                for rows, ts in parts:
                    c(nc.scalar.activation(eG[rows, ts], G[rows, ts], ACT.Exp))
                    c(nc.scalar.activation(kf[rows, ts], kf[rows, ts], ACT.Exp))
                nc.scalar.activation(egl[:], Gt[:], ACT.Exp).then_inc(grown, 1)

        def units(r, a):
            if r == 0:
                return [(2 * u + a, 0, 0) for u in range(4)]
            return [(2 * (r - 1) + a, t, TILES[t][0]) for t in range(1, 5)]

        R, A, U = range(5), range(2), range(4)
        width = lambda r: NS if r == 0 else 128
        levels = lambda r: range(5 if r == 0 else 7)
        base = lambda h: 64 * (h % 2)
        st = lambda r: Ss if r == 0 else S
        ra = [(r, a) for r in R for a in A]
        ral = [(r, l, a) for r in R for l in levels(r) for a in A]
        mid = [x for x in ral if 0 < x[1] < levels(x[0])[-1]]
        rua = [(r, u, a) for r in R for u in U for a in A]
        m = {n: k.marks("g_" + n, names) for n, names in dict(
            scores=ra, kq=ra, low=ral, grown=[x for x in ral if x[1] > 0], xt=mid, wt=ra, vsum=rua, upd=rua, egp=R, vT=ra,
            dec=ra, lowc=[x for x in ral if x[1] > 0], xc=mid, wtc=ra, outc=ra, egx=R, vtok=ra,
            mt=ra, at=ra, inv=ral, vnew=rua, state=rua,
            ml=ral, qd=R).items()}
        dec, mt, at, P, X, Xt, wT, vt = (k.sb("g_" + n, [128, 2, 512], F32, ctx)
                                         for n in ("dec", "mt", "at", "low", "inv", "invT", "wT", "vt"))
        ml = k.sb("g_ml", [128, 2, 2, 512], F32, ctx)
        qd = k.sb("g_qd", [128, 512], F32, ctx)
        egp = k.sb("g_egp", [128, 512], F32, ctx)
        vn = k.sb("g_vn", [128, 2, DV], F32, ctx)
        bank = lambda a, n: k.bank[4 * a + n]
        qcols = lambda r, h, t: slice(NS * (h // 2), NS * (h // 2) + NS) if r == 0 else slice(128 * (t - 1), 128 * t)
        with nc.Block() as block:
            @block.tensor
            def _(pe):
                def score(r, a):
                    w = width(r)
                    for u, (h, t, c0) in enumerate(units(r, a)):
                        kT_ = k.cT[base(h):base(h) + 64, 4 + h // 2, c0:c0 + w]
                        nc.tensor.matmul(bank(a, 0)[0:w, u * w:u * w + w], kT_, kT_, start=True, stop=True)
                    idn, neg = (k.ident[0:w, 0:w], smask[:]) if r == 0 else (
                        identr[:], negr[:].unsqueeze(1).broadcast_to([128, 4, 128]))
                    nc.tensor.matmul(bank(a, 2)[0:w, 0:4 * w], idn, neg, start=True, stop=False)
                    if r == 0:
                        for u, (h, t, c0) in enumerate(units(r, a)):
                            last = nc.tensor.matmul(bank(a, 2)[0:w, u * w:u * w + w], k.sel[:, h, 0:w], GT[:, 0:NS],
                                                    start=False, stop=(u == 3))
                    else:
                        sel = selr[:, units(r, a)[0][0], :]
                        nc.tensor.matmul(bank(a, 2)[:], sel, GTh[:], start=False, stop=False)
                        last = nc.tensor.matmul(bank(a, 2)[:], sel, GTl[:], start=False, stop=True)
                    m["scores"].mark(last, (r, a))

                def prepare(r):
                    w = width(r)
                    if r >= 1:
                        m["outc"].wait(pe, (r - 1, 0))
                    if r == 0:
                        for p in range(4):
                            last = nc.tensor.matmul(bank(0, 3)[:, NS * p:NS * p + NS], k.selpair[:, p, :], GT[:, 0:NS],
                                                    start=True, stop=True)
                    else:
                        nc.tensor.matmul(bank(0, 3)[:], selpr[:, r - 1, :], GTh[:], start=True, stop=False)
                        last = nc.tensor.matmul(bank(0, 3)[:], selpr[:, r - 1, :], GTl[:], start=False, stop=True)
                    m["egp"].mark(last, r)
                    for a in A:
                        if r >= 1:
                            m["state"].wait(pe, (r - 1, 3, a))
                        for u, (h, t, c0) in enumerate(units(r, a)):
                            b, cols = base(h), slice(c0, c0 + w)
                            last = nc.tensor.matmul(bank(a, 1)[0:w, u * w:u * w + w], k.cT[b:b + 64, 4 + h // 2, cols],
                                                    k.cT[b:b + 64, h // 2, cols], start=True, stop=True)
                        m["kq"].mark(last, (r, a))
                    m["egx"].wait(pe, r)
                    for a in A:
                        if r >= 1:
                            m["outc"].wait(pe, (r - 1, a))
                        for u, (h, t, c0) in enumerate(units(r, a)):
                            last = nc.tensor.transpose(bank(a, 3)[0:w, u * 128:u * 128 + 128], k.cT[:, 8 + h, c0:c0 + w],
                                                       k.ident[:])
                        m["vT"].mark(last, (r, a))

                for a in A:
                    score(0, a)
                for r in R:
                    w = width(r)
                    for l in levels(r):
                        for a in A if l >= 2 else ():
                            m["inv"].wait(pe, (r, l - 1, a))
                            if l == 2:
                                m["at"].wait(pe, (r, a))
                            for u in U:
                                o = slice(u * w, u * w + w)
                                last = nc.tensor.transpose(bank(a, 1)[0:w, o], Xt[0:w, a, o], k.ident[0:w, 0:w])
                            m["xt"].mark(last, (r, l - 1, a))
                        for a in A:
                            m["ml"].wait(pe, (r, l, a))
                            if l == 1:
                                m["inv"].wait(pe, (r, 0, a))
                            elif l >= 2:
                                m["xc"].wait(pe, (r, l - 1, a))
                            for u in U:
                                o = slice(u * w, u * w + w)
                                if l == 0:
                                    last = nc.tensor.transpose(bank(a, 0)[0:w, o], ml[0:w, a, 0, o], k.ident[0:w, 0:w])
                                else:
                                    last = nc.tensor.matmul(bank(a, 0)[0:w, o], ml[0:w, a, l % 2, o], X[0:w, a, o],
                                                            start=True, stop=True)
                            m["low"].mark(last, (r, l, a))
                        if l == 0:
                            prepare(r)
                            continue
                        for a in A:
                            m["lowc"].wait(pe, (r, l, a))
                            for u in U:
                                o = slice(u * w, u * w + w)
                                last = nc.tensor.matmul(bank(a, 2)[0:w, o], P[0:w, a, o], Xt[0:w, a, o], start=True, stop=True)
                            m["grown"].mark(last, (r, l, a))
                    for a in A:
                        m["inv"].wait(pe, (r, levels(r)[-1], a))
                        for u, (h, t, c0) in enumerate(units(r, a)):
                            b = base(h)
                            last = nc.tensor.matmul(bank(a, 0)[b:b + 64, u * w:u * w + w], kg[0:w, t, 64 * h:64 * h + 64],
                                                    Xt[0:w, a, u * w:u * w + w], start=True, stop=True)
                        m["wt"].mark(last, (r, a))
                    for u in U:
                        for a in A:
                            h, t, c0 = units(r, a)[u]
                            b, o = base(h), slice(u * w, u * w + w)
                            first = r > 0 and u == 0
                            if u == 0:
                                m["wtc"].wait(pe, (r, a))
                                m["vtok"].wait(pe, (r, a))
                            else:
                                m["state"].wait(pe, (r, u - 1, a))
                            if u > 0:
                                m["vnew"].wait(pe, (r, u - 1, a))
                            last = nc.tensor.matmul(bank(a, 1)[0:w, 0:DV], Xt[0:w, a, o], vt[0:w, a, u * DV:u * DV + DV],
                                                    start=True, stop=first)
                            if not first:
                                last = nc.tensor.matmul(bank(a, 1)[0:w, 0:DV], wT[b:b + 64, a, o],
                                                        st(r)[b:b + 64, h // 2, :], start=False, stop=True)
                            m["vsum"].mark(last, (r, u, a))
                        for a in A:
                            h, t, c0 = units(r, a)[u]
                            b, o = base(h), slice(u * w, u * w + w)
                            first = r > 0 and u == 0
                            if not first:
                                nc.tensor.matmul(bank(a, 3)[:, o], st(r)[b:b + 64, h // 2, :],
                                                 qd[b:b + 64, qcols(r, h, t)], start=True, stop=False)
                            m["vnew"].wait(pe, (r, u, a))
                            nc.tensor.matmul(bank(a, 3)[:, o], vn[0:w, a, :], at[0:w, a, o], start=first, stop=True)
                            last = nc.tensor.matmul(bank(a, 1)[b:b + 64, DV:2 * DV], kd[0:w, t, 64 * h:64 * h + 64],
                                                    vn[0:w, a, :], start=True, stop=True)
                            m["upd"].mark(last, (r, u, a))
                        if u in (1, 2) and r + 1 in R:
                            score(r + 1, u - 1)

            @block.scalar
            def _(s):
                def decay(r, a):
                    w = width(r)
                    m["scores"].wait(s, (r, a))
                    if r >= 1:
                        m["at"].wait(s, (r - 1, a))
                    for u, (h, t, c0) in enumerate(units(r, a)):
                        o = slice(u * w, u * w + w)
                        last = nc.scalar.activation(dec[0:w, a, o], bank(a, 2)[0:w, o], ACT.Exp, bias=nG[0:w, t, h:h + 1])
                    m["dec"].mark(last, (r, a))

                for a in A:
                    decay(0, a)
                for r in R:
                    w = width(r)
                    m["egp"].wait(s, r)
                    if r >= 1:
                        m["qd"].wait(s, r - 1)
                    m["egx"].mark(nc.scalar.activation(egp[:, 0:4 * w], bank(0, 3)[:, 0:4 * w], ACT.Exp), r)
                    for a in A:
                        m["vT"].wait(s, (r, a))
                        m["vtok"].mark(nc.scalar.activation(vt[0:w, a, :], bank(a, 3)[0:w, :], ACT.Copy), (r, a))
                    for l in levels(r)[1:]:
                        for a in A if l >= 2 else ():
                            m["xt"].wait(s, (r, l - 1, a))
                            m["xc"].mark(nc.scalar.activation(X[0:w, a, 0:4 * w], bank(a, 1)[0:w, 0:4 * w], ACT.Copy),
                                         (r, l - 1, a))
                        for a in A:
                            m["low"].wait(s, (r, l, a))
                            m["lowc"].mark(nc.scalar.activation(P[0:w, a, 0:4 * w], bank(a, 0)[0:w, 0:4 * w], ACT.Copy),
                                           (r, l, a))
                    for a in A:
                        m["wt"].wait(s, (r, a))
                        b = 64 * a
                        last = nc.scalar.activation(wT[b:b + 64, a, 0:4 * w], bank(a, 0)[b:b + 64, 0:4 * w], ACT.Copy,
                                                    scale=-1.0)
                        m["wtc"].mark(last, (r, a))
                    for a in A if r + 1 in R else ():
                        decay(r + 1, a)
                    for a in A:
                        m["upd"].wait(s, (r, 3, a))
                        if r == 0:
                            out, src = k.yb[:, a::2, 0:NS], bank(a, 3)[:, 0:128].rearrange("p (h n) -> p h n", h=4)
                        else:
                            out, src = k.yb[:, 2 * (r - 1) + a, NS:NT], bank(a, 3)[:]
                        m["outc"].mark(nc.scalar.activation(out, src, ACT.Copy), (r, a))

            @block.vector
            def _(v):
                def masked(r, a):
                    w = width(r)
                    m["dec"].wait(v, (r, a))
                    for u, (h, t, c0) in enumerate(units(r, a)):
                        o = slice(u * w, u * w + w)
                        last = nc.vector.scalar_tensor_tensor(out=mt[0:w, a, o], in0=bank(a, 0)[0:w, o],
                                                              scalar=beta[0:w, t, h:h + 1], in1=dec[0:w, a, o],
                                                              op0=ALU.mult, op1=ALU.mult)
                    m["mt"].mark(last, (r, a))

                for a in A:
                    masked(0, a)
                for r in R:
                    w = width(r)
                    idb = k.ident[0:w, 0:w].unsqueeze(1).broadcast_to([w, 4, w])
                    for l in levels(r):
                        for a in A:
                            f = slice(0, 4 * w)
                            if l == 0:
                                m["low"].wait(v, (r, l, a))
                                nc.vector.tensor_tensor(X[0:w, a, f].rearrange("p (u n) -> p u n", u=4), idb,
                                                        bank(a, 0)[0:w, f].rearrange("p (u n) -> p u n", u=4), ALU.subtract)
                                last = nc.vector.tensor_tensor(Xt[0:w, a, f].rearrange("p (u n) -> p u n", u=4), idb,
                                                               ml[0:w, a, 0, f].rearrange("p (u n) -> p u n", u=4),
                                                               ALU.subtract)
                            else:
                                m["grown"].wait(v, (r, l, a))
                                last = nc.vector.tensor_tensor(Xt[0:w, a, f], Xt[0:w, a, f], bank(a, 2)[0:w, f],
                                                               ALU.subtract)
                            m["inv"].mark(last, (r, l, a))
                        for a in A if l == 0 else ():
                            m["kq"].wait(v, (r, a))
                            m["at"].mark(nc.vector.tensor_tensor(at[0:w, a, 0:4 * w], bank(a, 1)[0:w, 0:4 * w],
                                                                 dec[0:w, a, 0:4 * w], ALU.mult), (r, a))
                    for u in U:
                        for a in A:
                            h, t, c0 = units(r, a)[u]
                            m["vsum"].wait(v, (r, u, a))
                            if u > 0:
                                m["upd"].wait(v, (r, u - 1, a))
                            m["vnew"].mark(nc.vector.tensor_scalar(vn[0:w, a, :], bank(a, 1)[0:w, 0:DV],
                                                                   beta[0:w, t, h:h + 1], None, ALU.mult), (r, u, a))
                        for a in A:
                            h, t, c0 = units(r, a)[u]
                            b = base(h)
                            m["upd"].wait(v, (r, u, a))
                            if u > 0:
                                m["state"].wait(v, (r, u - 1, a))
                            m["state"].mark(nc.vector.scalar_tensor_tensor(
                                out=st(r)[b:b + 64, h // 2, :], in0=st(r)[b:b + 64, h // 2, :],
                                scalar=egl[b:b + 64, t, h:h + 1], in1=bank(a, 1)[b:b + 64, DV:2 * DV],
                                op0=ALU.mult, op1=ALU.add), (r, u, a))
                        if u >= 2 and r + 1 in R:
                            masked(r + 1, u - 2)

            @block.gpsimd
            def _(g):
                for r in R:
                    w = width(r)
                    for l in levels(r):
                        if l == 2:
                            m["egx"].wait(g, r)
                            if r >= 1:
                                m["upd"].wait(g, (r - 1, 3, 1))
                            if r == 0:
                                q, e = qd[:, 0:4 * w].rearrange("p (c n) -> p c n", c=4), egp[:, 0:4 * w].rearrange("p (c n) -> p c n", c=4)
                                m["qd"].mark(nc.gpsimd.tensor_tensor(q, k.cT[:, 0:4, 0:NS], e, ALU.mult), r)
                            else:
                                m["qd"].mark(nc.gpsimd.tensor_tensor(qd[:], k.cT[:, r - 1, NS:NT], egp[:], ALU.mult), r)
                        for a in A:
                            if l == 0:
                                m["mt"].wait(g, (r, a))
                            if l >= 2:
                                m["low"].wait(g, (r, l - 2, a))
                            if l == 2:
                                m["inv"].wait(g, (r, 0, a))
                            f = slice(0, 4 * w)
                            m["ml"].mark(nc.gpsimd.tensor_tensor(
                                ml[0:w, a, l % 2, f].rearrange("p (u n) -> p u n", u=4),
                                mt[0:w, a, f].rearrange("p (u n) -> p u n", u=4),
                                k.level[0:w, l, 0:w].unsqueeze(1).broadcast_to([w, 4, w]), ALU.mult), (r, l, a))

            @block.sync
            def _(sp):
                for r, src, name in ((0, Ss, "state_s"), (4, S, "state_p")):
                    m["state"].wait(sp, (r, 3, 1))
                    for a in range(2):
                        sp.dma_start(k.o[name][0, 0].rearrange("(p a) k v -> a k p v", a=2)[a], src[64 * a:64 * a + 64])\
                            .then_inc(stored, 16)
                sp.wait_ge(stored, 64)


def attention(k):
    nc = k.nc
    with ExitStack() as ctx:
        fT = k.sb("fox_cols", [128, 12, NT], F32, ctx)
        with ExitStack() as inner:
            zs = k.sb("z_silu", [128, 2, NT], F32, inner)
            chunks = [([(0, w_in_cols(k, C_FQ + 128 * c))], KD, k.xhi, k.xlo) for c in range(12)]
            chunks += [([(0, w_in_cols(k, C_Z + 128 * c))], KD, k.xhi, k.xlo) for c in range(H)]
            s = Stream(k, "fz", chunks, inner, [0] * 12 + [1] * 8, raws=3)
            norms = Norms(k, "hn", [(k.yb, h, k.go[:], k.ones, 1.0 / DV, lambda g: None) for h in range(H)] +
                          [(fT, c, (k.gq if c < 4 else k.gk)[:], k.head_ones, 1.0 / DH,
                            lambda g, c=c: s.wait_emptied(g, c, 1)) for c in range(8)], inner)
            group_at = {2 * g + 1: (2 * g, 2 * g + 1) for g in range(8)}
            gate, hi, lo = k.sem("z_gated"), k.sem("z_hi"), k.sem("z_lo")
            with nc.Block() as block:
                @block.sync
                def _(sp):
                    for c in range(20):
                        s.load(sp, c)

                @block.gpsimd
                def _(g):
                    for c in range(20):
                        s.split_lo(g, c)
                        if c >= 2 and c < 18:
                            norms.square(g, c - 2)

                @block.tensor
                def _(pe):
                    for c in range(20):
                        s.product(pe, c)
                        norms.sums(pe, group_at.get(c, ()))

                def high(a, h):
                    a.wait_ge(gate, h + 1)
                    nc.scalar.activation(k.ybh[:, h, :], k.yb[:, h, :], ACT.Copy).then_inc(hi, 1)

                @block.scalar
                def _(a):
                    for c in range(LEAD):
                        s.split_hi(a, c)
                    for c in range(20):
                        if c + LEAD < 20:
                            s.split_hi(a, c + LEAD)
                        if c >= 14:
                            a.wait_ge(gate, c - 13)
                        for h in range(2 if c >= 12 else 0):
                            a.wait_ge(s.half, 2 * c + h + 1)
                            nc.scalar.activation(zs[:, c % 2, h * HALF:(h + 1) * HALF], s.bank(c, h)[:, 0:HALF],
                                                 ACT.Silu).then_inc(s.emptied_of(c), 1)
                        norms.roots(a, group_at.get(c - 1, ()))
                        if c >= 13:
                            high(a, c - 13)
                    high(a, H - 1)

                @block.vector
                def _(v):
                    for c in range(12):
                        for h in range(2):
                            v.wait_ge(s.half, 2 * c + h + 1)
                            nc.vector.tensor_copy(fT[:, c, h * HALF:(h + 1) * HALF], s.bank(c, h)[:, 0:HALF])\
                                .then_inc(s.emptied_of(c), 1)
                        norms.scale(v, group_at.get(c - 2, ()))
                    for h in range(H):
                        norms.scale(v, group_at.get(10 + h, ()))
                        s.wait_emptied(v, 12 + h, 1)
                        if h == 0:
                            v.wait_ge(norms.scaled, H)
                        nc.vector.tensor_tensor(k.yb[:, h, :], k.yb[:, h, :], zs[:, h % 2, :], ALU.mult)\
                            .then_inc(gate, 1)
                        v.wait_ge(hi, h + 1)
                        nc.vector.tensor_tensor(k.ybl[:, h, :], k.yb[:, h, :], k.ybh[:, h, :].bitcast(F32),
                                                ALU.subtract).then_inc(lo, 1)
        k.yb_ctx.close()
        k.yah = k.sb("ya_hi", [128, 4, NT], F32R, k.mixer)
        k.yal = k.sb("ya_lo", [128, 4, NT], F32R, k.mixer)
        vt = k.sb("fox_v", [128, 5, WA], F32, ctx)
        vp = k.sb("fox_vpast", [128, WA], F32, ctx)
        kTs = k.sb("fox_kT_s", [128, 4, PAST + NS], F32, ctx)
        ncT = k.sb("fox_nc", [H, PAST + NS + NP], F32, ctx)
        with ExitStack() as inner:
            kt = k.sb("fox_k", [128, 2, WA], F32, inner)
            kp = k.sb("fox_kpast", [128, WA], F32, inner)
            lp = k.sb("fox_logf_past", [128, H], F32, inner)
            loaded, tr, kc, vc, rest, restc, stored = (k.sem("f1_" + n) for n in
                                                       ("loaded", "tr", "kcopy", "vcopy", "rest", "restcopy", "stored"))
            with nc.Block() as block:
                @block.sync
                def _(sp):
                    sp.dma_start(kp[:], k.i["cache_fox_k"][0, 0].rearrange("p h c -> p (h c)")).then_inc(loaded, 16)
                    sp.dma_start(vp[:], k.i["cache_fox_v"][0, 0].rearrange("p h c -> p (h c)")).then_inc(loaded, 16)
                    sp.dma_start(lp[:], k.i["cache_fox_logf"][0, 0]).then_inc(loaded, 16)
                    for t, (c0, n) in enumerate(TILES):
                        for what, src, sem in (("k", kt[0:n, t % 2, :], kc), ("v", vt[0:n, t, :], vc)):
                            sp.wait_ge(sem, t + 1)
                            dst = k.o[what + ("_s" if t == 0 else "_p")][0, 0].rearrange("t h c -> t (h c)")
                            dst = dst if t == 0 else dst[128 * (t - 1):128 * t, :]
                            sp.dma_start(dst, src).then_inc(stored, 16)
                        sp.wait_ge(stored, 32 * (t + 1))
                    sp.wait_ge(loaded, 48)

                @block.tensor
                def _(pe):
                    for t, (c0, n) in enumerate(TILES):
                        if t >= 2:
                            pe.wait_ge(kc, t - 1)
                            pe.wait_ge(vc, t - 1)
                        for part in (4, 8):
                            b = k.bank[2 * (t % 2) + (part == 8)]
                            for c in range(4):
                                last = nc.tensor.transpose(b[0:n, 128 * c:128 * c + 128], fT[:, part + c, c0:c0 + n],
                                                           k.ident[:])
                        last.then_inc(tr, 1)
                    pe.wait_ge(loaded, 48)
                    for c in range(4):
                        nc.tensor.transpose(k.bank[4][:, 128 * c:128 * c + 128], kp[:, 128 * c:128 * c + 128], k.ident[:])
                    for j in range(4):
                        nc.tensor.matmul(k.bank[5][0:H, 128 * j:NP], k.smt[:, 1 + j, 0:H], k.triu[:, 0:NP - 128 * j],
                                         start=(j == 0), stop=(j == 3))
                    nc.tensor.matmul(k.bank[6][0:H, 0:PAST + NS], lp[:], k.triu[:, 0:PAST + NS], start=True, stop=False)
                    nc.tensor.matmul(k.bank[6][0:H, PAST:PAST + NS], k.smt[0:NS, 0, 0:H], k.triu[0:NS, 0:NS],
                                     start=False, stop=True).then_inc(rest, 1)

                @block.vector
                def _(v):
                    for t, (c0, n) in enumerate(TILES):
                        v.wait_ge(tr, t + 1)
                        if t >= 2:
                            v.wait_ge(stored, 32 * (t - 1))
                        nc.vector.tensor_copy(kt[0:n, t % 2, :], k.bank[2 * (t % 2)][0:n, :]).then_inc(kc, 1)
                    v.wait_ge(rest, 1)
                    nc.vector.tensor_copy(kTs[:, :, 0:PAST], k.bank[4][:].rearrange("p (c n) -> p c n", c=4))
                    nc.vector.tensor_copy(kTs[:, :, PAST:PAST + NS], fT[:, 4:8, 0:NS])
                    nc.vector.tensor_scalar(ncT[:, 0:PAST + NS], k.bank[6][0:H, 0:PAST + NS], -1.0, None, ALU.mult)
                    nc.vector.tensor_scalar(ncT[:, PAST + NS:], k.bank[5][0:H, :], -1.0, None, ALU.mult)

                @block.scalar
                def _(a):
                    for t, (c0, n) in enumerate(TILES):
                        a.wait_ge(tr, t + 1)
                        nc.scalar.activation(vt[0:n, t, :], k.bank[2 * (t % 2) + 1][0:n, :], ACT.Copy).then_inc(vc, 1)

        fox_heads(k, fT, vt, vp, kTs, ncT)


def fox_heads(k, fT, vt, vp, kTs, ncT):
    nc = k.nc
    items = [(h, t) for h in range(H) for t in range(5)]
    J = len(items)
    base = lambda h: 64 * (h % 2)

    def sizes(t):
        n = TILES[t][1]
        blocks = [(0, PAST), (PAST, NS)] if t == 0 else [(128 * b, 128) for b in range(t)]
        return n, blocks[-1][0] + blocks[-1][1], blocks

    with ExitStack() as ctx:
        nch = k.sb("fox_nc_hi", [H, NP], F32R, ctx)
        ncl = k.sb("fox_nc_lo", [H, NP], F32R, ctx)
        selr = k.sb("fox_sel_r", [H, H, 128], F32R, ctx)
        split, zeroed, filled = k.sem("f_split"), k.sem("f_zeroed"), k.sem("f_filled")
        zero = k.sb("f_zero", [128, D], F32, ctx)
        ncb = k.sb("ncb", [128, 2, PAST + NS + NP], F32, ctx)
        sc = k.sb("f_scores", [128, 2, NP], F32, ctx)
        pr = k.sb("f_probs", [128, 3, NP], F32, ctx)
        pT = k.sb("f_probsT", [128, 2, NP], F32, ctx)
        st = k.sb("f_stat", [128, 4, J], F32, ctx)
        bias, biasc, score, biased, probs, scaled, turned, turnedc, out, outh, outl = (
            k.sem("f_" + n) for n in ("bias", "biasc", "score", "biased", "probs", "scaled", "turned", "turnedc",
                                      "out", "outh", "outl"))
        with nc.Block() as block:
            @block.gpsimd
            def _(g):
                g.memset(zero[:], 0.0).then_inc(zeroed, 1)

            @block.sync
            def _(sp):
                sp.wait_ge(zeroed, 1)
                sp.dma_start(k.table[NT:NT + 1, :], zero[0:1, :]).then_inc(filled, 16)
                for row in range(NE * SLOTS, NB * SLOTS, 128):
                    sp.dma_start(k.yblk[row:row + 128, :], zero[:]).then_inc(filled, 16)
                sp.wait_ge(filled, 16 * (1 + MORE * SLOTS // 128))

            @block.tensor
            def _(pe):
                def scores(j):
                    h, t = items[j]
                    n, nk, blocks = sizes(t)
                    b, c0 = base(h), TILES[t][0]
                    if t == 0:
                        if h >= 1:
                            pe.wait_ge(biasc, h)
                        nc.tensor.matmul(k.bank[6][:, 0:PAST + NS], k.sel[:, h, :], ncT[:, 0:PAST + NS],
                                         start=True, stop=True)
                        if h == 0:
                            pe.wait_ge(split, 1)
                        nc.tensor.matmul(k.bank[7][:], selr[:, h, :], nch[:], start=True, stop=False)
                        nc.tensor.matmul(k.bank[7][:], selr[:, h, :], ncl[:], start=False, stop=True)\
                            .then_inc(bias, 1)
                    if j >= 2:
                        pe.wait_ge(biased, j - 1)
                    keys = kTs[b:b + 64, h // 2, :] if t == 0 else fT[b:b + 64, 4 + h // 2, NS:NS + nk]
                    nc.tensor.matmul(k.bank[j % 2][0:n, 0:nk], fT[b:b + 64, h // 2, c0:c0 + n], keys, start=True, stop=False)
                    m0, mn = blocks[-1]
                    nc.tensor.matmul(k.bank[j % 2][0:n, m0:m0 + mn], k.ident[0:n, 0:n], k.causal_neg[0:n, 0:mn],
                                     start=False, stop=True).then_inc(score, 1)

                def turn(j):
                    h, t = items[j]
                    n, nk, blocks = sizes(t)
                    pe.wait_ge(scaled, j + 1)
                    if j >= 2:
                        pe.wait_ge(turnedc, j - 1)
                    for i, (m0, mn) in enumerate(blocks):
                        last = nc.tensor.transpose(k.bank[2 + j % 2][0:mn, i * n:i * n + n], pr[0:n, j % 3, m0:m0 + mn],
                                                   k.ident[0:n, 0:n])
                    last.then_inc(turned, 1)

                def values(j):
                    h, t = items[j]
                    n, nk, blocks = sizes(t)
                    b = base(h)
                    pe.wait_ge(turnedc, j + 1)
                    if j >= 2:
                        pe.wait_ge(outl, j - 1)
                    for i, (m0, mn) in enumerate(blocks):
                        hv = slice(64 * h, 64 * h + 64)
                        v = (vp[:, hv] if i == 0 else vt[0:NS, 0, hv]) if t == 0 else vt[:, 1 + i, hv]
                        last = nc.tensor.matmul(k.bank[4 + j % 2][b:b + 64, 0:n], v, pT[0:mn, j % 2, i * n:i * n + n],
                                                start=(i == 0), stop=(i == len(blocks) - 1))
                    last.then_inc(out, 1)

                for j in range(J + 3):
                    if j < J:
                        scores(j)
                    if 2 <= j < J + 2:
                        turn(j - 2)
                    if j >= 3:
                        values(j - 3)

            @block.vector
            def _(v):
                own = k.chain(v, "vector")

                def biases(j):
                    h, t = items[j]
                    n, nk, blocks = sizes(t)
                    v.wait_ge(score, j + 1)
                    v.wait_ge(biasc, h + 1)
                    if j >= 2:
                        v.wait_ge(probs, j - 1)
                    cols = slice(0, nk) if t == 0 else slice(PAST + NS, PAST + NS + nk)
                    own(nc.vector.tensor_tensor_reduce(out=sc[0:n, j % 2, 0:nk], in0=k.bank[j % 2][0:n, 0:nk],
                                                   in1=ncb[0:n, h % 2, cols], scale=1.0, scalar=-3e38,
                                                   op0=ALU.add, op1=ALU.max, accum_out=st[0:n, 0, j:j + 1]))
                    nc.vector.tensor_scalar(st[0:n, 1, j:j + 1], st[0:n, 0, j:j + 1], -1.0, None, ALU.mult)\
                        .then_inc(biased, 1)

                def scale(j):
                    h, t = items[j]
                    n, nk, blocks = sizes(t)
                    v.wait_ge(probs, j + 1)
                    own(nc.vector.reciprocal(st[0:n, 3, j:j + 1], st[0:n, 2, j:j + 1]))
                    nc.vector.tensor_scalar(pr[0:n, j % 3, 0:nk], pr[0:n, j % 3, 0:nk], st[0:n, 3, j:j + 1], None,
                                            ALU.mult).then_inc(scaled, 1)

                def low(j):
                    h, t = items[j]
                    n, b, c0 = TILES[t][1], base(h), TILES[t][0]
                    v.wait_ge(outh, j + 1)
                    nc.vector.tensor_tensor(k.yal[b:b + 64, h // 2, c0:c0 + n], k.bank[4 + j % 2][b:b + 64, 0:n],
                                            k.yah[b:b + 64, h // 2, c0:c0 + n].bitcast(F32), ALU.subtract)\
                        .then_inc(outl, 1)

                nc.vector.tensor_copy(selr[:], k.sel[:])
                own(nc.vector.tensor_copy(nch[:], ncT[:, PAST + NS:]))
                nc.vector.tensor_tensor(ncl[:], ncT[:, PAST + NS:], nch[:].bitcast(F32), ALU.subtract).then_inc(split, 1)
                for j in range(J + 4):
                    if j < J:
                        biases(j)
                    if 1 <= j <= J:
                        scale(j - 1)
                    if j >= 4:
                        low(j - 4)

            @block.scalar
            def _(a):
                def spread(h):
                    a.wait_ge(bias, h + 1)
                    if h >= 2:
                        a.wait_ge(biased, 5 * (h - 1))
                    nc.scalar.activation(ncb[:, h % 2, 0:PAST + NS], k.bank[6][:, 0:PAST + NS], ACT.Copy)
                    nc.scalar.activation(ncb[:, h % 2, PAST + NS:], k.bank[7][:], ACT.Copy).then_inc(biasc, 1)

                def exps(j):
                    h, t = items[j]
                    n, nk, blocks = sizes(t)
                    a.wait_ge(biased, j + 1)
                    if j >= 3:
                        a.wait_ge(turned, j - 2)
                    nc.scalar.activation(pr[0:n, j % 3, 0:nk], sc[0:n, j % 2, 0:nk], ACT.Exp, bias=st[0:n, 1, j:j + 1],
                                         accum_out=st[0:n, 2, j:j + 1]).then_inc(probs, 1)

                def copy(j):
                    h, t = items[j]
                    n, nk, blocks = sizes(t)
                    a.wait_ge(turned, j + 1)
                    if j >= 2:
                        a.wait_ge(out, j - 1)
                    if t == 0:
                        nc.scalar.activation(pT[:, j % 2, 0:n], k.bank[2 + j % 2][:, 0:n], ACT.Copy)
                        last = nc.scalar.activation(pT[0:NS, j % 2, n:2 * n], k.bank[2 + j % 2][0:NS, n:2 * n], ACT.Copy)
                    else:
                        last = nc.scalar.activation(pT[:, j % 2, 0:nk], k.bank[2 + j % 2][:, 0:nk], ACT.Copy)
                    last.then_inc(turnedc, 1)

                def high(j):
                    h, t = items[j]
                    n, b, c0 = TILES[t][1], base(h), TILES[t][0]
                    a.wait_ge(out, j + 1)
                    nc.scalar.activation(k.yah[b:b + 64, h // 2, c0:c0 + n], k.bank[4 + j % 2][b:b + 64, 0:n], ACT.Copy)\
                        .then_inc(outh, 1)

                for j in range(J + 4):
                    if j < J:
                        if items[j][1] == 0:
                            spread(items[j][0])
                        exps(j)
                    if 2 <= j < J + 2:
                        copy(j - 2)
                    if j >= 4:
                        high(j - 4)


def gated_sum(k):
    nc = k.nc
    mh, ml = k.mh, k.ml
    with ExitStack() as ctx:
        gate = k.sb("m_gate", [128, 2, NT], F32, ctx)
        part = k.sb("m_part", [128, 2, NT], F32, ctx)
        cols = lambda name, c: k.i[name][0].rearrange("(k p) n -> p k n", p=128)[:, :, 128 * c:128 * c + 128]
        chunks = []
        for c in range(KD):
            chunks += [([(0, w_in_cols(k, C_GA + 128 * c))], KD, k.xhi, k.xlo), ([(0, cols("w_br_a", c))], 4, k.yah, k.yal),
                       ([(0, w_in_cols(k, C_GB + 128 * c))], KD, k.xhi, k.xlo), ([(0, cols("w_br_b", c))], KD, k.ybh, k.ybl)]
        n = len(chunks)
        s = Stream(k, "mg", chunks, ctx, [1 if c % 2 == 0 else 0 for c in range(n)])
        sumd, high, low = (k.sem("m_" + x) for x in ("sum", "high", "low"))
        with nc.Block() as block:
            @block.sync
            def _(sp):
                for c in range(n):
                    s.load(sp, c)

            @block.gpsimd
            def _(g):
                for c in range(n):
                    s.split_lo(g, c)

            @block.tensor
            def _(pe):
                for c in range(n):
                    s.product(pe, c)

            @block.scalar
            def _(a):
                def high_part(j):
                    a.wait_ge(sumd, j + 1)
                    nc.scalar.activation(mh[:, j, :], part[:, 0, :], ACT.Copy).then_inc(high, 1)

                for c in range(LEAD):
                    s.split_hi(a, c)
                for c in range(n):
                    if c + LEAD < n:
                        s.split_hi(a, c + LEAD)
                    if c % 2 == 0:
                        if c >= 4:
                            s.wait_emptied(a, c - 3, 1)
                        for h in range(2):
                            a.wait_ge(s.half, 2 * c + h + 1)
                            nc.scalar.activation(gate[:, c // 2 % 2, h * HALF:(h + 1) * HALF], s.bank(c, h)[:, 0:HALF],
                                                 ACT.Sigmoid, bias=k.bgate[:, (c // 4) + 8 * (c // 2 % 2):][:, 0:1])\
                                .then_inc(s.emptied_of(c), 1)
                    if c >= 4 and c % 4 == 0:
                        high_part(c // 4 - 1)
                high_part(KD - 1)

            @block.vector
            def _(v):
                for c in range(1, n, 2):
                    if c % 4 == 1 and c > 1:
                        v.wait_ge(low, c // 4)
                    s.wait_emptied(v, c - 1, 1)
                    for h in range(2):
                        f = slice(h * HALF, (h + 1) * HALF)
                        v.wait_ge(s.half, 2 * c + h + 1)
                        nc.vector.tensor_tensor(part[:, c // 2 % 2, f], s.bank(c, h)[:, 0:HALF], gate[:, c // 2 % 2, f],
                                                ALU.mult).then_inc(s.emptied_of(c), 1)
                    if c % 4 == 3:
                        s.wait_emptied(v, c, 1)
                        nc.vector.tensor_tensor(part[:, 0, :], part[:, 0, :], part[:, 1, :], ALU.add).then_inc(sumd, 1)
                        v.wait_ge(high, c // 4 + 1)
                        nc.vector.tensor_tensor(ml[:, c // 4, :], part[:, 0, :], mh[:, c // 4, :].bitcast(F32),
                                                ALU.subtract).then_inc(low, 1)


def project_out(k):
    nc = k.nc
    mh, ml = k.mh, k.ml
    with ExitStack() as ctx:
        raw = k.sb("o_raw", [128, 4, 512], F32, ctx)
        whi = k.sb("o_hi", [128, 3, 512], F32R, ctx)
        wlo = k.sb("o_lo", [128, 3, 512], F32R, ctx)
        loaded = [k.sem(f"o_loaded{s}") for s in range(4)]
        hi, lo, used, done, added = (k.sem("o_" + n) for n in ("hi", "lo", "used", "done", "added"))
        n = 2 * KD
        bank = lambda a, t: k.bank[(5 * a + t) % 8]
        with nc.Block() as block:
            @block.sync
            def _(sp):
                for j in range(n):
                    if j >= 4:
                        sp.wait_ge(lo, j - 3)
                    sp.dma_start(raw[:, j % 4, :], k.i["w_out"][0, 128 * (j % KD):128 * (j % KD) + 128,
                                                               512 * (j // KD):512 * (j // KD) + 512])\
                        .then_inc(loaded[j % 4], 16)
                    if j == 3:
                        load_router(k, sp)
                    e = (j - 4) // 6
                    if j in (5, 11):
                        load_up(k, sp, e, e)
                    elif j in (8, 14):
                        load_down(k, sp, e, e)

            @block.gpsimd
            def _(g):
                for j in range(n):
                    g.wait_ge(hi, j + 1)
                    nc.gpsimd.tensor_tensor(wlo[:, j % 3, :], raw[:, j % 4, :], whi[:, j % 3, :].bitcast(F32),
                                            ALU.subtract).then_inc(lo, 1)

            @block.scalar
            def _(a):
                for j in range(n):
                    a.wait_ge(loaded[j % 4], 16 * (j // 4 + 1))
                    if j >= 3:
                        a.wait_ge(used, j - 2)
                    nc.scalar.activation(whi[:, j % 3, :], raw[:, j % 4, :], ACT.Copy).then_inc(hi, 1)

            @block.tensor
            def _(pe):
                for j in range(n):
                    a, d = j // KD, j % KD
                    pe.wait_ge(lo, j + 1)
                    for t, (c0, _) in enumerate(TILES):
                        if a == 1 and d == 0 and t >= 3:
                            pe.wait_ge(added, t - 2)
                        for i, (x, w) in enumerate(((mh, whi), (mh, wlo), (ml, whi))):
                            last = nc.tensor.matmul(bank(a, t)[:], x[:, d, c0:c0 + 128], w[:, j % 3, :],
                                                    start=(d == 0 and i == 0), stop=(d == KD - 1 and i == 2))
                        if d == KD - 1 and t < 4:
                            last.then_inc(done, 1)
                    last.then_inc(used, 1)

            @block.vector
            def _(v):
                for a in range(2):
                    for t, (_, rows) in enumerate(TILES):
                        if t < 4:
                            v.wait_ge(done, 4 * a + t + 1)
                        else:
                            v.wait_ge(used, KD * (a + 1))
                        f = slice(512 * a, 512 * a + 512)
                        nc.vector.tensor_tensor(k.x[0:rows, t, f], k.x[0:rows, t, f], bank(a, t)[0:rows, :], ALU.add)\
                            .then_inc(added, 1)


def expert_tensors(k):
    nc, ctx = k.nc, k.experts
    sem = lambda name: k.sem(name, ctx)
    k.w1, k.w3, k.w2 = [], [], []
    k.w1_loaded, k.w3_loaded, k.w2_loaded = ([sem(f"{w}_loaded{s}") for s in range(RING)] for w in ("w1", "w3", "w2"))
    for _ in range(RING - 1):
        weight_slot(k)
    k.router_loaded = sem("router_loaded")
    k.idx = k.sb("slot_token", [SLOTS, NB], I32, ctx)
    k.eid = k.sb("more_expert", [1, MORE], I32, ctx)
    k.nmore = k.sb("more_blocks", [1, 1], I32, ctx)
    k.row = k.sb("token_slot", [128, 5, 2], I32, ctx)
    k.wt = k.sb("token_weight", [128, 5, 2], F32, ctx)
    k.lg = k.sb("logits", [128, 5, GROUPS + NE], F32, k.routing)
    k.gain = k.sb("g_ffn_rows", [128, D], F32, k.routing)
    k.wr = k.sb("w_router", [128, KD, GROUPS + NE], F32, k.routing)
    k.br = k.sb("b_router", [128, GROUPS + NE], F32, k.routing)


def load_router(k, sp):
    with k.nc.allow_non_contiguous_dma(reason="router columns"):
        for dst, src in ((k.gain[:], k.i["g_ffn"].broadcast_to([128, D])),
                         (k.wr[:, :, 0:GROUPS], k.i["w_grp"][0].rearrange("(k p) n -> p k n", p=128)),
                         (k.wr[:, :, GROUPS:], k.i["w_exp"][0].rearrange("(k p) n -> p k n", p=128)),
                         (k.br[:, 0:GROUPS], k.i["b_grp"].broadcast_to([128, GROUPS])),
                         (k.br[:, GROUPS:], k.i["b_exp"].broadcast_to([128, NE]))):
            sp.dma_start(dst, src).then_inc(k.router_loaded, 16)


def weight_slot(k):
    s = len(k.w1)
    k.w1.append(k.sb(f"e_w1_{s}", [128, KD, FE], F32, k.rings))
    k.w3.append(k.sb(f"e_w3_{s}", [128, KD, FE], F32, k.rings))
    k.w2.append(k.sb(f"e_w2_{s}", [128, FE // 128, D], F32, k.rings))


def load_weights(k, sp, name, tiles, loaded, e, slot):
    src = k.i[name]
    src = src[0, e] if isinstance(e, int) else src[0, bass.ds(e, 1)].rearrange("o r n -> (o r) n")
    sp.dma_start(tiles[slot][:], src.rearrange("(k p) n -> p k n", p=128)).then_inc(loaded[slot], 16)


def load_up(k, sp, e, slot):
    load_weights(k, sp, "w_e1", k.w1, k.w1_loaded, e, slot)
    load_weights(k, sp, "w_e3", k.w3, k.w3_loaded, e, slot)


def load_down(k, sp, e, slot):
    load_weights(k, sp, "w_e2", k.w2, k.w2_loaded, e, slot)


def normalise_rows(k):
    nc = k.nc
    ctx = k.stage
    NL = GROUPS + NE
    stat = k.sb("r_stat", [128, 3, 5], F32, ctx)
    xn = [k.sb(f"r_xn{b}", [128, D], F32, ctx) for b in range(2)]
    xT = k.sb("r_xT", [128, 2, KD, 128], F32, ctx)
    junk = xT[:, 1].rearrange("p k n -> p (k n)")
    rms, normed, moved, turned, scored, biased = (k.sem("r_" + n) for n in
                                                  ("rms", "normed", "moved", "turned", "scored", "biased"))
    stored = [k.sem(f"r_stored{s}") for s in range(2)]
    with nc.Block() as block:
        @block.sync
        def _(sp):
            for t, (c0, n) in enumerate(TILES):
                sp.wait_ge(normed, t + 1)
                sp.dma_start(k.table[c0:c0 + n, :], xn[t % 2][0:n, :]).then_inc(stored[t % 2], 16)
            load_up(k, sp, RING - 1, RING - 1)
            load_down(k, sp, RING - 1, RING - 1)
            sp.wait_ge(stored[0], 48)
            sp.wait_ge(stored[1], 32)

        @block.scalar
        def _(a):
            c = k.chain(a, "scalar")
            for t, (c0, n) in enumerate(TILES):
                c(nc.scalar.activation(junk[0:n, :], k.x[0:n, t, :], ACT.Square, accum_out=stat[0:n, 0, t:t + 1]))
            for t, (c0, n) in enumerate(TILES):
                nc.scalar.activation(stat[0:n, 1, t:t + 1], stat[0:n, 0, t:t + 1], ACT.Sqrt, bias=k.eps[0:n, :],
                                     scale=1.0 / D).then_inc(rms, 1)
            for t, (c0, n) in enumerate(TILES):
                a.wait_ge(moved, t + 1)
                if t >= 2:
                    a.wait_ge(scored, t - 1)
                for b in range(2):
                    nc.scalar.activation(xT[:, t % 2, 4 * b:4 * b + 4, 0:n],
                                         k.bank[2 * (t % 2) + b][:, 0:4 * n].rearrange("p (k n) -> p k n", k=4),
                                         ACT.Copy).then_inc(turned, 1)

        @block.vector
        def _(v):
            c = k.chain(v, "vector")
            c(nc.vector.memset(k.lg[:], 0.0))
            v.wait_ge(k.router_loaded, 80)
            for t, (c0, n) in enumerate(TILES):
                v.wait_ge(rms, t + 1)
                c(nc.vector.reciprocal(stat[0:n, 2, t:t + 1], stat[0:n, 1, t:t + 1]))
                if t >= 2:
                    v.wait_ge(moved, t - 1)
                    v.wait_ge(stored[t % 2], 16 * (t // 2))
                nc.vector.scalar_tensor_tensor(out=xn[t % 2][0:n, :], in0=k.x[0:n, t, :], scalar=stat[0:n, 2, t:t + 1],
                                               in1=k.gain[0:n, :], op0=ALU.mult, op1=ALU.mult).then_inc(normed, 1)
            for t, (c0, n) in enumerate(TILES):
                v.wait_ge(scored, t + 1)
                nc.vector.tensor_tensor(k.lg[0:n, t, :], k.bank[4 + t % 2][0:n, 0:NL], k.br[0:n, :], ALU.add)\
                    .then_inc(biased, 1)

        def score(pe, t):
            n = TILES[t][1]
            pe.wait_ge(turned, 2 * (t + 1))
            if t >= 2:
                pe.wait_ge(biased, t - 1)
            for d in range(KD):
                last = nc.tensor.matmul(k.bank[4 + t % 2][0:n, 0:NL], xT[:, t % 2, d, 0:n], k.wr[:, d, :],
                                        start=(d == 0), stop=(d == KD - 1))
            last.then_inc(scored, 1)

        @block.tensor
        def _(pe):
            pe.wait_ge(k.router_loaded, 80)
            for t, (c0, n) in enumerate(TILES):
                pe.wait_ge(normed, t + 1)
                if t >= 2:
                    pe.wait_ge(turned, 2 * (t - 1))
                for d in range(KD):
                    last = nc.tensor.transpose(k.bank[2 * (t % 2) + d // 4][:, (d % 4) * n:(d % 4) * n + n],
                                               xn[t % 2][0:n, 128 * d:128 * d + 128], k.ident[0:n, 0:n])
                last.then_inc(moved, 1)
                if t >= 1:
                    score(pe, t - 1)
            score(pe, 4)


def choose_experts(k):
    nc = k.nc
    ctx = k.stage
    V = nc.vector
    T = lambda name, *dims, dt=F32, p=128: k.sb("c_" + name, [p] + list(dims), dt, ctx)
    iN = T("iota_i", max(NB, SLOTS), dt=I32)
    iota = T("iota", max(NB, SLOTS))
    token_i, token, valid = T("token_i", 5, dt=I32), T("token", 5), T("valid", 5)
    g8, gm, gi, gf = T("g8", 5, 8), T("gmax", 5, 8), T("gidx", 5, 8, dt=U32), T("gsel", 5)
    goh, gd, ge, gs = T("goh", 5, GROUPS), T("gdiff", 5, GROUPS), T("gexp", 5, GROUPS), T("gsum", 5)
    em, em8, ei, ef = T("em", 5, NE), T("emax", 5, 8), T("eidx", 5, 8, dt=U32), T("esel", 5, 2)
    e2, wa = T("e2", 5), T("wa", 5)
    oh, both, pre, tmp = T("oh", 2, 5, NE), T("both", 5, NE), T("pre", 5, NE), T("tmp", 2, 5, NE)
    tot, ov, oi, ob = T("tot", NE), T("over", NE), T("cum", 2, NE), T("before", NE)
    run = T("run", 6, NE)
    rank, obr, q, s, blk, pos = T("rank", 2, 5), T("obr", 2, 5), T("q", 2, 5), T("s", 2, 5), T("blk", 2, 5), T("pos", 2, 5)
    more = T("more", 2, 5)
    further = -(-NT // SLOTS)
    full = T("full", further - 1)
    cmpt, cmpq = T("cmpt", NE, further - 1), T("cmpq", 10, further - 1)
    cmpj, ejf = T("cmpj", MORE, NE), T("ejf", MORE)
    r1, b1 = T("rank_oh", 10, SLOTS), T("blk_oh", 10, NB)
    made, diffs, exps, chosen, counted, coded, listed = (k.sem("c_" + n) for n in
                                                        ("made", "diffs", "exps", "chosen", "counted", "coded", "listed"))
    with nc.Block() as block:
        @block.gpsimd
        def _(g):
            g.iota(iN[:], pattern=[[1, max(NB, SLOTS)]], base=0, channel_multiplier=0).then_inc(made, 1)
            g.iota(token_i[:], pattern=[[128, 5]], base=NS - 128, channel_multiplier=1).then_inc(made, 1)
            g.wait_ge(made, 2)
            g.iota(token_i[:, 0:1], pattern=[[0, 1]], base=0, channel_multiplier=1).then_inc(made, 1)

        @block.scalar
        def _(a):
            a.wait_ge(diffs, 2)
            nc.scalar.activation(ge[:], gd[:], ACT.Exp).then_inc(exps, 1)
            nc.scalar.activation(e2[:], e2[:], ACT.Exp).then_inc(exps, 1)

        @block.tensor
        def _(pe):
            pe.wait_ge(chosen, 1)
            nc.tensor.matmul(k.bank[0][:, 0:5 * NE], k.striu[:], both[:].rearrange("p t e -> p (t e)"), start=True, stop=False)
            nc.tensor.matmul(k.bank[0][:, 0:5 * NE], k.ones[:], run[:, 0:5].rearrange("p t e -> p (t e)"), start=False, stop=True)
            nc.tensor.matmul(k.bank[1][:, 0:NE], k.ones[:], run[:, 5, :], start=True, stop=True).then_inc(counted, 1)
            pe.wait_ge(coded, 1)
            for j in range(10):
                last = nc.tensor.matmul(k.bank[2][0:SLOTS, 0:NB], r1[:, j, :], b1[:, j, :], start=(j == 0), stop=(j == 9))
            last.then_inc(listed, 1)

        @block.vector
        def _(v):
            c = k.chain(v, "vector")
            bc = lambda ap, n: ap.unsqueeze(2).broadcast_to([128, 5, n])
            c(V.memset(valid[:], 1.0))
            c(V.memset(valid[:, 0:1], 0.0))
            c(V.memset(valid[0:NS, 0:1], 1.0))
            c(V.memset(g8[:], NEG))
            v.wait_ge(made, 3)
            c(V.tensor_copy(iota[:], iN[:]))
            c(V.tensor_scalar(full[:], iota[:, 1:further], float(SLOTS), None, ALU.mult))
            c(V.tensor_copy(token[:], token_i[:]))
            c(V.tensor_copy(g8[:, :, 0:GROUPS], k.lg[:, :, 0:GROUPS]))
            for t in range(5):
                c(V.max(out=gm[:, t, :], in_=g8[:, t, :]))
                c(V.max_index(out=gi[:, t, :], in_max=gm[:, t, :], in_values=g8[:, t, :]))
            c(V.tensor_copy(gf[:], gi[:, :, 0]))
            V.tensor_tensor(gd[:], k.lg[:, :, 0:GROUPS], bc(gm[:, :, 0], GROUPS), ALU.subtract).then_inc(diffs, 1)
            c(V.tensor_tensor(goh[:], iota[:, 0:GROUPS].unsqueeze(1).broadcast_to([128, 5, GROUPS]), bc(gf[:], GROUPS),
                              ALU.is_equal))
            c(V.tensor_scalar(goh[:], goh[:], -NEG, NEG, ALU.mult, ALU.add))
            c(V.tensor_tensor(em[:].rearrange("p t (g e) -> p t g e", g=GROUPS),
                              k.lg[:, :, GROUPS:].rearrange("p t (g e) -> p t g e", g=GROUPS),
                              goh[:].unsqueeze(3).broadcast_to([128, 5, GROUPS, PER_GROUP]), ALU.add))
            for t in range(5):
                c(V.max(out=em8[:, t, :], in_=em[:, t, :]))
                c(V.max_index(out=ei[:, t, :], in_max=em8[:, t, :], in_values=em[:, t, :]))
            V.tensor_tensor(e2[:], em8[:, :, 1], em8[:, :, 0], ALU.subtract).then_inc(diffs, 1)
            c(V.tensor_copy(ef[:], ei[:, :, 0:2]))
            for j in range(2):
                c(V.tensor_tensor(oh[:, j], iota[:, 0:NE].unsqueeze(1).broadcast_to([128, 5, NE]), bc(ef[:, :, j], NE),
                                  ALU.is_equal))
                c(V.tensor_tensor(oh[:, j], oh[:, j], bc(valid[:], NE), ALU.mult))
            c(V.tensor_tensor(both[:], oh[:, 0], oh[:, 1], ALU.add))
            c(V.memset(run[:, 0, :], 0.0))
            for t in range(5):
                op = V.tensor_tensor(run[:, t + 1, :], run[:, t, :], both[:, t, :], ALU.add)
                if t < 4:
                    c(op)
            op.then_inc(chosen, 1)
            v.wait_ge(exps, 2)
            c(V.tensor_reduce(gs[:], ge[:], AX.X, ALU.add))
            c(V.tensor_scalar(wa[:], e2[:], 1.0, None, ALU.add))
            c(V.tensor_tensor(gs[:], gs[:], wa[:], ALU.mult))
            c(V.reciprocal(k.wt[:, :, 0], gs[:]))
            c(V.tensor_tensor(k.wt[:, :, 1], k.wt[:, :, 0], e2[:], ALU.mult))
            v.wait_ge(counted, 1)
            c(V.tensor_copy(pre[:].rearrange("p t e -> p (t e)"), k.bank[0][:, 0:5 * NE]))
            c(V.tensor_copy(tot[:], k.bank[1][:, 0:NE]))
            c(V.tensor_tensor(cmpt[:], tot[:].unsqueeze(2).broadcast_to([128, NE, further - 1]),
                              full[:].unsqueeze(1).broadcast_to([128, NE, further - 1]), ALU.is_gt))
            c(V.tensor_reduce(ov[:], cmpt[:], AX.X, ALU.add))
            c(V.tensor_copy(oi[:, 0], ov[:]))
            cur, step = 0, 1
            while step < NE:
                c(V.tensor_copy(oi[:, 1 - cur, 0:step], oi[:, cur, 0:step]))
                c(V.tensor_tensor(oi[:, 1 - cur, step:], oi[:, cur, step:], oi[:, cur, 0:NE - step], ALU.add))
                cur, step = 1 - cur, 2 * step
            c(V.tensor_tensor(ob[:], oi[:, cur], ov[:], ALU.subtract))
            c(V.tensor_tensor(tmp[:], oh[:], pre[:].unsqueeze(1).broadcast_to([128, 2, 5, NE]), ALU.mult))
            c(V.tensor_reduce(rank[:], tmp[:], AX.X, ALU.add))
            c(V.tensor_tensor(tmp[:].rearrange("p j t e -> p (j t) e"), oh[:].rearrange("p j t e -> p (j t) e"),
                              ob[:].unsqueeze(1).broadcast_to([128, 10, NE]), ALU.mult))
            c(V.tensor_reduce(obr[:], tmp[:], AX.X, ALU.add))
            c(V.tensor_tensor(cmpq[:], rank[:].rearrange("p j t -> p (j t)").unsqueeze(2).broadcast_to([128, 10, further - 1]),
                              full[:].unsqueeze(1).broadcast_to([128, 10, further - 1]), ALU.is_ge))
            c(V.tensor_reduce(q[:].rearrange("p j t -> p (j t)"), cmpq[:], AX.X, ALU.add))
            c(V.scalar_tensor_tensor(out=s[:], in0=q[:], scalar=-float(SLOTS), in1=rank[:], op0=ALU.mult, op1=ALU.add))
            c(V.scalar_tensor_tensor(out=blk[:], in0=q[:], scalar=NE - 1.0, in1=obr[:], op0=ALU.add, op1=ALU.add))
            c(V.tensor_scalar(more[:], q[:], 0.5, None, ALU.is_gt))
            est = ef[:].rearrange("p t j -> p j t")
            c(V.tensor_tensor(blk[:], blk[:], est, ALU.subtract))
            c(V.tensor_tensor(blk[:], blk[:], more[:], ALU.mult))
            c(V.tensor_tensor(blk[:], blk[:], est, ALU.add))
            c(V.scalar_tensor_tensor(out=pos[:], in0=blk[:], scalar=float(SLOTS), in1=s[:], op0=ALU.mult, op1=ALU.add))
            c(V.tensor_copy(k.row[:].rearrange("p t j -> p j t"), pos[:]))
            c(V.tensor_scalar(token[:], token[:], float(NT), None, ALU.subtract))
            c(V.tensor_tensor(token[:], token[:], valid[:], ALU.mult))
            col = lambda ap, n: ap.rearrange("p j t -> p (j t)").unsqueeze(2).broadcast_to([128, 10, n])
            row = lambda n: iota[:, 0:n].unsqueeze(1).broadcast_to([128, 10, n])
            V.tensor_tensor(r1[:], row(SLOTS), col(s[:], SLOTS), ALU.is_equal)
            c(V.tensor_tensor(b1[:], row(NB), col(blk[:], NB), ALU.is_equal))
            V.tensor_tensor(b1[:].rearrange("p (j t) b -> p j t b", j=2), b1[:].rearrange("p (j t) b -> p j t b", j=2),
                            token[:].unsqueeze(1).unsqueeze(3).broadcast_to([128, 2, 5, NB]), ALU.mult).then_inc(coded, 1)
            c(V.tensor_tensor(cmpj[:], oi[:, cur].unsqueeze(1).broadcast_to([128, MORE, NE]),
                              iota[:, 0:MORE].unsqueeze(2).broadcast_to([128, MORE, NE]), ALU.is_le))
            c(V.tensor_reduce(ejf[:], cmpj[:], AX.X, ALU.add))
            c(V.tensor_copy(k.eid[:], ejf[0:1, :]))
            c(V.tensor_copy(k.nmore[:], oi[0:1, cur, NE - 1:NE]))
            v.wait_ge(listed, 1)
            c(V.tensor_scalar(k.idx[:], k.bank[2][0:SLOTS, 0:NB], float(NT), None, ALU.add))


def expert_blocks(k):
    nc = k.nc
    FH, NF = FE // 2, FE // 128
    STEPS = NE // RING
    with ExitStack() as ctx:
        at = k.sb("b_index", [SLOTS, RING], I32, ctx)
        spare = k.sb("b_spare", [SLOTS, 2], F32, ctx)
        xg = k.sb("b_rows", [SLOTS, RING, D], F32, ctx)
        xT = k.sb("b_xT", [128, KD, SLOTS], F32, ctx)
        act = k.sb("b_silu", [128, FH], F32, ctx)
        hm = k.sb("b_hidden", [128, FH], F32, ctx)
        hT = k.sb("b_hiddenT", [128, 2, 128], F32, ctx)
        y = k.sb("b_y", [128, RING, D // 2], F32, ctx)
        names = ("index", "turned", "copied", "first", "up", "silu", "hidden", "hturned", "hcopied", "down", "out")
        index, turned, copied, first, up, silu, hidden, hturned, hcopied, down, out = (k.sem("b_" + n) for n in names)
        gathered = k.gathered
        stored = [k.sem(f"b_stored{s}") for s in range(RING)]
        lo, hi = slice(0, 64), slice(64, 128)
        sl = (lo, hi)

        def wait(eng, sem, value):
            if not isinstance(value, int) or value > 0:
                eng.wait_ge(sem, value)

        def fetch(g, b, slot, n, prev):
            wait(g, turned, prev + 1)
            nc.gpsimd.tensor_copy(at[:, slot:slot + 1], k.idx[:, bass.ds(b, 1)]).then_inc(index, 1)
            g.wait_ge(index, b + 1)
            nc.gpsimd.tensor_tensor(spare[:, 0:1], k.one[0:SLOTS, :], k.one[0:SLOTS, :], ALU.add)
            g.indirect_dma_start(out=xg[:, slot, :], out_offset=None, in_=k.table,
                                 in_offset=bass.IndirectOffsetOnAxis(ap=at[:, slot:slot + 1], axis=0))\
                .then_inc(gathered[slot], 16)
            g.wait_ge(gathered[slot], 16 * n + 16)

        def products(pe, b, slot, n, prev):
            pe.wait_ge(gathered[slot], 16 * n + 16)
            wait(pe, copied, b)
            nc.tensor.matmul(k.bank[0][:, 0:64], xg[:, slot, 0:128], k.ident[0:64, 0:64], start=True, stop=True)
            for d in range(1, KD):
                last = nc.tensor.transpose(k.bank[0][:, 64 * d:64 * d + 64], xg[:, slot, 128 * d:128 * d + 128],
                                           k.ident[0:64, 0:64])
            last.then_inc(turned, 1)
            pe.wait_ge(copied, b + 1)
            wait(pe, hidden, b)
            for bank, w, loaded, made in ((1, k.w1, k.w1_loaded, first), (2, k.w3, k.w3_loaded, up)):
                pe.wait_ge(loaded[slot], 16 * n + 16)
                for d in range(KD):
                    for a in range(2):
                        last = nc.tensor.matmul(k.bank[bank][sl[a], 0:FH], xT[:, d, :], w[slot][:, d, FH * a:FH * a + FH],
                                                start=(d == 0), stop=(d == KD - 1))
                last.then_inc(made, 1)
            pe.wait_ge(hidden, b + 1)
            for c in range(2):
                last = nc.tensor.transpose(k.bank[3][:, 128 * c:128 * c + 128], hm[:, 128 * c:128 * c + 128], k.ident[:])
            last.then_inc(hturned, 1)
            pe.wait_ge(hcopied, b + 1)
            pe.wait_ge(k.w2_loaded[slot], 16 * n + 16)
            wait(pe, out, b)
            for f in range(NF):
                for a in range(2):
                    last = nc.tensor.matmul(k.bank[4][sl[a], :], hT[:, f % 2, sl[f // 2]],
                                            k.w2[slot][:, f, 512 * a:512 * a + 512], start=(f == 0), stop=(f == NF - 1))
            last.then_inc(down, 1)

        def scalar_part(a, b, slot, n, prev):
            a.wait_ge(first, b + 1)
            wait(a, hidden, b)
            nc.scalar.activation(act[:], k.bank[1][:, 0:FH], ACT.Silu).then_inc(silu, 1)
            a.wait_ge(down, b + 1)
            wait(a, stored[slot], 32 * n)
            nc.scalar.activation(y[:, slot, :], k.bank[4][:], ACT.Copy).then_inc(out, 1)
            a.wait_ge(out, b + 1)
            for h in range(2):
                a.dma_start(k.yblk[bass.ds(b * SLOTS, SLOTS), 512 * h:512 * h + 512], y[sl[h], slot, :])\
                    .then_inc(stored[slot], 16)

        def vector_part(v, b, slot, n, prev):
            v.wait_ge(turned, b + 1)
            wait(v, up, b)
            nc.vector.tensor_copy(xT[:].rearrange("p k s -> p (k s)"), k.bank[0][:]).then_inc(copied, 1)
            v.wait_ge(silu, b + 1)
            v.wait_ge(up, b + 1)
            wait(v, hturned, b)
            nc.vector.tensor_tensor(hm[:], act[:], k.bank[2][:, 0:FH], ALU.mult).then_inc(hidden, 1)
            v.wait_ge(hturned, b + 1)
            wait(v, down, b)
            nc.vector.tensor_copy(hT[:].rearrange("p c s -> p (c s)"), k.bank[3][:, 0:256]).then_inc(hcopied, 1)

        def loads(sp, e, b, slot, prev):
            sp.wait_ge(first, prev + 1)
            load_weights(k, sp, "w_e1", k.w1, k.w1_loaded, e, slot)
            sp.wait_ge(up, prev + 1)
            load_weights(k, sp, "w_e3", k.w3, k.w3_loaded, e, slot)
            sp.wait_ge(down, prev + 1)
            load_down(k, sp, e, slot)

        def run_blocks(eng, part):
            for s in range(RING):
                part(eng, s, s, 0, s - RING)
            with eng.Fori(1, STEPS) as i:
                for s in range(RING):
                    part(eng, RING * i + s, s, i, RING * i + s - RING)
            for b in range(RING * STEPS, NE):
                part(eng, b, b % RING, b // RING, b - RING)
            n = eng.value_load(k.nmore[0:1, 0:1], min_val=0, max_val=MORE)
            with eng.If(n > 0):
                with eng.Fori(0, n) as j:
                    part(eng, j + NE, RING - 1, j + STEPS, j + NE - 1)
            return n

        with nc.Block() as block:
            @block.sync
            def _(sp):
                with sp.Fori(1, STEPS) as i:
                    for s in range(RING):
                        b = RING * i + s
                        loads(sp, b, b, s, b - RING)
                for b in range(RING * STEPS, NE):
                    loads(sp, b, b, b % RING, b - RING)
                n = sp.value_load(k.nmore[0:1, 0:1], min_val=0, max_val=MORE)
                with sp.If(n > 0):
                    with sp.Fori(0, n) as j:
                        e = sp.value_load(k.eid[0:1, bass.ds(j, 1)], min_val=0, max_val=NE - 1)
                        loads(sp, e, j + NE, RING - 1, j + NE - 1)

            @block.gpsimd
            def _(g):
                run_blocks(g, fetch)

            @block.tensor
            def _(pe):
                run_blocks(pe, products)

            @block.scalar
            def _(a):
                n = run_blocks(a, scalar_part)
                for s in range(RING - 1):
                    a.wait_ge(stored[s], 32 * len(range(s, NE, RING)))
                a.wait_ge(stored[RING - 1], n * 32 + 32 * STEPS)
                nc.scalar.activation(spare[:, 1:2], k.one[0:SLOTS, :], ACT.Copy)

            @block.vector
            def _(v):
                run_blocks(v, vector_part)


def combine(k):
    nc = k.nc
    with ExitStack() as ctx:
        rows = k.sb("y_rows", [128, 10, D], F32, ctx)
        idx = k.sb("y_index", [128, 10], I32, ctx)
        ready = k.sem("y_ready")
        got = k.got
        added, stored = k.sem("y_added"), k.sem("y_stored")
        with nc.Block() as block:
            @block.gpsimd
            def _(g):
                nc.gpsimd.tensor_copy(idx[:], k.row[:].rearrange("p t j -> p (t j)")).then_inc(ready, 1)
                g.wait_ge(ready, 1)
                for m in range(10):
                    n = TILES[m // 2][1]
                    g.indirect_dma_start(out=rows[0:n, m, :], out_offset=None, in_=k.yblk,
                                         in_offset=bass.IndirectOffsetOnAxis(ap=idx[0:n, m:m + 1], axis=0))\
                        .then_inc(got[m], 16)
                for m in range(10):
                    g.wait_ge(got[m], 16)

            @block.vector
            def _(v):
                for m in range(10):
                    t, j = m // 2, m % 2
                    n = TILES[t][1]
                    v.wait_ge(got[m], 16)
                    if j:
                        v.wait_ge(added, m)
                    nc.vector.scalar_tensor_tensor(out=k.x[0:n, t, :], in0=rows[0:n, m, :],
                                                   scalar=k.wt[0:n, t, j:j + 1], in1=k.x[0:n, t, :],
                                                   op0=ALU.mult, op1=ALU.add).then_inc(added, 1)

            @block.sync
            def _(sp):
                for t, (c0, n) in enumerate(TILES):
                    sp.wait_ge(added, 2 * t + 2)
                    dst = k.o["y_s"][0] if t == 0 else k.o["y_p"][0, 128 * (t - 1):128 * t, :]
                    sp.dma_start(dst, k.x[0:n, t, :]).then_inc(stored, 16)
                sp.wait_ge(stored, 80)
                sp.wait_ge(k.late, 16 * 4)


_INS = ["x_prompt", "x_sample", "cache_fox_k", "cache_fox_v", "cache_fox_logf", "state_gdn", "state_gdn_conv", "g_mix",
        "w_in", "b_f", "g_qnorm", "g_knorm", "w_conv", "a_log", "dt_bias", "g_onorm", "b_gate", "w_br_a", "w_br_b",
        "w_out", "g_ffn", "w_grp", "b_grp", "w_exp", "b_exp", "w_e1", "w_e3", "w_e2"]
_OUTS = {"y_p": (1, NP, D), "y_s": (1, NS, D)}
for _s, _n in (("p", NP), ("s", NS)):
    _OUTS.update({"k_" + _s: (1, 1, _n, H, DH), "v_" + _s: (1, 1, _n, H, DH), "logf_" + _s: (1, 1, _n, H),
                  "state_" + _s: (1, 1, H, DH, DV), "conv_" + _s: (1, 1, CONV_W - 1, CONV_CH)})


def kernel(**inputs):
    import numpy as _np
    import concourse.bacc as _bacc
    from concourse.bass_utils import run_bass_kernel_spmd as _run

    nc = _bacc.Bacc("TRN2", target_bir_lowering=False, num_devices=1)
    arrays, ins, outs = {}, {}, {}
    for name in _INS:
        a = _np.ascontiguousarray(inputs[name])
        arrays["in_" + name] = a
        ins[name] = nc.dram_tensor("in_" + name, a.shape, F32, kind="ExternalInput").ap()
    for name, shape in _OUTS.items():
        outs[name] = nc.dram_tensor("out_" + name, shape, F32, kind="ExternalOutput").ap()
    build(nc, ins, outs)
    r = _run(nc, [arrays], core_ids=[0])
    return tuple(r.results[0]["out_" + name] for name in _OUTS)
```
